# Optimizing a Trainium2 kernel written in Bass

```python
import math
import jax, jax.numpy as jnp
from jax import lax
import numpy as np

D_MODEL = 1024
BATCH = 1
SEQ = 256
DEPTH = 4

CHUNK = 64
N_MIXERS = 3
EPS = 1e-6

DSA_HEADS = 16
DSA_HEAD_DIM = D_MODEL // DSA_HEADS
IDX_HEADS = 8
IDX_DIM = 64
TOPK_MAX = 256
Q_BLOCK = CHUNK
DSA_IN = 3 * D_MODEL + IDX_HEADS * IDX_DIM + IDX_DIM + IDX_HEADS
NEG_INF = -1e30

RWKV_HEAD = 64
RWKV_HEADS = D_MODEL // RWKV_HEAD
LORA_DECAY = 64
LORA_A = 64
LORA_GATE = 128
GN_EPS = 64e-5

S5_GROUP = 16
S5_GROUPS = D_MODEL // S5_GROUP
S5_STATE = 64
DT_MIN = 1e-3
DT_MAX = 1e-1

D_FF = 2816
CONV_W = 3

N_A = (DEPTH + 2) // 3
N_B = (DEPTH + 1) // 3
N_C = DEPTH // 3

kernel_name = 'hybrid_dsa_rwkv7_s5_convffn'

def rms_norm(x, g):
    x32 = x.astype(jnp.float32)
    y = x32 * lax.rsqrt(jnp.mean(x32 * x32, axis=-1, keepdims=True) + EPS)
    return (y * g.astype(jnp.float32)).astype(x.dtype)

def dsa_mixer(h, w_in, q_gain, k_gain, kidx_gain, w_out):
    bsz, seq, _ = h.shape
    topk = min(TOPK_MAX, seq // 4)
    D = D_MODEL
    proj = h @ w_in
    q, k, v, q_idx, k_idx, w_idx = jnp.split(
        proj, [D, 2 * D, 3 * D, 3 * D + IDX_HEADS * IDX_DIM, 3 * D + IDX_HEADS * IDX_DIM + IDX_DIM], axis=-1)
    q = rms_norm(q.reshape(bsz, seq, DSA_HEADS, DSA_HEAD_DIM), q_gain)
    k = rms_norm(k.reshape(bsz, seq, DSA_HEADS, DSA_HEAD_DIM), k_gain)
    v = v.reshape(bsz, seq, DSA_HEADS, DSA_HEAD_DIM)
    q_idx = q_idx.reshape(bsz, seq, IDX_HEADS, IDX_DIM)
    k_idx32 = rms_norm(k_idx, kidx_gain).astype(jnp.float32)
    w_idx = w_idx * (IDX_HEADS ** -0.5)

    nblk = seq // Q_BLOCK
    key_pos = jnp.arange(seq)

    def to_blocks(t):
        return jnp.moveaxis(t.reshape(bsz, nblk, Q_BLOCK, *t.shape[2:]), 1, 0)

    def block(args):
        blk, qb, qib, wb = args
        limit = (blk + 1) * Q_BLOCK
        logits = jnp.einsum('bqhd,bsd->bqhs', qib.astype(jnp.float32), k_idx32) * (IDX_DIM ** -0.5)
        score = jnp.einsum('bqh,bqhs->bqs', wb.astype(jnp.float32), jax.nn.relu(logits))
        score = jnp.where(key_pos[None, None, :] < limit, score, NEG_INF)
        _, idx = lax.top_k(score, topk)
        k_sel = jax.vmap(lambda kk, ii: kk[ii])(k, idx)
        v_sel = jax.vmap(lambda vv, ii: vv[ii])(v, idx)
        att = jnp.einsum('bqhd,bqkhd->bqhk', qb.astype(jnp.float32), k_sel.astype(jnp.float32))
        att = att * (DSA_HEAD_DIM ** -0.5)
        att = jnp.where((idx < limit)[:, :, None, :], att, NEG_INF)
        p = jax.nn.softmax(att, axis=-1)
        o = jnp.einsum('bqhk,bqkhd->bqhd', p, v_sel.astype(jnp.float32))
        return o.astype(qb.dtype)

    out = lax.map(block, (jnp.arange(nblk), to_blocks(q), to_blocks(q_idx), to_blocks(w_idx)))
    out = jnp.moveaxis(out, 0, 1).reshape(bsz, seq, D)
    return out @ w_out

def rwkv7_mixer(h, mu, w_rkv, w0, w1, w2, a0, a1, a2, g1, g2, k_k, k_a, r_k, ln_g, ln_b, w_out):
    bsz, seq, _ = h.shape
    f32 = jnp.float32
    h_prev = jnp.pad(h, ((0, 0), (1, 0), (0, 0)))[:, :-1]
    dh = h_prev - h
    xs = h[None] + dh[None] * mu[:, None, None, :]
    rkv = jnp.einsum('nbsd,nde->nbse', xs[:3], w_rkv)
    r, k, v = rkv[0], rkv[1], rkv[2]
    xw, xa, xg = xs[3], xs[4], xs[5]
    w_log = -jax.nn.softplus(-(w0 + jnp.tanh(xw @ w1) @ w2)) - 0.5
    decay = jnp.exp(-jnp.exp(w_log.astype(f32)))
    a = jax.nn.sigmoid(a0 + (xa @ a1) @ a2)
    g = jax.nn.sigmoid(xg @ g1) @ g2

    def heads(t):
        return t.reshape(bsz, seq, RWKV_HEADS, RWKV_HEAD).astype(f32)

    kk = heads(k * k_k)
    kk = kk / jnp.maximum(jnp.sqrt(jnp.sum(kk * kk, axis=-1, keepdims=True)), 1e-12)
    k = k * (1.0 + (a - 1.0) * k_a)
    r_h, k_h, v_h, a_h, w_h = heads(r), heads(k), heads(v), heads(a), heads(decay)

    def tm(t):
        return jnp.moveaxis(t, 1, 0)

    def step(state, inp):
        r_t, w_t, k_t, v_t, kk_t, a_t = inp
        sa = jnp.einsum('bhij,bhj->bhi', state, -kk_t)
        state = (state * w_t[:, :, None, :]
                 + sa[..., None] * (kk_t * a_t)[:, :, None, :]
                 + v_t[..., None] * k_t[:, :, None, :])
        y = jnp.einsum('bhij,bhj->bhi', state, r_t)
        return state, y

    state0 = jnp.zeros((bsz, RWKV_HEADS, RWKV_HEAD, RWKV_HEAD), f32)
    _, y = lax.scan(step, state0, (tm(r_h), tm(w_h), tm(k_h), tm(v_h), tm(kk), tm(a_h)))
    y = jnp.moveaxis(y, 0, 1)
    mean = jnp.mean(y, axis=-1, keepdims=True)
    var = jnp.mean(jnp.square(y - mean), axis=-1, keepdims=True)
    y = (y - mean) * lax.rsqrt(var + GN_EPS)
    y = y * ln_g.astype(f32).reshape(RWKV_HEADS, RWKV_HEAD) + ln_b.astype(f32).reshape(RWKV_HEADS, RWKV_HEAD)
    bonus = jnp.sum(r_h * k_h * r_k.astype(f32), axis=-1, keepdims=True) * v_h
    y = (y + bonus).reshape(bsz, seq, D_MODEL).astype(h.dtype) * g
    return y @ w_out

def s5_mixer(h, a_re, a_im, log_step, b_re, b_im, c_re, c_im, d_skip, w_glu, b_glu):
    bsz, seq, _ = h.shape
    f32 = jnp.float32
    step = jnp.exp(log_step.astype(f32))[:, None]
    lam = lax.complex(a_re.astype(f32), a_im.astype(f32))
    lam_bar = jnp.exp(lam * step)
    b = lax.complex(b_re.astype(f32), b_im.astype(f32))
    b_bar = ((lam_bar - 1.0) / lam)[..., None] * b
    c = lax.complex(c_re.astype(f32), c_im.astype(f32))
    u = jnp.swapaxes(h, 0, 1).astype(f32).reshape(seq, bsz, S5_GROUPS, S5_GROUP)
    bu = jnp.einsum('gpc,sbgc->sbgp', b_bar, u.astype(jnp.complex64))
    lam_t = jnp.broadcast_to(lam_bar, (seq, 1, S5_GROUPS, S5_STATE))

    def combine(e_i, e_j):
        a_i, x_i = e_i
        a_j, x_j = e_j
        return a_j * a_i, a_j * x_i + x_j

    _, states = lax.associative_scan(combine, (lam_t, bu), axis=0)
    y = jnp.real(jnp.einsum('gcp,sbgp->sbgc', c, states)).reshape(seq, bsz, D_MODEL)
    y = jnp.swapaxes(y, 0, 1) + d_skip.astype(f32) * h.astype(f32)
    y = jax.nn.gelu(y).astype(h.dtype)
    z = y @ w_glu + b_glu
    z1, z2 = jnp.split(z, 2, axis=-1)
    return z1 * jax.nn.sigmoid(z2)

def conv_ffn(h, w_up, conv_w, conv_b, w_down):
    u = h @ w_up
    u = lax.conv_general_dilated(
        u, conv_w[:, None, :], window_strides=(1,), padding=[(CONV_W - 1, 0)],
        dimension_numbers=('NWC', 'WIO', 'NWC'), feature_group_count=u.shape[-1]) + conv_b
    gate, val = jnp.split(u, 2, axis=-1)
    return (jax.nn.silu(gate) * val) @ w_down

def setup_inputs(seed: int = 0) -> dict:
    key = jax.random.key(seed)
    ks = iter(jax.random.split(key, 64))
    D, F = D_MODEL, D_FF
    G, P, GC = S5_GROUPS, S5_STATE, S5_GROUP

    def nrm(shape, scale):
        return jax.random.normal(next(ks), shape, jnp.float32) * scale

    def gain(shape):
        return 1.0 + nrm(shape, 0.02)

    x = nrm((BATCH, SEQ, D), 1.0)
    norm_mix = gain((DEPTH, D))
    norm_ffn = gain((DEPTH, D))
    dsa_w_in = nrm((N_A, D, DSA_IN), D ** -0.5)
    dsa_q_norm = gain((N_A, DSA_HEAD_DIM))
    dsa_k_norm = gain((N_A, DSA_HEAD_DIM))
    dsa_kidx_norm = gain((N_A, IDX_DIM))
    dsa_w_out = nrm((N_A, D, D), D ** -0.5)
    rwkv_mu = jax.random.uniform(next(ks), (N_B, 6, D), jnp.float32)
    rwkv_w_rkv = nrm((N_B, 3, D, D), D ** -0.5)
    rwkv_w0 = jax.random.uniform(next(ks), (N_B, D), jnp.float32, -5.0, 0.0)
    rwkv_w1 = nrm((N_B, D, LORA_DECAY), D ** -0.5)
    rwkv_w2 = nrm((N_B, LORA_DECAY, D), 0.1 * LORA_DECAY ** -0.5)
    rwkv_a0 = nrm((N_B, D), 0.1)
    rwkv_a1 = nrm((N_B, D, LORA_A), D ** -0.5)
    rwkv_a2 = nrm((N_B, LORA_A, D), 0.1 * LORA_A ** -0.5)
    rwkv_g1 = nrm((N_B, D, LORA_GATE), D ** -0.5)
    rwkv_g2 = nrm((N_B, LORA_GATE, D), LORA_GATE ** -0.5)
    rwkv_k_k = 0.85 + nrm((N_B, D), 0.02)
    rwkv_k_a = gain((N_B, D))
    rwkv_r_k = nrm((N_B, RWKV_HEADS, RWKV_HEAD), 0.1)
    rwkv_ln_g = gain((N_B, D))
    rwkv_ln_b = nrm((N_B, D), 0.01)
    rwkv_w_out = nrm((N_B, D, D), D ** -0.5)
    s5_a_re = -0.5 + nrm((N_C, G, P), 0.01)
    s5_a_im = jnp.broadcast_to(math.pi * jnp.arange(P, dtype=jnp.float32), (N_C, G, P))
    s5_log_step = jax.random.uniform(next(ks), (N_C, G), jnp.float32, math.log(DT_MIN), math.log(DT_MAX))
    s5_b_re = nrm((N_C, G, P, GC), (2 * GC) ** -0.5)
    s5_b_im = nrm((N_C, G, P, GC), (2 * GC) ** -0.5)
    s5_c_re = nrm((N_C, G, GC, P), P ** -0.5)
    s5_c_im = nrm((N_C, G, GC, P), P ** -0.5)
    s5_d = nrm((N_C, D), 1.0)
    s5_w_glu = nrm((N_C, D, 2 * D), D ** -0.5)
    s5_b_glu = nrm((N_C, 2 * D), 0.01)
    ffn_w_up = nrm((DEPTH, D, 2 * F), D ** -0.5)
    ffn_conv_w = nrm((DEPTH, CONV_W, 2 * F), CONV_W ** -0.5)
    ffn_conv_b = nrm((DEPTH, 2 * F), 0.01)
    ffn_w_down = nrm((DEPTH, F, D), F ** -0.5)
    return {
        'x': x, 'norm_mix': norm_mix, 'norm_ffn': norm_ffn,
        'dsa_w_in': dsa_w_in, 'dsa_q_norm': dsa_q_norm, 'dsa_k_norm': dsa_k_norm,
        'dsa_kidx_norm': dsa_kidx_norm, 'dsa_w_out': dsa_w_out,
        'rwkv_mu': rwkv_mu, 'rwkv_w_rkv': rwkv_w_rkv, 'rwkv_w0': rwkv_w0, 'rwkv_w1': rwkv_w1,
        'rwkv_w2': rwkv_w2, 'rwkv_a0': rwkv_a0, 'rwkv_a1': rwkv_a1, 'rwkv_a2': rwkv_a2,
        'rwkv_g1': rwkv_g1, 'rwkv_g2': rwkv_g2, 'rwkv_k_k': rwkv_k_k, 'rwkv_k_a': rwkv_k_a,
        'rwkv_r_k': rwkv_r_k, 'rwkv_ln_g': rwkv_ln_g, 'rwkv_ln_b': rwkv_ln_b, 'rwkv_w_out': rwkv_w_out,
        's5_a_re': s5_a_re, 's5_a_im': s5_a_im, 's5_log_step': s5_log_step,
        's5_b_re': s5_b_re, 's5_b_im': s5_b_im, 's5_c_re': s5_c_re, 's5_c_im': s5_c_im,
        's5_d': s5_d, 's5_w_glu': s5_w_glu, 's5_b_glu': s5_b_glu,
        'ffn_w_up': ffn_w_up, 'ffn_conv_w': ffn_conv_w, 'ffn_conv_b': ffn_conv_b, 'ffn_w_down': ffn_w_down,
    }

def reference(x, norm_mix, norm_ffn,
              dsa_w_in, dsa_q_norm, dsa_k_norm, dsa_kidx_norm, dsa_w_out,
              rwkv_mu, rwkv_w_rkv, rwkv_w0, rwkv_w1, rwkv_w2, rwkv_a0, rwkv_a1, rwkv_a2,
              rwkv_g1, rwkv_g2, rwkv_k_k, rwkv_k_a, rwkv_r_k, rwkv_ln_g, rwkv_ln_b, rwkv_w_out,
              s5_a_re, s5_a_im, s5_log_step, s5_b_re, s5_b_im, s5_c_re, s5_c_im,
              s5_d, s5_w_glu, s5_b_glu,
              ffn_w_up, ffn_conv_w, ffn_conv_b, ffn_w_down):
    for i in range(DEPTH):
        kind = i % N_MIXERS
        j = i // N_MIXERS
        h = rms_norm(x, norm_mix[i])
        if kind == 0:
            y = dsa_mixer(h, dsa_w_in[j], dsa_q_norm[j], dsa_k_norm[j], dsa_kidx_norm[j], dsa_w_out[j])
        elif kind == 1:
            y = rwkv7_mixer(h, rwkv_mu[j], rwkv_w_rkv[j], rwkv_w0[j], rwkv_w1[j], rwkv_w2[j],
                            rwkv_a0[j], rwkv_a1[j], rwkv_a2[j], rwkv_g1[j], rwkv_g2[j],
                            rwkv_k_k[j], rwkv_k_a[j], rwkv_r_k[j], rwkv_ln_g[j], rwkv_ln_b[j],
                            rwkv_w_out[j])
        else:
            y = s5_mixer(h, s5_a_re[j], s5_a_im[j], s5_log_step[j], s5_b_re[j], s5_b_im[j],
                         s5_c_re[j], s5_c_im[j], s5_d[j], s5_w_glu[j], s5_b_glu[j])
        x = x + y
        h = rms_norm(x, norm_ffn[i])
        x = x + conv_ffn(h, ffn_w_up[i], ffn_conv_w[i], ffn_conv_b[i], ffn_w_down[i])
    return x


_drawn_inputs = setup_inputs


def setup_inputs(seed=0):
    import zlib

    import numpy as np

    out = dict(_drawn_inputs(seed))
    spreads = {}
    factors = {'dsa_q_norm': 4.451,
     'dsa_k_norm': 4.213,
     'rwkv_w1': 7.374,
     'rwkv_w2': 7.357,
     'rwkv_k_k': 4.685,
     'rwkv_k_a': 3.178,
     'rwkv_ln_g': 3.234,
     'rwkv_ln_b': 4.805,
     's5_a_re': 8.0,
     's5_b_glu': 5.58,
     'ffn_conv_b': 2.714}
    for name, (base, spread) in spreads.items():
        noise = np.random.default_rng([zlib.crc32(name.encode()), seed]).standard_normal(out[name].shape)
        drawn = base * np.exp(spread * noise) if base else spread * noise
        out[name] = __import__('jax').numpy.asarray(drawn.astype(out[name].dtype))
    for name, factor in factors.items():
        out[name] = (out[name] * factor).astype(out[name].dtype)
    return out
```

```python
from contextlib import ExitStack

import numpy as np

import concourse.bass as bass
from concourse import mybir

ALU = mybir.AluOpType
ACT = mybir.ActivationFunctionType
AX_X = mybir.AxisListType.X
F32 = mybir.dt.float32

P = 128
D = 1024
T = 256
DEPTH = 4
DC = D // P
TT = T // P
HALF = 64
EPS = 1e-6
GN_EPS = 64e-5

DSA_HEADS = 16
IDX_HEADS = 8
TOPK = T // 4
Q_BLOCK = 64
F = 2816
FC = F // P
MASKED = -1e30
TAKEN = -3e38

TILE = 256
SLOT = DC * TILE
NSLOT = 6
NBANK = 6

CH = 32
NCH = T // CH
UNITS = 4

S5_L = 8
S5_N = T // S5_L
S5_G = 64
S5_C = 16
TWO_PI = 6.283185307179586

PAR = {}
_n = 0
for _name, _rows in (("ffn_conv_w", DEPTH * 3 * 2 * FC), ("ffn_conv_b", DEPTH * 2 * FC),
                     ("norm_mix", DEPTH * DC), ("norm_ffn", DEPTH * DC), ("rwkv_mu", 6 * DC),
                     ("rwkv_w0", DC), ("rwkv_a0", DC), ("rwkv_k_k", DC), ("rwkv_k_a", DC),
                     ("rwkv_ln_g", DC), ("rwkv_ln_b", DC), ("rwkv_r_k", DC), ("s5_d", DC),
                     ("s5_b_glu", 2 * DC), ("dsa_q_norm", 2), ("dsa_k_norm", 2), ("dsa_kidx_norm", 2)):
    PAR[_name] = (_n, _rows)
    _n += _rows
PAR_ROWS = _n
PAR_BLOCKS = -(-PAR_ROWS // P)


class Marks:

    def __init__(self, sem):
        self.sem, self.n = sem, 0

    def mark(self, ins):
        ins.then_inc(self.sem, 1)
        self.n = self.n + 1
        return self.n


class Plan:

    def __init__(self):
        self.tiles = []
        self.tile = {}
        self.release = {}
        self.slot_dmas = [0] * NSLOT
        self.fills = [0] * NBANK
        self.bank = {}

    def weights(self, key, dmas=1):
        n = len(self.tiles)
        slot = n % NSLOT
        self.slot_dmas[slot] += 16 * dmas
        self.tiles.append(key)
        self.tile[key] = (n, slot, self.slot_dmas[slot])

    def fill(self, key, bank):
        self.fills[bank] += 1
        self.bank[key] = (bank, self.fills[bank])


def make_plan(layers):
    plan = Plan()

    def simple(keys, dmas=1):
        for i, key in enumerate(keys):
            plan.weights(key, dmas)
            plan.fill(key, plan.next % NBANK)
            plan.next += 1
            plan.release[plan.tile[key][0]] = ("bank_full", plan.bank[key])

    plan.next = 0
    for L in layers:
        kind = L % 3
        plan.next = 0
        if kind == 0:
            simple([(L, s, i) for s in "qkv" for i in range(4)])
            simple([(L, "i", i) for i in range(2)])
            simple([(L, "s", 0)], 3)
            simple([(L, "o", i) for i in range(4)])
        elif kind == 1:
            simple([(L, s, i) for s in "rkv" for i in range(4)])
            simple([(L, "lora1", 0)], 3)
            plan.weights((L, "lora2", 0), 3)
            for s in "wag":
                for i in range(4):
                    plan.fill((L, s, i), plan.next % NBANK)
                    plan.next += 1
            plan.release[plan.tile[(L, "lora2", 0)][0]] = ("bank_full", plan.bank[(L, "g", 3)])
            simple([(L, "o", i) for i in range(4)])
        else:
            simple([(L, "glu", i) for i in range(8)])
        plan.next = 0
        simple([(L, "up", i) for i in range(2 * FC // 2)])
        for m in range(4):
            for g in range(3):
                plan.weights((L, "down", m, g))
            plan.fill((L, "down", m), 4 + m % 2)
            for g in range(3):
                n = plan.tile[(L, "down", m, g)][0]
                plan.release[n] = (("down_part", L), 2 * m + g + 1) if g < 2 else \
                    ("bank_full", plan.bank[(L, "down", m)])
    return plan


def trunk(nc, A, out, layers=(0, 1, 2, 3)):
    plan = make_plan(layers)
    ctx = ExitStack()
    with ctx:
        sems = {}

        def sem(*name):
            if name not in sems:
                sems[name] = ctx.enter_context(nc.semaphore("_".join(str(x) for x in name)))
            return sems[name]

        def sb(name, *shape):
            return ctx.enter_context(nc.sbuf_tensor(name, [P, *shape], F32))

        xT = sb("xT", DC, T)
        hT = sb("hT", DC, T)
        ring = sb("ring", NSLOT, SLOT)
        par = sb("par", PAR_BLOCKS * P)
        ident = sb("ident", P)
        mean_all = sb("mean_all", P)
        mean_head = sb("mean_head", P)
        sum_head = sb("sum_head", P)
        rstd = sb("rstd", T)
        masks = sb("masks", 4, P)
        pair_masks = sb("pair_masks", 6, P)
        chunk_cols = sb("chunk_cols", P // CH)
        chunk_reset = sb("chunk_reset", T)
        head_eye = sb("head_eye", HALF)
        chunk_decay = sb("chunk_decay", DC, NCH)
        causal = sb("causal", P)
        swap = sb("swap", P)
        sign = sb("sign", 1)
        half_pi = sb("half_pi", 1)
        lam8 = sb("lam8", 3, S5_G)
        eps = sb("eps", 2)
        work = sb("work", 16, 2048)
        banks = [ctx.enter_context(nc.psum_tensor(f"bank{i}", [P, 512], F32)) for i in range(8)]

        def slot_view(s, a, b):
            return work[:, s, 0:a * b].rearrange("p (a b) -> p a b", a=a)

        def col(name, i=0):
            base = PAR[name][0]
            return par[:, base + i:base + i + 1] if isinstance(i, int) else par[:, bass.ds(i + base, 1)]

        def bank_of(key):
            return banks[plan.bank[key][0]]

        def wait_full(eng, key, more=0):
            b, n = plan.bank[key]
            eng.wait_ge(sem("bank_full", b), n + more)

        per_layer = dict(tap2_done=2 * FC, tap1_done=2 * FC, taps_done=2 * FC, silu_done=FC // 2,
                         inner_ready=FC // 2, down_part=8,
                         qk_raw=8, qk_squares=8, qk_mean=8, qk_root=8, qk_normed=8, v_ready=4, qi_ready=2,
                         ki_raw=2, ki_squares=1, ki_mean=1, ki_root=1, ki_ready=1, logits=2, relu_done=6,
                         att_full=8, att_masked=16, neg_max=8, exp_done=32, pt_full=8, pt_copied=12,
                         o_full=8, o_scaled=8, ot_full=2, ot_copied=4)
        mlp_names = ("tap2_done", "tap1_done", "taps_done", "silu_done", "inner_ready", "down_part")

        def since(name, L):
            if name not in per_layer:
                return 0
            earlier = [x for x in layers if x < L and (name in mlp_names or x % 3 == 0)]
            return per_layer[name] * len(earlier)

        def signal(name):
            return sem(name[0]), since(*name) if len(name) > 1 else 0

        sq = slot_view(15, DC, T)

        def updates(L, ffn=0):
            return 4 * (1 + 2 * layers.index(L) + ffn)

        freed = {}
        for L in layers:
            if L % 3 == 0:
                for i in range(4):
                    freed[(L, "q", i)] = (("qk_raw", L), i + 1)
                    freed[(L, "k", i)] = (("qk_raw", L), 4 + i + 1)
                    freed[(L, "v", i)] = (("v_ready", L), i + 1)
                for i in range(2):
                    freed[(L, "i", i)] = (("qi_ready", L), i + 1)
                freed[(L, "s", 0)] = (("ki_raw", L), 2)
            if L % 3 == 1:
                for i in range(4):
                    for n, s in enumerate("rkv"):
                        freed[(L, s, i)] = (("rkv_ready", L), 4 * n + i + 1)
                    freed[(L, "w", i)] = (("wa_ready", L), 2 * i + 2)
                    freed[(L, "a", i)] = (("wa_ready", L), 8 + 2 * i + 2)
                    freed[(L, "g", i)] = (("g_ready", L), i + 1)
                freed[(L, "lora1", 0)] = (("lora_ready", L), 3)
            if L % 3 == 2:
                for m in range(4):
                    freed[(L, "glu", 2 * m)] = (("glu_ready", L), m + 1)
                    freed[(L, "glu", 2 * m + 1)] = (("glu_gate", L), 2 * m + 2)
            else:
                for m in range(4):
                    freed[(L, "o", m)] = (("x_ready",), updates(L) + m + 1)
            for j in range(FC // 2):
                freed[(L, "up", 2 * j)] = (("taps_done", L), 4 * j + 2)
                freed[(L, "up", 2 * j + 1)] = (("taps_done", L), 4 * j + 4)
            for m in range(4):
                freed[(L, "down", m)] = (("x_ready",), updates(L, 1) + m + 1)
        by_fill = {v: k for k, v in plan.bank.items()}

        def wait_free(pe, key, more=0):
            b, n = plan.bank[key]
            if n > 1:
                name, value = freed[by_fill[(b, n - 1)]]
                done, offset = signal(name)
                pe.wait_ge(done, value + offset + more)

        def landed(pe, key, rounds=0):
            _, slot, count = plan.tile[key]
            pe.wait_ge(sem("weights_in", slot), count + rounds)
            return ring[:, slot, :].rearrange("p (k n) -> p k n", n=TILE)

        def norm_squares(act, n):
            for m in range(4):
                act.wait_ge(sem("x_ready"), 4 * n + m + 1)
                act.activation(sq[:, 2 * m:2 * m + 2, :], xT[:, 2 * m:2 * m + 2, :],
                               ACT.Square).then_inc(sem("squares"), 1)

        def norm_mean(pe, n):
            for c in range(DC):
                if c % 2 == 0:
                    pe.wait_ge(sem("squares"), 4 * n + c // 2 + 1)
                mm = pe.matmul(banks[7][:, 0:T], mean_all[:, :], sq[:, c, :], start=c == 0, stop=c == DC - 1)
            mm.then_inc(sem("mean_square"), 1)

        def norm_root(act, n):
            act.wait_ge(sem("mean_square"), n + 1)
            act.activation(rstd[:, :], banks[7][:, 0:T], ACT.Sqrt, bias=eps[:, 0:1]).then_inc(sem("root"), 1)

        def norm_scale(dve, n, gain, L):
            dve.wait_ge(sem("root"), n + 1)
            dve.reciprocal(rstd[:, :], rstd[:, :]).then_inc(sem("rstd"), 1)
            dve.wait_ge(sem("rstd"), n + 1)
            for c in range(DC):
                dve.scalar_tensor_tensor(out=hT[:, c, :], in0=xT[:, c, :], scalar=col(gain, L * DC + c),
                                         in1=rstd[:, :], op0=ALU.mult, op1=ALU.mult).then_inc(sem("h_ready"), 1)

        def norm_index(L, ffn):
            return 2 * layers.index(L) + ffn

        def wait_h(eng, n, c=DC - 1):
            eng.wait_ge(sem("h_ready"), DC * n + c + 1)

        def project(pe, key, rhs, ready=None):
            w = landed(pe, key)
            wait_free(pe, key)
            for b in range(2):
                for k in range(DC):
                    if ready and b == 0:
                        ready(k)
                    mm = pe.matmul(bank_of(key)[:, b * T:(b + 1) * T], w[:, k, b * P:(b + 1) * P], rhs[:, k, :],
                                   start=k == 0, stop=k == DC - 1)
            mm.then_inc(sem("bank_full", plan.bank[key][0]), 1)

        def project_tokens(pe, key, lhs):
            w = landed(pe, key)
            wait_free(pe, key)
            for b in range(TT):
                for k in range(DC):
                    mm = pe.matmul(bank_of(key)[:, b * TILE:(b + 1) * TILE], lhs[:, k, b * P:(b + 1) * P], w[:, k, :],
                                   start=k == 0, stop=k == DC - 1)
            mm.then_inc(sem("bank_full", plan.bank[key][0]), 1)

        def add_residual(dve, L, s, start):
            for m in range(4):
                wait_full(dve, (L, s, m))
                pair = xT[:, 2 * m:2 * m + 2, :]
                dve.tensor_tensor(pair, pair, bank_of((L, s, m))[:, :].rearrange("p (a b) -> p a b", a=2),
                                  ALU.add).then_inc(sem("x_ready"), 1)

        def send(sp, key, pieces):
            n, slot, _ = plan.tile[key]
            if n >= NSLOT:
                (name, at) = plan.release[n - NSLOT]
                if name == "bank_full":
                    sp.wait_ge(sem("bank_full", at[0]), at[1])
                else:
                    done, offset = signal(name)
                    sp.wait_ge(done, at + offset)
            dst = ring[:, slot, :].rearrange("p (k n) -> p k n", n=TILE)
            for place, src in pieces(dst):
                sp.dma_start(place, src).then_inc(sem("weights_in", slot), 16)

        def rows(w, c0, k0=0, kn=DC, cn=TILE):
            v = w.rearrange("(k p) n -> p k n", p=P)
            cols = slice(c0, c0 + cn) if isinstance(c0, int) else bass.ds(c0, cn)
            return v[:, k0:k0 + kn, cols]

        def send_plain(sp, key, w, c0):
            send(sp, key, lambda dst: [(dst, rows(w, c0))])

        def send_dsa(sp, L):
            w = A["dsa_w_in"][L // 3]
            for n, s in enumerate("qkv"):
                for i in range(4):
                    send_plain(sp, (L, s, i), w, n * D + i * TILE)
            for i in range(2):
                send_plain(sp, (L, "i", i), w, 3 * D + i * TILE)
            c = 3 * D + IDX_HEADS * HALF
            send(sp, (L, "s", 0), lambda dst: [(dst[:, :, 0:HALF], rows(w, c, cn=HALF)),
                                               (dst[:, :, HALF:P], rows(w, c, cn=HALF)),
                                               (dst[:, :, P:P + IDX_HEADS], rows(w, c + HALF, cn=IDX_HEADS))])
            for i in range(4):
                send_plain(sp, (L, "o", i), A["dsa_w_out"][L // 3], i * TILE)

        def send_mlp(sp, L):
            up, down = A["ffn_w_up"][L], A["ffn_w_down"][L]

            def up_round(i, tiles):
                for k in range(tiles):
                    c0 = (k % 2) * F + (k // 2) * TILE + i * (3 * TILE)
                    key = (L, "up", k) if not isinstance(i, int) else (L, "up", k + 6 * i)
                    if isinstance(i, int):
                        send_plain(sp, key, up, c0)
                        continue
                    n, slot, _ = plan.tile[key]
                    b, full = plan.bank[key]
                    sp.wait_ge(sem("bank_full", b), full + i)
                    dst = ring[:, slot, :].rearrange("p (k n) -> p k n", n=TILE)
                    sp.dma_start(dst, rows(up, c0 + 3 * TILE)).then_inc(sem("weights_in", slot), 16)

            up_round(0, 6)
            with sp.Fori(0, 2) as i:
                up_round(i, 6)
            up_round(3, 4)
            for m in range(4):
                for g in range(3):
                    kn = min(DC, FC - g * DC)
                    send(sp, (L, "down", m, g),
                         lambda dst: [(dst[:, 0:kn, :], rows(down, m * TILE, g * DC, kn))])

        inner = work[:, 0:3, :].rearrange("p a b -> p (a b)")[:, 0:FC * T].rearrange("p (c t) -> p c t", t=T)
        conv = work[:, 3:5, :].rearrange("p a b -> p (a b)")[:, 0:3 * 1024].rearrange(
            "p (j h c t) -> p j h c t", j=3, h=2, c=2)
        UP_ROUNDS, UP_REST = divmod(FC // 2, 3)

        def mlp_pe(pe, L):
            n = norm_index(L, 1)

            def up_tile(k, i, first):
                key = (L, "up", k)
                w = landed(pe, key, 16 * i)
                if isinstance(i, int):
                    wait_free(pe, key)
                else:
                    name, value = freed[key]
                    done, offset = signal(name)
                    pe.wait_ge(done, (i - 1) * 12 + (value + offset))
                bank = plan.bank[key][0]
                for b in range(2):
                    for c in range(DC):
                        if first and b == 0:
                            wait_h(pe, n, c)
                        mm = pe.matmul(banks[bank][:, b * T:(b + 1) * T], w[:, c, b * P:(b + 1) * P], hT[:, c, :],
                                       start=c == 0, stop=c == DC - 1)
                mm.then_inc(sem("bank_full", bank), 1)

            for k in range(6):
                up_tile(k, 0, k == 0)
            with pe.Fori(1, UP_ROUNDS) as i:
                for k in range(6):
                    up_tile(k, i, False)
            for k in range(6 * UP_ROUNDS, 6 * UP_ROUNDS + 2 * UP_REST):
                up_tile(k, 0, False)
            for m in range(4):
                key = (L, "down", m)
                bank = plan.bank[key][0]
                wait_free(pe, key)
                for g in range(3):
                    w = landed(pe, (L, "down", m, g))
                    if m == 0:
                        pe.wait_ge(sem("inner_ready"), min(4 * (g + 1), FC // 2) + since("inner_ready", L))
                    kn = min(DC, FC - g * DC)
                    for b in range(2):
                        for k in range(kn):
                            mm = pe.matmul(banks[bank][:, b * T:(b + 1) * T], w[:, k, b * P:(b + 1) * P],
                                           inner[:, g * DC + k, :], start=g == 0 and k == 0 and b == 0,
                                           stop=g == 2 and k == kn - 1, skip_group_check=True)
                    mm.then_inc(sem("down_part") if g < 2 else sem("bank_full", bank), 1)

        def mlp_act(act, L):
            def step(j, i, jj):
                for h in range(2):
                    key = (L, "up", 2 * (j if isinstance(i, int) else jj) + h)
                    wait_full(act, key, 0 if isinstance(i, int) else i)
                    if not isinstance(i, int) or j >= 3:
                        act.wait_ge(sem("inner_ready"), j - 2 + since("inner_ready", L))
                    bank = bank_of(key)
                    for b in range(2):
                        c = h * FC + 2 * j + b
                        act.activation(conv[:, jj, h, b, :], bank[:, b * T:(b + 1) * T], ACT.Identity,
                                       bias=col("ffn_conv_b", c + L * 2 * FC),
                                       scale=col("ffn_conv_w", c + (L * 3 + 2) * 2 * FC)).then_inc(sem("tap2_done"), 1)
                act.wait_ge(sem("taps_done"), 4 * j + 2 + since("taps_done", L))
                act.activation(conv[:, jj, 0], conv[:, jj, 0], ACT.Silu).then_inc(sem("silu_done"), 1)

            for jj in range(3):
                step(jj, 0, jj)
            with act.Fori(1, UP_ROUNDS) as i:
                for jj in range(3):
                    step(i * 3 + jj, i, jj)
            for j in range(3 * UP_ROUNDS, FC // 2):
                step(j, 0, j % 3)

        def mlp_dve(dve, L):
            def step(j, i, jj):
                for h in range(2):
                    key = (L, "up", 2 * (j if isinstance(i, int) else jj) + h)
                    bank = bank_of(key)
                    for tap in (1, 0):
                        for b in range(2):
                            c = h * FC + 2 * j + b
                            lag = 2 - tap
                            if tap == 1:
                                dve.wait_ge(sem("tap2_done"), 4 * j + 2 * h + 2 + since("tap2_done", L))
                                done = sem("tap1_done")
                            else:
                                dve.wait_ge(sem("tap1_done"), 4 * j + 2 * h + b + 1 + since("tap1_done", L))
                                done = sem("taps_done")
                            row = conv[:, jj, h, b, lag:T]
                            dve.scalar_tensor_tensor(
                                out=row, in0=bank[:, b * T:(b + 1) * T - lag],
                                scalar=col("ffn_conv_w", c + (L * 3 + tap) * 2 * FC),
                                in1=row, op0=ALU.mult, op1=ALU.add).then_inc(done, 1)
                dve.wait_ge(sem("silu_done"), j + 1 + since("silu_done", L))
                dve.wait_ge(sem("taps_done"), 4 * j + 4 + since("taps_done", L))
                pair = slice(2 * j, 2 * j + 2) if isinstance(i, int) else bass.ds(j * 2, 2)
                dve.tensor_tensor(inner[:, pair, :], conv[:, jj, 0], conv[:, jj, 1],
                                  ALU.mult).then_inc(sem("inner_ready"), 1)

            for jj in range(3):
                step(jj, 0, jj)
            with dve.Fori(1, UP_ROUNDS) as i:
                for jj in range(3):
                    step(i * 3 + jj, i, jj)
            for j in range(3 * UP_ROUNDS, FC // 2):
                step(j, 0, j % 3)
            add_residual(dve, L, "down", updates(L, 1))

        qT, kT = slot_view(0, DC, T), slot_view(1, DC, T)
        v_tok = slot_view(2, TT, D)
        qiT = work[:, 3, 0:1024].rearrange("p (c t) -> p c t", t=T)
        kiT = work[:, 3, 1024:1280]
        ki_sq = work[:, 3, 1280:1536]
        rs_qk = work[:, 7, 0:1024].rearrange("p (b n) -> p b n", b=2)
        qk_sq = work[:, 4, 0:1024].rearrange("p (b n) -> p b n", b=2)
        relu = [work[:, 4, 1024:2048].rearrange("p (h k) -> p h k", h=IDX_HEADS),
                work[:, 5, :].rearrange("p (h k) -> p h k", h=IDX_HEADS)]
        score = [work[:, 6, 0:128], work[:, 6, 256:512]]
        bias = [work[:, 6, 512:640], work[:, 6, 768:1024]]
        top8 = work[:, 6, 1024:1032]
        w_idx = work[:, 6, 1040:1056]
        row_max = work[:, 6, 1056:1088]
        neg_max = work[:, 6, 1088:1120]
        row_sum = work[:, 6, 1120:1152]
        recip = work[:, 6, 1152:1184]
        att = work[:, 7, :].rearrange("p (b n) -> p b n", b=2)
        prob = work[:, 8, :].rearrange("p (b n) -> p b n", b=2)
        probT = work[:, 9, :].rearrange("p (b n) -> p b n", b=2)
        o_tok = slot_view(10, TT, D)
        oT = slot_view(11, DC, T)
        HG = 4
        NU = TT * DSA_HEADS // HG

        def unit(u):
            qt, g = divmod(u, DSA_HEADS // HG)
            return qt, HG * g, qt + 1

        def before(u):
            return sum(unit(x)[2] for x in range(u))

        def order(h0, i):
            return h0 + 2 * (i % 2) + i // 2

        IDX_ORDER = [0, 2, 4, 6, 1, 3, 5, 7]

        def heads(x, h):
            return x[HALF * (h % 2):HALF * (h % 2) + HALF, h // 2, :]

        def dsa_pe(pe, L):
            n = norm_index(L, 0)

            def mean_square(i):
                pe.wait_ge(sem("qk_raw"), i + 1 + since("qk_raw", L))
                if i >= 2:
                    pe.wait_ge(sem("qk_root"), i - 1 + since("qk_root", L))
                pe.matmul(banks[6 + i % 2][:, :], mean_head[:, :], qk_sq[:, i % 2, :], start=True,
                          stop=True).then_inc(sem("qk_mean"), 1)

            for i, key in enumerate([(L, s, i) for s in "qk" for i in range(4)]):
                project(pe, key, hT, (lambda c: wait_h(pe, n, c)) if i == 0 else None)
                if i:
                    mean_square(i - 1)
            project_tokens(pe, (L, "v", 0), hT)
            mean_square(7)
            for i in range(1, 4):
                project_tokens(pe, (L, "v", i), hT)
            for i in range(2):
                project(pe, (L, "i", i), hT)
            key = (L, "s", 0)
            w = landed(pe, key)
            wait_free(pe, key)
            bank = bank_of(key)
            for k in range(DC):
                pe.matmul(bank[:, 0:T], w[:, k, 0:P], hT[:, k, :], start=k == 0, stop=k == DC - 1)
            for b in range(TT):
                for k in range(DC):
                    mm = pe.matmul(bank[:, T + b * IDX_HEADS:T + (b + 1) * IDX_HEADS], hT[:, k, b * P:(b + 1) * P],
                                   w[:, k, P:P + IDX_HEADS], start=k == 0, stop=k == DC - 1)
            mm.then_inc(sem("bank_full", plan.bank[key][0]), 1)
            pe.wait_ge(sem("ki_raw"), 2 + since("ki_raw", L))
            pe.matmul(banks[6][:, 0:T], mean_head[:, :], ki_sq, start=True, stop=True).then_inc(sem("ki_mean"), 1)

            def scores(u):
                qt, h0, nk = unit(u)
                if u >= 2:
                    pe.wait_ge(sem("att_masked"), 2 * (u - 1) + since("att_masked", L))
                for i in range(HG):
                    bank = banks[2 * (u % 2) + i // 2]
                    at = (i % 2) * nk * P
                    h = order(h0, i)
                    mm = pe.matmul(bank[:, at:at + nk * P], heads(qT, h)[:, qt * P:(qt + 1) * P],
                                   heads(kT, h)[:, 0:nk * P], start=True, stop=True)
                mm.then_inc(sem("att_full"), 1)

            pe.wait_ge(sem("ki_ready"), 1 + since("ki_ready", L))
            for qt, first, per in ((0, 4, 4), (1, 0, 2)):
                kw = (qt + 1) * P
                for i, h in enumerate(IDX_ORDER):
                    at = (i % per) * kw
                    mm = pe.matmul(banks[first + i // per][:, at:at + kw],
                                   heads(qiT, h)[:, qt * P:(qt + 1) * P],
                                   kiT[HALF * (h % 2):HALF * (h % 2) + HALF, 0:kw], start=True, stop=True)
                mm.then_inc(sem("logits"), 1)

            def turn(u):
                qt, h0, nk = unit(u)
                pe.wait_ge(sem("exp_done"), HG * (u + 1) + since("exp_done", L))
                if u:
                    pe.wait_ge(sem("pt_copied"), before(u) + since("pt_copied", L))
                for i in range(HG * nk):
                    mm = pe.transpose(banks[4 + i // 4][:, (i % 4) * P:(i % 4 + 1) * P],
                                      prob[:, u % 2, i * P:(i + 1) * P], ident[:, :])
                mm.then_inc(sem("pt_full"), 1)

            def values(u):
                qt, h0, nk = unit(u)
                pe.wait_ge(sem("pt_copied"), before(u + 1) + since("pt_copied", L))
                if u >= 2:
                    pe.wait_ge(sem("o_scaled"), u - 1 + since("o_scaled", L))
                for i in range(HG):
                    h = order(h0, i)
                    for kt in range(nk):
                        at = (i * nk + kt) * P
                        mm = pe.matmul(banks[6 + u % 2][:, (h - h0) * HALF:(h - h0 + 1) * HALF], probT[:, u % 2, at:at + P],
                                       v_tok[:, kt, h * HALF:(h + 1) * HALF], start=kt == 0, stop=kt == nk - 1)
                mm.then_inc(sem("o_full"), 1)

            pe.wait_ge(sem("relu_done"), 6 + since("relu_done", L))
            scores(0)
            for u in range(NU):
                if u + 1 < NU:
                    scores(u + 1)
                turn(u)
                values(u)
            pe.wait_ge(sem("o_scaled"), NU + since("o_scaled", L))
            for qt in range(TT):
                for c in range(DC):
                    mm = pe.transpose(banks[2 * qt + c // 4][:, (c % 4) * P:(c % 4 + 1) * P],
                                      o_tok[:, qt, c * P:(c + 1) * P], ident[:, :])
                mm.then_inc(sem("ot_full"), 1)
            pe.wait_ge(sem("ot_copied"), 4 + since("ot_copied", L))
            for m in range(4):
                project(pe, (L, "o", m), oT)

        def dsa_act(act, L):
            def root(i):
                act.wait_ge(sem("qk_mean"), i + 1 + since("qk_mean", L))
                if i >= 2:
                    act.wait_ge(sem("qk_normed"), i - 1 + since("qk_normed", L))
                act.activation(rs_qk[:, i % 2, :], banks[6 + i % 2][:, :], ACT.Sqrt,
                               bias=eps[:, 0:1]).then_inc(sem("qk_root"), 1)

            for i, key in enumerate([(L, s, i) for s in "qk" for i in range(4)]):
                x = qT if i < 4 else kT
                m = i % 4
                wait_full(act, key)
                if i >= 2:
                    act.wait_ge(sem("qk_mean"), i - 1 + since("qk_mean", L))
                act.activation(qk_sq[:, i % 2, :], bank_of(key)[:, :], ACT.Square).then_inc(sem("qk_squares"), 1)
                act.activation(x[:, 2 * m:2 * m + 2, :].rearrange("p a b -> p (a b)"), bank_of(key)[:, :],
                               ACT.Copy).then_inc(sem("qk_raw"), 1)
                if i:
                    root(i - 1)
            root(7)
            for i in range(4):
                wait_full(act, (L, "v", i))
                act.activation(v_tok[:, :, i * TILE:(i + 1) * TILE],
                               bank_of((L, "v", i))[:, :].rearrange("p (a b) -> p a b", a=TT),
                               ACT.Copy).then_inc(sem("v_ready"), 1)
            for i in range(2):
                wait_full(act, (L, "i", i))
                act.activation(qiT[:, 2 * i:2 * i + 2, :].rearrange("p a b -> p (a b)"), bank_of((L, "i", i))[:, :],
                               ACT.Copy).then_inc(sem("qi_ready"), 1)
            key = (L, "s", 0)
            wait_full(act, key)
            act.activation(ki_sq, bank_of(key)[:, 0:T], ACT.Square).then_inc(sem("ki_squares"), 1)
            act.activation(kiT, bank_of(key)[:, 0:T], ACT.Copy).then_inc(sem("ki_raw"), 1)
            act.activation(w_idx, bank_of(key)[:, T:T + TT * IDX_HEADS], ACT.Copy,
                           scale=IDX_HEADS ** -0.5).then_inc(sem("ki_raw"), 1)
            act.wait_ge(sem("ki_mean"), 1 + since("ki_mean", L))
            act.wait_ge(sem("qk_normed"), 7 + since("qk_normed", L))
            act.activation(rs_qk[:, 0, 0:T], banks[6][:, 0:T], ACT.Sqrt, bias=eps[:, 0:1]).then_inc(sem("ki_root"), 1)
            for qt, first, per in ((0, 4, 4), (1, 0, 2)):
                act.wait_ge(sem("logits"), qt + 1 + since("logits", L))
                for b in range(IDX_HEADS // per):
                    act.activation(relu[qt][:, b * per:(b + 1) * per, :].rearrange("p a b -> p (a b)"),
                                   banks[first + b][:, :], ACT.Relu,
                                   scale=HALF ** -0.5).then_inc(sem("relu_done"), 1)

            def copy_turned(u):
                _, _, nk = unit(u)
                act.wait_ge(sem("pt_full"), u + 1 + since("pt_full", L))
                if u >= 2:
                    act.wait_ge(sem("o_full"), u - 1 + since("o_full", L))
                for b in range(nk):
                    act.activation(probT[:, u % 2, b * 512:(b + 1) * 512], banks[4 + b][:, :],
                                   ACT.Copy).then_inc(sem("pt_copied"), 1)

            for u in range(NU):
                qt, h0, nk = unit(u)
                act.wait_ge(sem("neg_max"), u + 1 + since("neg_max", L))
                if u >= 2:
                    act.wait_ge(sem("pt_full"), u - 1 + since("pt_full", L))
                for i in range(HG):
                    r = slice(i * nk * P, (i + 1) * nk * P)
                    n, m = u * HG + i, u * HG + order(0, i)
                    act.activation(prob[:, u % 2, r], att[:, u % 2, r], ACT.Exp, bias=neg_max[:, n:n + 1],
                                   scale=HALF ** -0.5, accum_out=row_sum[:, m:m + 1]).then_inc(sem("exp_done"), 1)
                if u:
                    copy_turned(u - 1)
            copy_turned(NU - 1)
            for qt in range(TT):
                act.wait_ge(sem("ot_full"), qt + 1 + since("ot_full", L))
                for b in range(2):
                    act.activation(oT[:, 4 * b:4 * b + 4, qt * P:(qt + 1) * P],
                                   banks[2 * qt + b][:, :].rearrange("p (a b) -> p a b", a=4),
                                   ACT.Copy).then_inc(sem("ot_copied"), 1)

        dsa_step = Marks(sem("dsa_step"))

        def dsa_dve(dve, L):
            j = L // 3
            step = dsa_step

            def then(ins):
                dve.wait_ge(step.sem, step.mark(ins))

            for i in range(8):
                x = qT if i < 4 else kT
                m = i % 4
                dve.wait_ge(sem("qk_root"), i + 1 + since("qk_root", L))
                then(dve.reciprocal(rs_qk[:, i % 2, :], rs_qk[:, i % 2, :]))
                pair = x[:, 2 * m:2 * m + 2, :].rearrange("p a b -> p (a b)")
                dve.scalar_tensor_tensor(out=pair, in0=pair, scalar=col("dsa_q_norm" if i < 4 else "dsa_k_norm", j),
                                         in1=rs_qk[:, i % 2, :], op0=ALU.mult, op1=ALU.mult).then_inc(sem("qk_normed"), 1)
            dve.wait_ge(sem("ki_root"), 1 + since("ki_root", L))
            then(dve.reciprocal(rs_qk[:, 0, 0:T], rs_qk[:, 0, 0:T]))
            dve.scalar_tensor_tensor(out=kiT, in0=kiT, scalar=col("dsa_kidx_norm", j), in1=rs_qk[:, 0, 0:T],
                                     op0=ALU.mult, op1=ALU.mult).then_inc(sem("ki_ready"), 1)
            for qt in range(TT):
                s = score[qt]
                w = w_idx[:, qt * IDX_HEADS:(qt + 1) * IDX_HEADS]
                dve.wait_ge(sem("relu_done"), 2 + 4 * qt + since("relu_done", L))
                then(dve.tensor_scalar(s, relu[qt][:, 0, :], w[:, 0:1], None, ALU.mult))
                for i, h in list(enumerate(IDX_ORDER))[1:]:
                    then(dve.scalar_tensor_tensor(out=s, in0=relu[qt][:, i, :], scalar=w[:, h:h + 1], in1=s,
                                                  op0=ALU.mult, op1=ALU.add))
                then(dve.memset(s[0:Q_BLOCK, qt * P + Q_BLOCK:(qt + 1) * P], MASKED))
                for _ in range(TOPK // 8):
                    then(dve.max(top8, s))
                    then(dve.match_replace(s, top8, s, TAKEN))
                then(dve.tensor_scalar(bias[qt], s, TAKEN / 2, MASKED, ALU.is_gt, ALU.mult))

            def scale_values(u):
                qt, h0, _ = unit(u)
                dve.wait_ge(sem("o_full"), u + 1 + since("o_full", L))
                r = slice(u * HG, (u + 1) * HG)
                then(dve.reciprocal(recip[:, r], row_sum[:, r]))
                o = o_tok[:, qt, h0 * HALF:(h0 + HG) * HALF].rearrange("p (h d) -> p h d", h=HG)
                dve.tensor_tensor(o, banks[6 + u % 2][:, 0:HG * HALF].rearrange("p (h d) -> p h d", h=HG),
                                  recip[:, r].unsqueeze(2).to_broadcast([P, HG, HALF]),
                                  ALU.mult).then_inc(sem("o_scaled"), 1)

            for u in range(NU):
                qt, h0, nk = unit(u)
                dve.wait_ge(sem("att_full"), u + 1 + since("att_full", L))
                if u >= 2:
                    dve.wait_ge(sem("exp_done"), HG * (u - 1) + since("exp_done", L))
                w = 2 * nk * P
                for b in range(2):
                    dve.tensor_tensor(
                        att[:, u % 2, b * w:(b + 1) * w].rearrange("p (h k) -> p h k", h=2),
                        banks[2 * (u % 2) + b][:, 0:w].rearrange("p (h k) -> p h k", h=2),
                        bias[qt].unsqueeze(1).to_broadcast([P, 2, nk * P]),
                        ALU.add).then_inc(sem("att_masked"), 1)
                dve.wait_ge(sem("att_masked"), 2 * (u + 1) + since("att_masked", L))
                r = slice(u * HG, (u + 1) * HG)
                then(dve.tensor_reduce(row_max[:, r], att[:, u % 2, 0:512 * nk].rearrange("p (h k) -> p h k", h=HG),
                                       AX_X, ALU.max))
                dve.tensor_scalar(neg_max[:, r], row_max[:, r], -HALF ** -0.5, None,
                                  ALU.mult).then_inc(sem("neg_max"), 1)
                if u:
                    scale_values(u - 1)
            scale_values(NU - 1)
            add_residual(dve, L, "o", updates(L))

        flat = work[:, :, :].rearrange("p a b -> p (a b)")
        big = flat[:, 0:4 * 2048].rearrange("p (h s t) -> p h s t", h=DC, s=4)
        PT_all = flat[:, 0:4 * 2048].rearrange("p (h s c j) -> p h s c j", h=DC, s=2, j=HALF)
        rT, bonus, gT, y0T = (slot_view(i, DC, T) for i in (4, 5, 6, 7))
        dh = slot_view(8, DC, T)
        mixed = [slot_view(i, DC, T) for i in (9, 10, 11)]
        kraw, sg, aT = (slot_view(i, DC, T) for i in (12, 14, 15))
        hidden = work[:, 7, 0:512]
        csum, e_prev, e_in, e_neg = (slot_view(i, DC, T) for i in (8, 9, 10, 11))
        kk, tmp7 = slot_view(5, DC, T), slot_view(7, DC, T)
        inv, rk = hT, hT
        GROUP = 5888
        SHARED = 8 * 2048 + 2 * GROUP

        def group(par_, first, n):
            base = 8 * 2048 + par_ * GROUP + first
            return flat[:, base:base + n]

        MM = [group(p, 0, 2560).rearrange("p (s u t) -> p s u t", s=5, t=P) for p in (0, 1)]
        Tm = [group(p, 2560, 512) for p in (0, 1)]
        TmT = [group(p, 3072, 512) for p in (0, 1)]
        Zm = [group(p, 3584, 512) for p in (0, 1)]
        M12 = [group(p, 4096, 512).rearrange("p (s u d) -> p s u d", s=2, d=HALF) for p in (0, 1)]
        AkV = [group(p, 4608, 256) for p in (0, 1)]
        Nat = [group(p, 4864, 1024).rearrange("p (s u d) -> p s u d", s=4, d=HALF) for p in (0, 1)]
        BX, VX, M2X = (flat[:, SHARED + i * 1024:SHARED + (i + 1) * 1024] for i in range(3))
        NLEV = 4

        def send_rwkv(sp, L):
            for n, s in enumerate("rkv"):
                for i in range(4):
                    send_plain(sp, (L, s, i), A["rwkv_w_rkv"][0, n], i * TILE)
            send(sp, (L, "lora1", 0), lambda dst: [(dst[:, :, 0:HALF], rows(A["rwkv_w1"][0], 0, cn=HALF)),
                                                   (dst[:, :, HALF:P], rows(A["rwkv_a1"][0], 0, cn=HALF)),
                                                   (dst[:, :, P:2 * P], rows(A["rwkv_g1"][0], 0, cn=P))])

            def second(dst):
                wide = dst.rearrange("p k n -> p (k n)")
                return [(wide[0:HALF, 0:D], A["rwkv_w2"][0]), (wide[HALF:P, 0:D], A["rwkv_a2"][0]),
                        (wide[:, D:2 * D], A["rwkv_g2"][0])]

            send(sp, (L, "lora2", 0), second)
            for i in range(4):
                send_plain(sp, (L, "o", i), A["rwkv_w_out"][0], i * TILE)

        def level(l, hp):
            return (hp // 2) * 2 * NLEV + 2 * l + hp % 2 + 1

        def by_pairs(steps):
            for g in range(0, DC, 2):
                for step in steps:
                    for hp in (g, g + 1):
                        step(hp)

        def half_rows(h):
            return slice(HALF * h, HALF * h + HALF)

        def rwkv_pe(pe, L):
            for n, s in enumerate("rkv"):
                for i in range(4):
                    project(pe, (L, s, i), mixed[n % 3],
                            (lambda c, n=n: pe.wait_ge(sem("mixed"), DC * n + c + 1)) if i == 0 else None)
            key = (L, "lora1", 0)
            w = landed(pe, key)
            wait_free(pe, key)
            bank = bank_of(key)
            pe.wait_ge(sem("mixed"), 6 * DC)
            for dst, c0, c1, x in ((bank[0:HALF, 0:T], 0, HALF, mixed[0]), (bank[HALF:P, 0:T], HALF, P, mixed[1]),
                                   (bank[:, T:2 * T], P, 2 * P, mixed[2])):
                for k in range(DC):
                    mm = pe.matmul(dst, w[:, k, c0:c1], x[:, k, :], start=k == 0, stop=k == DC - 1)
            mm.then_inc(sem("bank_full", plan.bank[key][0]), 1)
            w = landed(pe, (L, "lora2", 0)).rearrange("p k n -> p (k n)")
            pe.wait_ge(sem("lora_ready"), 3)
            for s, r, c0, x in (("w", slice(0, HALF), 0, hidden[:, 0:T]), ("a", slice(HALF, P), 0, hidden[:, 0:T]),
                                ("g", slice(0, P), D, hidden[:, T:2 * T])):
                for i in range(4):
                    key = (L, s, i)
                    wait_free(pe, key)
                    for b in range(2):
                        c = c0 + (2 * i + b) * P
                        mm = pe.matmul(bank_of(key)[:, b * T:(b + 1) * T], w[r, c:c + P], x[r, :], start=True, stop=True)
                    mm.then_inc(sem("bank_full", plan.bank[key][0]), 1)
            pe.wait_ge(sem("g_ready"), 4)
            for m in range(4):
                pe.wait_ge(sem("kk_squares"), m + 1)
                pe.matmul(banks[m][:, :], sum_head[:, :], tmp7[:, 2 * m:2 * m + 2, :], start=True,
                          stop=True).then_inc(sem("kk_sum"), 1)
            for m in range(4):
                pe.wait_ge(sem("rk_done"), 2 * m + 2)
                if m >= 2:
                    pe.wait_ge(sem("bonus_done"), m - 1)
                pe.matmul(banks[4 + m % 2][:, :], sum_head[:, :], rk[:, 2 * m:2 * m + 2, :], start=True,
                          stop=True).then_inc(sem("rk_sum"), 1)
            pe.wait_ge(sem("bonus_done"), 4)
            pe.wait_ge(sem("factors_done"), 4)

            def bank3(hp):
                return banks[3 * (hp % 2):3 * (hp % 2) + 3]

            def natural(hp):
                X, Y, _ = bank3(hp)
                if hp >= 2:
                    pe.wait_ge(sem("r1_done"), hp - 1)
                    pe.wait_ge(sem("y0_done"), hp - 1)
                for s in range(4):
                    for b in range(TT):
                        mm = pe.transpose((X, Y)[s // 2][:, ((s % 2) * 2 + b) * P:((s % 2) * 2 + b + 1) * P],
                                          big[:, hp, s, b * P:(b + 1) * P], ident[:, :])
                mm.then_inc(sem("nat_full"), 1)

            def products(hp, h):
                X, Y, Z = bank3(hp)
                pe.wait_ge(*((sem("nat_done"), 2 * hp + 2) if h == 0 else (sem("a0_done"), 3 * hp + 3)))
                if h == 0 and hp >= 2:
                    pe.wait_ge(sem("pt_done"), hp - 1)
                r = half_rows(h)
                a, b, k = (big[r, hp, s, :] for s in range(3))
                rr = rT[r, hp, :]
                for n, (lhs, rhs) in enumerate(((a, b), (b, a), (b, rr), (k, a), (k, rr))):
                    for t in range(TT):
                        c = slice(t * P, (t + 1) * P)
                        at = ((n % 2) * 2 + t) * P
                        mm = pe.matmul((X, Y, Z)[n // 2][:, at:at + P], lhs[:, c], rhs[:, c], start=True, stop=True)
                mm.then_inc(sem(f"a{h}_full"), 1)

            def unit_cols(u, n=P):
                return slice(u * n, (u + 1) * n)

            def akv(hp):
                pe.wait_ge(sem("a1_done"), 3 * hp + 3)
                if hp >= 2:
                    pe.wait_ge(sem("q_done"), hp - 1)
                p = hp % 2
                for u in range(UNITS):
                    mm = pe.matmul(banks[6 + p][:, unit_cols(u, HALF)], MM[p][:, 3, u, :], Nat[p][:, 3, u, :],
                                   start=True, stop=True)
                mm.then_inc(sem("akv_full"), 1)

            def z_product(l):
                def step(hp):
                    p = hp % 2
                    pe.wait_ge(*((sem("base_done"), hp + 1) if l == 0 else (sem("tt_done"), level(l - 1, hp))))
                    for u in range(UNITS):
                        mm = pe.matmul(bank3(hp)[0][:, unit_cols(u)], MM[p][:, 1, u, :], Tm[p][:, unit_cols(u)],
                                       start=True, stop=True)
                    mm.then_inc(sem("z_full"), 1)
                return step

            def t_product(l):
                def step(hp):
                    p = hp % 2
                    _, Y, Z = bank3(hp)
                    pe.wait_ge(sem("z_done"), level(l, hp))
                    for u in range(UNITS):
                        c = unit_cols(u)
                        mm = pe.matmul(Y[:, c], Zm[p][:, c], TmT[p][:, c], start=True, stop=True)
                    if l < NLEV - 1:
                        for u in range(UNITS):
                            c = unit_cols(u)
                            mm = pe.matmul(Z[:, c], TmT[p][:, c], Zm[p][:, c], start=True, stop=True)
                    mm.then_inc(sem("t_full"), 1)
                return step

            def solve(hp):
                p = hp % 2
                pe.wait_ge(sem("tt_done"), level(NLEV - 1, hp))
                pe.wait_ge(sem("akv_done"), hp + 1)
                for u in range(UNITS):
                    pe.matmul(banks[6 + p][:, unit_cols(u, HALF)], TmT[p][:, unit_cols(u)], Nat[p][:, 0, u, :],
                              start=True, stop=True)
                    mm = pe.matmul(banks[6 + p][:, 256 + u * HALF:256 + (u + 1) * HALF], TmT[p][:, unit_cols(u)],
                                   AkV[p][:, unit_cols(u, HALF)], start=True, stop=True)
                mm.then_inc(sem("m_full"), 1)

            def outputs(hp):
                p = hp % 2
                X, Y, _ = bank3(hp)
                pe.wait_ge(sem("m_done"), hp + 1)
                for u in range(UNITS):
                    t, h = divmod(u, 2)
                    r, c = half_rows(h), slice(t * P, (t + 1) * P)
                    pe.matmul(X[r, c], M12[p][:, 0, u, :], MM[p][:, 2, u, :], start=True, stop=True)
                    pe.matmul(Y[r, c], M12[p][:, 1, u, :], MM[p][:, 2, u, :], start=True, stop=False)
                    mm = pe.matmul(Y[r, c], Nat[p][:, 3, u, :], MM[p][:, 4, u, :], start=False, stop=True)
                mm.then_inc(sem("ry_full"), 1)

            def transitions(hp):
                p = hp % 2
                Z, Q = bank3(hp)[2], banks[6 + p]
                pe.wait_ge(sem("expanded"), 3 * hp + 3)
                for u in range(UNITS):
                    t, h = divmod(u, 2)
                    r, c = half_rows(h), slice(t * 256, (t + 1) * 256)
                    x = slice(u * 256, (u + 1) * 256)
                    pe.matmul(Z[r, c], M12[p][:, 0, u, :], BX[:, x], start=True, stop=True)
                    pe.matmul(Q[r, c], Nat[p][:, 1, u, :], M2X[:, x], start=True, stop=False)
                    mm = pe.matmul(Q[r, c], Nat[p][:, 2, u, :], VX[:, x], start=False, stop=True)
                mm.then_inc(sem("pq_full"), 1)

            levels = [f(l) for l in range(NLEV) for f in (z_product, t_product)]
            by_pairs([natural, lambda hp: products(hp, 0), lambda hp: products(hp, 1), akv, *levels, solve,
                      outputs, transitions])
            pe.wait_ge(sem("q_done"), DC)
            pe.wait_ge(sem("y0_done"), DC)
            for c in range(1, NCH - 1):
                for q in range(2):
                    if c > 1:
                        pe.wait_ge(sem("state_done"), 8 * (2 * (c - 2) + q + 1))
                    for i in range(4):
                        hp = 4 * q + i
                        for h in range(2):
                            r = half_rows(h)
                            mm = pe.matmul(banks[2 * q + h][r, i * HALF:(i + 1) * HALF], PT_all[r, hp, 0, c, :],
                                           PT_all[r, hp, 1, c - 1, :], start=True, stop=True)
                    mm.then_inc(sem("state_full"), 1)
            pe.wait_ge(sem("state_done"), 16 * (NCH - 2))
            for q in range(4):
                if q >= 3:
                    pe.wait_ge(sem("y_done"), 2 * (q - 2))
                for h in range(2):
                    for hp in (2 * q, 2 * q + 1):
                        for c in range(1, NCH):
                            r = half_rows(h)
                            at = (hp % 2) * T + c * CH
                            mm = pe.matmul(banks[2 * (q % 3) + h][r, at:at + CH], PT_all[r, hp, 1, c - 1, :],
                                           rT[r, hp, c * CH:(c + 1) * CH], start=True, stop=True)
                mm.then_inc(sem("y_full"), 1)
            for q in range(4):
                pe.wait_ge(sem("y_done"), 2 * q + 2)
                if q >= 1:
                    pe.wait_ge(sem("centred"), q)
                pe.matmul(banks[6][:, :], mean_head[:, :], y0T[:, 2 * q:2 * q + 2, :], start=True,
                          stop=True).then_inc(sem("y_mean"), 1)
                pe.wait_ge(sem("y_squares"), q + 1)
                if q >= 1:
                    pe.wait_ge(sem("y_root"), q)
                pe.matmul(banks[7][:, :], mean_head[:, :], slot_view(9, DC, T)[:, 2 * q:2 * q + 2, :], start=True,
                          stop=True).then_inc(sem("y_var"), 1)
            for m in range(4):
                project(pe, (L, "o", m), y0T, (lambda c: pe.wait_ge(sem("gated"), c // 2 + 1)) if m == 0 else None)

        def rwkv_act(act, L):
            dsts = (rT, kraw, None)
            for n, s in enumerate("rkv"):
                for i in range(4):
                    wait_full(act, (L, s, i))
                    dst = big[:, 2 * i:2 * i + 2, 3, :] if s == "v" else dsts[n][:, 2 * i:2 * i + 2, :]
                    act.activation(dst, bank_of((L, s, i))[:, :].rearrange("p (a b) -> p a b", a=2),
                                   ACT.Copy).then_inc(sem("rkv_ready"), 1)
            key = (L, "lora1", 0)
            wait_full(act, key)
            act.activation(hidden[0:HALF, 0:T], bank_of(key)[0:HALF, 0:T], ACT.Tanh).then_inc(sem("lora_ready"), 1)
            act.activation(hidden[HALF:P, 0:T], bank_of(key)[HALF:P, 0:T], ACT.Copy).then_inc(sem("lora_ready"), 1)
            act.activation(hidden[:, T:2 * T], bank_of(key)[:, T:2 * T], ACT.Sigmoid).then_inc(sem("lora_ready"), 1)
            for s, dst, b0 in (("w", sg, "rwkv_w0"), ("a", aT, "rwkv_a0")):
                for i in range(4):
                    key = (L, s, i)
                    wait_full(act, key)
                    for b in range(2):
                        act.activation(dst[:, 2 * i + b, :], bank_of(key)[:, b * T:(b + 1) * T], ACT.Sigmoid,
                                       bias=col(b0, 2 * i + b)).then_inc(sem("wa_ready"), 1)
            for i in range(4):
                key = (L, "g", i)
                wait_full(act, key)
                act.activation(gT[:, 2 * i:2 * i + 2, :].rearrange("p a b -> p (a b)"), bank_of(key)[:, :],
                               ACT.Copy).then_inc(sem("g_ready"), 1)
            for m in range(4):
                act.wait_ge(sem("kk_raw"), 2 * m + 2)
                act.activation(tmp7[:, 2 * m:2 * m + 2, :], kk[:, 2 * m:2 * m + 2, :],
                               ACT.Square).then_inc(sem("kk_squares"), 1)
            for m in range(4):
                act.wait_ge(sem("kk_sum"), m + 1)
                act.activation(inv[:, 2 * m:2 * m + 2, :].rearrange("p a b -> p (a b)"), banks[m][:, :],
                               ACT.Sqrt).then_inc(sem("kk_root"), 1)
            act.wait_ge(sem("csum_done"), 2)
            for dst, src, scale in ((e_prev, e_prev, 1.0), (e_in, csum, 1.0), (e_neg, csum, -1.0)):
                act.activation(dst[:, :, :], src[:, :, :], ACT.Exp, scale=scale).then_inc(sem("exps_done"), 1)

            def nat_copy(hp):
                p = hp % 2
                act.wait_ge(sem("nat_full"), hp + 1)
                for i in range(2):
                    act.activation(Nat[p][:, 2 * i:2 * i + 2, :, :].rearrange("p a b c -> p (a b c)"),
                                   banks[3 * p + i][:, :], ACT.Copy).then_inc(sem("nat_done"), 1)

            def akv_copy(hp):
                p = hp % 2
                act.wait_ge(sem("akv_full"), hp + 1)
                act.activation(AkV[p], banks[6 + p][:, 0:256], ACT.Copy).then_inc(sem("akv_done"), 1)

            def m_copy(hp):
                p = hp % 2
                act.wait_ge(sem("m_full"), hp + 1)
                act.activation(M12[p][:, :, :, :].rearrange("p a b c -> p (a b c)"), banks[6 + p][:, :],
                               ACT.Copy).then_inc(sem("m_done"), 1)

            def y0_copy(hp):
                p = hp % 2
                act.wait_ge(sem("ry_full"), hp + 1)
                act.activation(y0T[:, hp, :], banks[3 * p + 1][:, 0:T], ACT.Copy).then_inc(sem("y0_done"), 1)

            by_pairs([nat_copy, akv_copy, m_copy, y0_copy])
            for q in range(4):
                act.wait_ge(sem("centred"), q + 1)
                act.activation(slot_view(9, DC, T)[:, 2 * q:2 * q + 2, :], slot_view(8, DC, T)[:, 2 * q:2 * q + 2, :],
                               ACT.Square).then_inc(sem("y_squares"), 1)
                act.wait_ge(sem("y_var"), q + 1)
                act.activation(slot_view(10, DC, T)[:, 2 * q:2 * q + 2, :].rearrange("p a b -> p (a b)"), banks[7][:, :],
                               ACT.Sqrt, bias=eps[:, 1:2]).then_inc(sem("y_root"), 1)

        def rwkv_pool(pool, L):
            def expand(hp):
                p = hp % 2
                pool.wait_ge(sem("nat_done"), 2 * hp + 2)
                pool.wait_ge(sem("m_done"), hp + 1)
                if hp:
                    pool.wait_ge(sem("pq_full"), hp)
                mask = chunk_cols[:, :].unsqueeze(1).unsqueeze(3).to_broadcast([P, UNITS, 4, HALF])
                for dst, src in ((BX, Nat[p][:, 1]), (VX, Nat[p][:, 3]), (M2X, M12[p][:, 1])):
                    pool.tensor_tensor(dst.rearrange("p (u c d) -> p u c d", u=UNITS, c=4),
                                       src.unsqueeze(2).to_broadcast([P, UNITS, 4, HALF]), mask,
                                       ALU.mult).then_inc(sem("expanded"), 1)

            by_pairs([expand])

        def rwkv_dve(dve, L):
            step = Marks(sem("rwkv_step"))
            n = norm_index(L, 0)

            def then(ins):
                dve.wait_ge(step.sem, step.mark(ins))

            wait_h(dve, n)
            dve.tensor_tensor(dh[:, :, 1:T], hT[:, :, 0:T - 1], hT[:, :, 1:T], ALU.subtract).then_inc(step.sem, 1)
            step.n += 1
            then(dve.tensor_scalar(dh[:, :, 0:1], hT[:, :, 0:1], -1.0, None, ALU.mult))
            for i in range(6):
                if i >= 3:
                    wait_full(dve, (L, "rkv"[i - 3], 3))
                for c in range(DC):
                    dve.scalar_tensor_tensor(out=mixed[i % 3][:, c, :], in0=dh[:, c, :], scalar=col("rwkv_mu", i * DC + c),
                                             in1=hT[:, c, :], op0=ALU.mult, op1=ALU.add).then_inc(sem("mixed"), 1)
            dve.wait_ge(sem("mixed"), 6 * DC)
            dve.wait_ge(sem("rkv_ready"), 8)
            for c in range(DC):
                dve.tensor_scalar(kk[:, c, :], kraw[:, c, :], col("rwkv_k_k", c), None,
                                  ALU.mult).then_inc(sem("kk_raw"), 1)
            dve.wait_ge(sem("wa_ready"), 8)
            then(dve.tensor_scalar(sg[:, :, :], sg[:, :, :], -float(np.exp(-0.5)), None, ALU.mult))
            for c in range(DC):
                ins = dve.tensor_tensor_scan(csum[:, c, :], chunk_reset[:, :], sg[:, c, :], 0.0, ALU.mult, ALU.add)
                if c < DC - 1:
                    ins.then_inc(step.sem, 1)
                    step.n += 1
            ins.then_inc(sem("csum_done"), 1)
            dve.wait_ge(sem("csum_done"), 1)
            dve.wait_ge(sem("bank_full", plan.bank[(L, "lora1", 0)][0]), plan.bank[(L, "lora1", 0)][1])
            dve.tensor_tensor(e_prev[:, :, :], csum[:, :, :], sg[:, :, :], ALU.subtract).then_inc(sem("csum_done"), 1)
            dve.wait_ge(sem("wa_ready"), 16)
            dve.wait_ge(sem("csum_done"), 2)
            for c in range(DC):
                dve.tensor_scalar(sg[:, c, :], aT[:, c, :], -1.0, col("rwkv_k_a", c), ALU.add,
                                  ALU.mult).then_inc(step.sem, 1)
                step.n += 1
            dve.wait_ge(step.sem, step.n)
            then(dve.scalar_tensor_tensor(out=kraw[:, :, :].rearrange("p a b -> p (a b)"),
                                          in0=sg[:, :, :].rearrange("p a b -> p (a b)"), scalar=1.0,
                                          in1=kraw[:, :, :].rearrange("p a b -> p (a b)"), op0=ALU.add, op1=ALU.mult))
            for m in range(4):
                dve.wait_ge(sem("kk_root"), m + 1)
                pair = slice(2 * m, 2 * m + 2)
                then(dve.tensor_scalar(inv[:, pair, :], inv[:, pair, :], 1e-12, None, ALU.max))
                then(dve.reciprocal(inv[:, pair, :], inv[:, pair, :]))
                then(dve.tensor_tensor(kk[:, pair, :], kk[:, pair, :], inv[:, pair, :], ALU.mult))
            for c in range(DC):
                dve.scalar_tensor_tensor(out=rk[:, c, :], in0=rT[:, c, :], scalar=col("rwkv_r_k", c), in1=kraw[:, c, :],
                                         op0=ALU.mult, op1=ALU.mult).then_inc(sem("rk_done"), 1)
            then(dve.tensor_tensor(aT[:, :, :], kk[:, :, :], aT[:, :, :], ALU.mult))
            dve.wait_ge(sem("exps_done"), 3)
            dve.wait_ge(sem("rk_done"), DC)
            dve.scalar_tensor_tensor(out=big[:, :, 0, :], in0=kk[:, :, :], scalar=-1.0, in1=e_prev[:, :, :],
                                     op0=ALU.mult, op1=ALU.mult).then_inc(sem("factors_done"), 1)
            for dst, x, y in ((big[:, :, 1, :], aT, e_neg), (big[:, :, 2, :], kraw, e_neg), (rT[:, :, :], rT, e_in)):
                dve.tensor_tensor(dst, x[:, :, :], y[:, :, :], ALU.mult).then_inc(sem("factors_done"), 1)
            then(dve.tensor_copy(chunk_decay[:, :, :],
                                 e_in[:, :, :].rearrange("p h (c s) -> p h c s", s=CH)[:, :, :, CH - 1]))
            dve.wait_ge(sem("factors_done"), 1)
            for m in range(4):
                dve.wait_ge(sem("rk_sum"), m + 1)
                dve.tensor_tensor(bonus[:, 2 * m:2 * m + 2, :],
                                  banks[4 + m % 2][:, :].rearrange("p (a b) -> p a b", a=2),
                                  big[:, 2 * m:2 * m + 2, 3, :], ALU.mult).then_inc(sem("bonus_done"), 1)

            def mask_products(h):
                def run(hp):
                    p = hp % 2
                    dve.wait_ge(sem(f"a{h}_full"), hp + 1)
                    for i, (s, m, k) in enumerate(((0, 0, 2), (2, 2, 2), (4, 2, 1))):
                        dve.tensor_tensor(
                            MM[p][:, s:s + k].rearrange("p s (t h) n -> p s t h n", h=2)[:, :, :, h, :],
                            banks[3 * p + i][:, 0:k * 256].rearrange("p (s t n) -> p s t n", s=k, t=TT),
                            masks[:, m:m + k, :].unsqueeze(2).to_broadcast([P, k, TT, P]),
                            ALU.mult).then_inc(sem(f"a{h}_done"), 1)
                return run

            def four(x):
                return x.rearrange("p (u n) -> p u n", u=UNITS)

            def everywhere(m):
                return m.unsqueeze(1).to_broadcast([P, UNITS, P])

            def base(hp):
                p = hp % 2
                dve.wait_ge(sem("a1_done"), 3 * hp + 3)
                for dst, s, m in ((Tm[p], 0, 0), (TmT[p], 1, 1)):
                    then(dve.tensor_tensor(four(dst), MM[p][:, s], everywhere(pair_masks[:, m, :]), ALU.mult))
                then(dve.tensor_tensor(four(Tm[p]), four(Tm[p]), everywhere(ident[:, :]), ALU.add))
                dve.tensor_tensor(four(TmT[p]), four(TmT[p]), everywhere(ident[:, :]),
                                  ALU.add).then_inc(sem("base_done"), 1)

            def z_mask(l):
                def run(hp):
                    p = hp % 2
                    dve.wait_ge(sem("z_full"), level(l, hp))
                    dve.tensor_tensor(four(Zm[p]), four(banks[3 * p][:, :]), everywhere(pair_masks[:, 2 + l, :]),
                                      ALU.mult).then_inc(sem("z_done"), 1)
                return run

            def t_add(l):
                def run(hp):
                    p = hp % 2
                    dve.wait_ge(sem("t_full"), level(l, hp))
                    if l < NLEV - 1:
                        dve.tensor_tensor(Tm[p], Tm[p], banks[3 * p + 2][:, :], ALU.add).then_inc(step.sem, 1)
                        step.n += 1
                    dve.tensor_tensor(TmT[p], TmT[p], banks[3 * p + 1][:, :], ALU.add).then_inc(sem("tt_done"), 1)
                return run

            def r1(hp):
                p = hp % 2
                dve.wait_ge(sem("ry_full"), hp + 1)
                dve.tensor_tensor(rT[:, hp, :], rT[:, hp, :], banks[3 * p][:, 0:T], ALU.add).then_inc(sem("r1_done"), 1)

            def chunks(hp):
                p = hp % 2
                dve.wait_ge(sem("pq_full"), hp + 1)
                dve.tensor_tensor(PT_all[:, hp, 0], banks[3 * p + 2][:, :].rearrange("p (c j) -> p c j", j=HALF),
                                  head_eye[:, :].unsqueeze(1).to_broadcast([P, NCH, HALF]),
                                  ALU.add).then_inc(sem("pt_done"), 1)
                dve.tensor_tensor(PT_all[:, hp, 1], banks[6 + p][:, :].rearrange("p (c j) -> p c j", j=HALF),
                                  chunk_decay[:, hp, :].unsqueeze(2).to_broadcast([P, NCH, HALF]),
                                  ALU.mult).then_inc(sem("q_done"), 1)

            levels = [f(l) for l in range(NLEV) for f in (z_mask, t_add)]
            by_pairs([mask_products(0), mask_products(1), base, *levels, r1, chunks])
            dve.wait_ge(sem("q_done"), DC)
            for c in range(1, NCH - 1):
                for q in range(2):
                    dve.wait_ge(sem("state_full"), 2 * (c - 1) + q + 1)
                    for i in range(4):
                        hp = 4 * q + i
                        for h in range(2):
                            r = half_rows(h)
                            dve.scalar_tensor_tensor(out=PT_all[r, hp, 1, c, :],
                                                     in0=banks[2 * q + h][r, i * HALF:(i + 1) * HALF],
                                                     scalar=chunk_decay[r, hp, c:c + 1], in1=PT_all[r, hp, 1, c, :],
                                                     op0=ALU.mult, op1=ALU.add).then_inc(sem("state_done"), 1)
            yc, sq_, root = (slot_view(i, DC, T) for i in (8, 9, 10))
            for q in range(4):
                dve.wait_ge(sem("y_full"), q + 1)
                if q == 0:
                    dve.wait_ge(sem("y0_done"), DC)
                for h in range(2):
                    r = half_rows(h)
                    y = y0T[r, 2 * q:2 * q + 2, CH:T]
                    dve.tensor_tensor(y, y, banks[2 * (q % 3) + h][r, :].rearrange("p (a b) -> p a b", a=2)[:, :, CH:T],
                                      ALU.add).then_inc(sem("y_done"), 1)
            for q in range(4):
                pair = slice(2 * q, 2 * q + 2)
                dve.wait_ge(sem("y_mean"), q + 1)
                dve.tensor_tensor(yc[:, pair, :], y0T[:, pair, :], banks[6][:, :].rearrange("p (a b) -> p a b", a=2),
                                  ALU.subtract).then_inc(sem("centred"), 1)
                dve.wait_ge(sem("y_root"), q + 1)
                then(dve.reciprocal(root[:, pair, :], root[:, pair, :]))
                then(dve.tensor_tensor(yc[:, pair, :], yc[:, pair, :], root[:, pair, :], ALU.mult))
                for c in (2 * q, 2 * q + 1):
                    dve.tensor_scalar(yc[:, c, :], yc[:, c, :], col("rwkv_ln_g", c), col("rwkv_ln_b", c), ALU.mult,
                                      ALU.add).then_inc(step.sem, 1)
                    step.n += 1
                dve.wait_ge(step.sem, step.n)
                then(dve.tensor_tensor(yc[:, pair, :], yc[:, pair, :], bonus[:, pair, :], ALU.add))
                dve.tensor_tensor(y0T[:, pair, :], yc[:, pair, :], gT[:, pair, :], ALU.mult).then_inc(sem("gated"), 1)
            add_residual(dve, L, "o", updates(L))

        NCOL = S5_G * S5_N
        GW = S5_L * S5_C
        FB, GC = flat[:, 0:8192], flat[:, 8192:16384]
        tok = flat[0:S5_N, 16384:24576]
        h_tok = tok.rearrange("p (g s c) -> p g s c", g=S5_G, s=S5_L)
        y_tok = tok.rearrange("p (s d) -> p s d", s=S5_L)
        u_all = work[:, 12, :]
        c_rows = work[:, 12, :].rearrange("p (v b q) -> p v b q", v=2, b=DC)
        V_all = work[:, 13, :]
        coef = work[:, 13, :].rearrange("p (v k g) -> p v k g", v=4, k=S5_L)
        b_raw = work[:, 14, :].rearrange("p (v g c) -> p v g c", v=2, c=S5_C)
        c_raw = work[:, 15, :].rearrange("p (v g c) -> p v g c", v=2, c=S5_C)
        FT = [work[:, 14, i * 512:(i + 1) * 512] for i in (0, 1)]
        TZ = [work[:, 14, i * 512:(i + 1) * 512] for i in (2, 3)]
        decay8 = work[:, 15, :]
        cos_n, sin_n, turned, Z_all = (work[:, i, :] for i in (0, 1, 2, 3))
        a_rows = work[0:S5_G, 6, 0:256].rearrange("p (v q) -> p v q", v=2)
        as_rows = work[0:S5_G, 6, 256:512].rearrange("p (v q) -> p v q", v=2)
        step_col = work[0:S5_G, 6, 512:513]
        y_s5 = slot_view(0, DC, T)
        glu_gate = work[:, 4, :].rearrange("p (i t) -> p i t", t=T)
        glu_out = work[:, 5, 0:1024].rearrange("p (i t) -> p i t", t=T)

        def small(i, n=1):
            return work[:, 7, i * S5_G:(i + n) * S5_G]

        def table(i, n):
            return small(i, n).rearrange("p (k g) -> p k g", g=S5_G)

        A_RE, A_IM, AS_RE, TH = 0, 1, 2, 3
        TURNS, ANGLE, CO_ARG, DEN, B_RE, B_IM, TMP = 4, 5, 6, 7, 8, 9, 10
        U_RE, U_IM, GROW = 12, 20, 28

        def send_s5(sp, L):
            for i in range(8):
                send_plain(sp, (L, "glu", i), A["s5_w_glu"][0], (i % 2) * D + (i // 2) * TILE)

        def s5_pool(pool, L):
            if layers.index(L):
                pool.wait_ge(sem("x_ready"), updates(L) - 4)
            for v, (re, im) in enumerate((("re", "im"), ("im", "re"))):
                for half, part in enumerate((re, im)):
                    r = half_rows(half)
                    pool.dma_start(b_raw[r, v], A[f"s5_b_{part}"][0].rearrange("g p c -> p g c")).then_inc(sem("s5_in"), 16)
                    pool.dma_start(c_rows[:, v, :, half * HALF:(half + 1) * HALF],
                                   A[f"s5_c_{part}"][0].rearrange("(b g) c p -> (g c) b p", g=DC)).then_inc(sem("s5_in"), 16)
            for v, part in enumerate(("re", "im")):
                for half in range(2):
                    pool.dma_start(a_rows[:, v, half * HALF:(half + 1) * HALF], A[f"s5_a_{part}"][0]).then_inc(sem("s5_in"), 16)
            pool.dma_start(step_col, A["s5_log_step"].rearrange("a g -> g a")).then_inc(sem("s5_in"), 16)
            pool.wait_ge(sem("coef_done"), 2)
            pool.wait_ge(sem("c_ready"), 4)
            pool.wait_ge(sem("u_done"), 4)
            fill_factors(pool, L, GC, c_raw, 2, work[:, 9, :], "gc")

        def fill_factors(eng, L, dst, raw, v, tmp, name):
            G4 = S5_G // 4
            chain = Marks(sem(name + "_step"))

            def spread(x):
                return x.unsqueeze(2).to_broadcast([P, G4, S5_L, S5_C])

            def along(x):
                return x.rearrange("p k g -> p g k").unsqueeze(3).to_broadcast([P, G4, S5_L, S5_C])

            for q in range(4):
                g = slice(q * G4, (q + 1) * G4)
                out_ = dst[:, q * 2048:(q + 1) * 2048].rearrange("p (g k c) -> p g k c", g=G4, k=S5_L)
                t = tmp.rearrange("p (g k c) -> p g k c", g=G4, k=S5_L)
                chain.mark(eng.tensor_tensor(out_, spread(raw[:, 0, g]), along(coef[:, v, :, g]), ALU.mult))
                if q:
                    eng.wait_ge(sem(name + "_done"), q)
                chain.mark(eng.tensor_tensor(t, spread(raw[:, 1, g]), along(coef[:, v + 1, :, g]), ALU.mult))
                eng.wait_ge(chain.sem, chain.n)
                eng.tensor_tensor(out_, out_, t, ALU.subtract).then_inc(sem(name + "_done"), 1)

        def s5_act(act, L):
            act.wait_ge(sem("s5_in"), 16 * 13)
            act.activation(step_col, step_col, ACT.Exp).then_inc(sem("step_exp"), 1)
            for i in range(4):
                act.wait_ge(sem("c_full"), i + 1)
                v, b = divmod(i, 2)
                dst = c_raw[:, v, b * 32:(b + 1) * 32, :].rearrange("p g c -> p (g c)")
                act.activation(dst, banks[i][:, :], ACT.Copy,
                               scale=sign[:, 0:1] if v == 0 else 1.0).then_inc(sem("c_ready"), 1)
            for i in range(16):
                act.wait_ge(sem("h_full"), i + 1)
                act.activation(h_tok[:, 32 * (i % 2):32 * (i % 2) + 32, i // 2, :],
                               banks[i % 4][0:S5_N, :].rearrange("p (g c) -> p g c", c=S5_C), ACT.Copy).then_inc(sem("htok_done"), 1)
            for i in range(4):
                act.wait_ge(sem("u_full"), i + 1)
                act.activation(u_all[:, i * 512:(i + 1) * 512], banks[i][:, :], ACT.Copy).then_inc(sem("u_done"), 1)
            act.wait_ge(sem("as_ready"), 1)
            for k in range(S5_L):
                for v, s in ((0, -1.0), (1, 1.0)):
                    act.activation(coef[:, 2 * v, k, :], small(AS_RE), ACT.Exp,
                                   scale=s * (k + 1)).then_inc(sem("mag_done"), 1)
            act.wait_ge(sem("angle_done"), 1)
            act.activation(small(CO_ARG), small(ANGLE), ACT.Abs).then_inc(sem("abs_done"), 1)
            act.activation(small(U_IM), small(ANGLE), ACT.Sin).then_inc(sem("sin_done"), 1)
            act.wait_ge(sem("abs_done"), 1)
            act.activation(small(U_RE), small(CO_ARG), ACT.Sin, bias=half_pi[:, 0:1],
                           scale=-1.0).then_inc(sem("sin_done"), 1)
            for i in range(16):
                act.wait_ge(sem("ft_full"), i + 1)
                if i >= 2:
                    act.wait_ge(sem("vy_full"), i - 1)
                act.activation(FT[i % 2], banks[i % 2][:, :], ACT.Copy).then_inc(sem("ft_done"), 1)
                if i:
                    pass_one_copies(act, L, i - 1)
            pass_one_copies(act, L, 15)
            for m in range(4):
                act.wait_ge(sem("ys5_done"), 2 * m + 2)
                pair = y_s5[:, 2 * m:2 * m + 2, :]
                act.activation(pair, pair, ACT.Gelu_apprx_tanh).then_inc(sem("gelu_done"), 1)
            for m in range(4):
                wait_full(act, (L, "glu", 2 * m + 1))
                for b in range(2):
                    c = 2 * m + b
                    act.activation(glu_gate[:, c, :], bank_of((L, "glu", 2 * m + 1))[:, b * T:(b + 1) * T], ACT.Sigmoid,
                                   bias=col("s5_b_glu", DC + c)).then_inc(sem("glu_gate"), 1)

        def pass_one_copies(act, L, i):
            act.wait_ge(sem("vy_full"), i + 1)
            act.activation(V_all[:, i * P:(i + 1) * P], banks[4 + i % 2][:, 0:P], ACT.Copy).then_inc(sem("v_done"), 1)
            act.activation(y_tok.rearrange("p s (g c) -> p g s c", c=S5_C)[:, 4 * i:4 * i + 4],
                           banks[6 + i % 2][0:S5_N, :].rearrange("p (g s c) -> p g s c", g=4, s=S5_L),
                           ACT.Copy).then_inc(sem("v_done"), 1)

        def s5_pe(pe, L):
            pe.wait_ge(sem("s5_in"), 16 * 13)
            for i in range(4):
                v, b = divmod(i, 2)
                for j in range(4):
                    mm = pe.transpose(banks[i][:, j * P:(j + 1) * P], c_rows[:, v, 4 * b + j, :], ident[:, :])
                mm.then_inc(sem("c_full"), 1)
            pe.wait_ge(sem("a_scaled"), 2)
            for i, src in enumerate((a_rows[:, 0], a_rows[:, 1], as_rows[:, 0], as_rows[:, 1])):
                mm = pe.transpose(banks[4][:, i * S5_G:(i + 1) * S5_G], src, ident[0:S5_G, 0:S5_G])
            mm.then_inc(sem("as_full"), 1)
            wait_h(pe, norm_index(L, 0))
            for i in range(16):
                pe.wait_ge(*((sem("c_ready"), i + 1) if i < 4 else (sem("htok_done"), i - 3)))
                for j in range(4):
                    x = hT[:, 4 * (i % 2) + j, :].rearrange("p (n s) -> p s n", s=S5_L)[:, i // 2, :]
                    mm = pe.transpose(banks[i % 4][0:S5_N, j * P:(j + 1) * P], x, ident[:, :])
                mm.then_inc(sem("h_full"), 1)
            for i in range(4):
                pe.wait_ge(sem("htok_done"), 16)
                for j in range(16):
                    g = 16 * i + j
                    x = h_tok[:, g].rearrange("p s c -> p (s c)")
                    mm = pe.transpose(banks[i][:, j * S5_N:(j + 1) * S5_N], x, ident[0:S5_N, 0:S5_N])
                mm.then_inc(sem("u_full"), 1)

            def tables(i):
                if i == 0:
                    pe.wait_ge(sem("fb_done"), 4)
                    pe.wait_ge(sem("gc_done"), 4)
                if i < 2:
                    pe.wait_ge(sem("u_done"), 4)
                else:
                    pe.wait_ge(sem("ft_done"), i - 1)
                    pe.wait_ge(sem("toeplitz"), i - 1)
                for j in range(4):
                    g = slice((4 * i + j) * GW, (4 * i + j + 1) * GW)
                    pe.transpose(banks[i % 2][:, j * P:(j + 1) * P], FB[:, g], ident[:, :])
                    mm = pe.matmul(banks[2 + i % 2][:, j * P:(j + 1) * P], FB[:, g], GC[:, g], start=True, stop=True)
                mm.then_inc(sem("ft_full"), 1)

            def apply(i):
                pe.wait_ge(sem("ft_done"), i + 1)
                pe.wait_ge(sem("toeplitz"), i + 1)
                if i >= 2:
                    pe.wait_ge(sem("v_done"), 2 * (i - 1))
                for j in range(4):
                    u = u_all[:, (4 * i + j) * S5_N:(4 * i + j + 1) * S5_N]
                    c = slice(j * P, (j + 1) * P)
                    pe.matmul(banks[4 + i % 2][:, j * S5_N:(j + 1) * S5_N], FT[i % 2][:, c], u, start=True, stop=True)
                    mm = pe.matmul(banks[6 + i % 2][0:S5_N, c], u, TZ[i % 2][:, c], start=True, stop=True)
                mm.then_inc(sem("vy_full"), 1)

            tables(0)
            for i in range(16):
                if i < 15:
                    tables(i + 1)
                apply(i)
            pe.wait_ge(sem("v_done"), 32)
            for i in range(4):
                pe.matmul(banks[i][:, :], swap[:, :], V_all[:, i * 512:(i + 1) * 512], start=True,
                          stop=True).then_inc(sem("vs_full"), 1)
            pe.wait_ge(sem("z_ready"), 1)
            for i in range(4):
                pe.matmul(banks[4 + i][:, :], swap[:, :], Z_all[:, i * 512:(i + 1) * 512], start=True,
                          stop=True).then_inc(sem("zs_full"), 1)
            for i in range(16):
                pe.wait_ge(sem("x_state"), i // 4 + 1)
                if i >= 4:
                    pe.wait_ge(sem("y_added"), i - 3)
                for j in range(4):
                    g = 4 * i + j
                    mm = pe.matmul(banks[i % 4][0:S5_N, j * P:(j + 1) * P], V_all[:, g * S5_N:(g + 1) * S5_N],
                                   GC[:, g * GW:(g + 1) * GW], start=True, stop=True)
                mm.then_inc(sem("yx_full"), 1)
            pe.wait_ge(sem("y_added"), 16)
            for m in range(4):
                for b in range(2):
                    for s in range(S5_L):
                        at = b * T + s * S5_N
                        mm = pe.transpose(banks[4 + m][:, at:at + S5_N],
                                          y_tok[:, s, (2 * m + b) * P:(2 * m + b + 1) * P], ident[0:S5_N, 0:S5_N])
                mm.then_inc(sem("yt_full"), 1)
            pe.wait_ge(sem("ys5_done"), 8)
            for i in range(8):
                project(pe, (L, "glu", i), y_s5, (lambda c: pe.wait_ge(sem("gelu_done"), c // 2 + 1)) if i == 0 else None)

        def s5_dve(dve, L):
            step = Marks(sem("s5_step"))

            def then(ins):
                dve.wait_ge(step.sem, step.mark(ins))

            def tt(out_, x, y, op):
                then(dve.tensor_tensor(out_, x, y, op))

            def ts(out_, x, a, b, op0, op1):
                then(dve.tensor_scalar(out_, x, a, b, op0, op1))

            def complex_product(re, im, a, b, t):
                tt(t, a[1], b[1], ALU.mult)
                tt(re, a[0], b[0], ALU.mult)
                tt(re, re, t, ALU.subtract)
                tt(t, a[1], b[0], ALU.mult)
                tt(im, a[0], b[1], ALU.mult)
                tt(im, im, t, ALU.add)

            dve.wait_ge(sem("s5_in"), 16 * 13)
            ts(b_raw[:, 1], b_raw[:, 1], sign[:, 0:1], None, ALU.mult, ALU.bypass)
            dve.wait_ge(sem("step_exp"), 1)
            for v in range(2):
                dve.tensor_scalar(as_rows[:, v], a_rows[:, v], step_col, None, ALU.mult).then_inc(sem("a_scaled"), 1)
            dve.wait_ge(sem("as_full"), 1)
            dve.tensor_copy(small(0, 4), banks[4][:, 0:4 * S5_G]).then_inc(sem("as_ready"), 1)
            dve.wait_ge(sem("as_ready"), 1)
            big_ = 1.5 * 2.0 ** 23
            ts(small(TURNS), small(TH), 1.0 / TWO_PI, big_, ALU.mult, ALU.add)
            ts(small(TURNS), small(TURNS), -big_, None, ALU.add, ALU.bypass)
            turn_hi = 6.28125
            then(dve.scalar_tensor_tensor(out=small(ANGLE), in0=small(TURNS), scalar=-turn_hi, in1=small(TH),
                                          op0=ALU.mult, op1=ALU.add))
            then(dve.scalar_tensor_tensor(out=small(ANGLE), in0=small(TURNS), scalar=-(TWO_PI - turn_hi),
                                          in1=small(ANGLE), op0=ALU.mult, op1=ALU.add))
            dve.tensor_scalar(small(ANGLE), small(ANGLE), 3.1415925, -3.1415925, ALU.min,
                              ALU.max).then_inc(sem("angle_done"), 1)
            tt(small(DEN), small(A_RE), small(A_RE), ALU.mult)
            tt(small(TMP), small(A_IM), small(A_IM), ALU.mult)
            tt(small(DEN), small(DEN), small(TMP), ALU.add)
            then(dve.reciprocal(small(DEN), small(DEN)))
            dve.wait_ge(sem("sin_done"), 2)
            have = 1
            while have < S5_L:
                last = [table(x + have - 1, 1).to_broadcast([P, have, S5_G]) for x in (U_RE, U_IM)]
                complex_product(table(U_RE + have, have), table(U_IM + have, have),
                                (table(U_RE, have), table(U_IM, have)), last, table(GROW, have))
                have *= 2
            dve.wait_ge(sem("mag_done"), 16)
            tt(small(B_RE), coef[:, 2, 0, :], small(U_RE), ALU.mult)
            ts(small(B_RE), small(B_RE), -1.0, None, ALU.add, ALU.bypass)
            tt(small(B_IM), coef[:, 2, 0, :], small(U_IM), ALU.mult)
            tt(small(TURNS), small(B_RE), small(A_RE), ALU.mult)
            tt(small(TMP), small(B_IM), small(A_IM), ALU.mult)
            tt(small(TURNS), small(TURNS), small(TMP), ALU.add)
            tt(small(B_IM), small(B_IM), small(A_RE), ALU.mult)
            tt(small(TMP), small(B_RE), small(A_IM), ALU.mult)
            tt(small(B_IM), small(B_IM), small(TMP), ALU.subtract)
            tt(small(B_RE), small(TURNS), small(DEN), ALU.mult)
            tt(small(B_IM), small(B_IM), small(DEN), ALU.mult)
            then(dve.tensor_copy(lam8[:, 0, :], coef[:, 2, S5_L - 1, :]))
            then(dve.tensor_copy(lam8[:, 1, :], small(U_RE + S5_L - 1)))
            then(dve.tensor_copy(lam8[:, 2, :], small(U_IM + S5_L - 1)))
            tt(coef[:, 3], coef[:, 2], table(U_IM, S5_L), ALU.mult)
            tt(coef[:, 2], coef[:, 2], table(U_RE, S5_L), ALU.mult)
            bre, bim = (table(x, 1).to_broadcast([P, S5_L, S5_G]) for x in (B_RE, B_IM))
            tt(coef[:, 1], table(U_RE, S5_L), bim, ALU.mult)
            half4 = S5_L // 2
            for k in (0, half4):
                ks = slice(k, k + half4)
                b4 = [table(x, 1).to_broadcast([P, half4, S5_G]) for x in (B_RE, B_IM)]
                t = table(GROW, half4)
                tt(t, table(U_IM + k, half4), b4[0], ALU.mult)
                tt(coef[:, 1, ks], coef[:, 1, ks], t, ALU.subtract)
                tt(t, table(U_IM + k, half4), b4[1], ALU.mult)
                tt(table(U_RE + k, half4), table(U_RE + k, half4), b4[0], ALU.mult)
                tt(table(U_RE + k, half4), table(U_RE + k, half4), t, ALU.add)
            dve.tensor_tensor(coef[:, 1], coef[:, 1], coef[:, 0], ALU.mult).then_inc(sem("coef_done"), 1)
            dve.wait_ge(sem("coef_done"), 1)
            dve.tensor_tensor(coef[:, 0], coef[:, 0], table(U_RE, S5_L), ALU.mult).then_inc(sem("coef_done"), 1)
            dve.wait_ge(sem("coef_done"), 2)
            dve.wait_ge(sem("u_done"), 4)
            fill_factors(dve, L, FB, b_raw, 0, work[:, 8, :], "fb")
            for i in range(16):
                dve.wait_ge(sem("ft_full"), i + 1)
                if i >= 2:
                    dve.wait_ge(sem("vy_full"), i - 1)
                dve.tensor_tensor(TZ[i % 2].rearrange("p (g n) -> p g n", g=4),
                                  banks[2 + i % 2][:, :].rearrange("p (g n) -> p g n", g=4),
                                  causal[:, :].unsqueeze(1).to_broadcast([P, 4, P]),
                                  ALU.mult).then_inc(sem("toeplitz"), 1)
            grid = [x.rearrange("p (g n) -> p g n", n=S5_N) for x in (cos_n, sin_n, turned)]
            dve.wait_ge(sem("vy_full"), 16)
            then(dve.memset(cos_n, 1.0))
            then(dve.memset(sin_n, 0.0))
            have = 1
            while have < S5_N:
                n = slice(have, 2 * have)
                factor = [x.unsqueeze(2).to_broadcast([P, S5_G, have]) for x in (lam8[:, 1, :], lam8[:, 2, :])]
                complex_product(grid[0][:, :, n], grid[1][:, :, n],
                                [x[:, :, 0:have] for x in grid[0:2]], factor, grid[2][:, :, 0:have])
                if 2 * have < S5_N:
                    t = [turned[:, i * S5_G:(i + 1) * S5_G] for i in range(3)]
                    complex_product(t[0], t[1], (lam8[:, 1, :], lam8[:, 2, :]), (lam8[:, 1, :], lam8[:, 2, :]), t[2])
                    then(dve.tensor_copy(lam8[:, 1, :], t[0]))
                    then(dve.tensor_copy(lam8[:, 2, :], t[1]))
                have *= 2
            d8 = decay8.rearrange("p (g n) -> p g n", n=S5_N)
            then(dve.tensor_copy(d8, lam8[:, 0, :].unsqueeze(2).to_broadcast([P, S5_G, S5_N])))
            then(dve.memset(d8[:, :, S5_N - 1:S5_N], 0.0))
            dve.wait_ge(sem("v_done"), 32)
            dve.wait_ge(sem("vs_full"), 4)
            for i in range(4):
                c = slice(i * 512, (i + 1) * 512)
                tt(turned[:, c], sin_n[:, c], banks[i][:, :], ALU.mult)
            tt(V_all, V_all, cos_n, ALU.mult)
            tt(V_all, V_all, turned, ALU.add)
            then(dve.memset(Z_all[:, 0:1], 0.0))
            dve.tensor_tensor_scan(Z_all[:, 1:NCOL], V_all[:, 0:NCOL - 1], decay8[:, 0:NCOL - 1], 0.0, ALU.add,
                                   ALU.mult).then_inc(sem("z_ready"), 1)
            dve.wait_ge(sem("z_ready"), 1)
            for i in range(4):
                c = slice(i * 512, (i + 1) * 512)
                dve.wait_ge(sem("zs_full"), i + 1)
                tt(turned[:, c], sin_n[:, c], banks[4 + i][:, :], ALU.mult)
                tt(V_all[:, c], Z_all[:, c], cos_n[:, c], ALU.mult)
                dve.tensor_tensor(V_all[:, c], V_all[:, c], turned[:, c], ALU.subtract).then_inc(sem("x_state"), 1)
            for i in range(16):
                dve.wait_ge(sem("yx_full"), i + 1)
                y = y_tok.rearrange("p s (g c) -> p g s c", c=S5_C)[:, 4 * i:4 * i + 4]
                dve.tensor_tensor(y, y, banks[i % 4][0:S5_N, :].rearrange("p (g s c) -> p g s c", g=4, s=S5_L),
                                  ALU.add).then_inc(sem("y_added"), 1)
            for m in range(4):
                dve.wait_ge(sem("yt_full"), m + 1)
                for b in range(2):
                    c = 2 * m + b
                    dve.scalar_tensor_tensor(
                        out=y_s5[:, c, :].rearrange("p (n s) -> p n s", s=S5_L),
                        in0=hT[:, c, :].rearrange("p (n s) -> p n s", s=S5_L), scalar=col("s5_d", c),
                        in1=banks[4 + m][:, b * T:(b + 1) * T].rearrange("p (s n) -> p n s", s=S5_L),
                        op0=ALU.mult, op1=ALU.add).then_inc(sem("ys5_done"), 1)
            for m in range(4):
                wait_full(dve, (L, "glu", 2 * m))
                dve.wait_ge(sem("glu_gate"), 2 * m + 2)
                for b in range(2):
                    c = 2 * m + b
                    ins = dve.scalar_tensor_tensor(out=glu_out[:, 2 * (m % 2) + b, :],
                                                   in0=bank_of((L, "glu", 2 * m))[:, b * T:(b + 1) * T],
                                                   scalar=col("s5_b_glu", c), in1=glu_gate[:, c, :],
                                                   op0=ALU.add, op1=ALU.mult)
                    if b == 0:
                        step.mark(ins)
                ins.then_inc(sem("glu_ready"), 1)
                dve.wait_ge(sem("glu_ready"), m + 1)
                pair = xT[:, 2 * m:2 * m + 2, :]
                dve.tensor_tensor(pair, pair, glu_out[:, 2 * (m % 2):2 * (m % 2) + 2, :],
                                  ALU.add).then_inc(sem("x_ready"), 1)
                dve.wait_ge(sem("x_ready"), updates(L) + m + 1)

        x_tok = slot_view(0, TT, D)
        par_rows = slot_view(1, PAR_BLOCKS, P)

        def load_sp(sp):
            for b in range(TT):
                sp.dma_start(x_tok[:, b, :], A["x"][0, b * P:(b + 1) * P, :]).then_inc(sem("x_in"), 16)

        def load_params(q):
            count = 0
            for name, (first, n) in PAR.items():
                a = A[name]
                if name.startswith("dsa"):
                    for r in range(n):
                        row = first + r
                        for half in range(2):
                            q.dma_start(par_rows[row % P:row % P + 1, row // P, half * HALF:(half + 1) * HALF],
                                        a[r:r + 1, :]).then_inc(sem("par_in"), 16)
                            count += 1
                    continue
                letters = "abcd"[:len(a.shape)]
                flat = a.rearrange(f"{' '.join(letters)} -> ({' '.join(letters)})").rearrange("(r c) -> r c", c=P)
                r = 0
                while r < n:
                    row = first + r
                    m = min(n - r, P - row % P)
                    q.dma_start(par_rows[row % P:row % P + m, row // P, :], flat[r:r + m, :]).then_inc(sem("par_in"), 16)
                    count += 1
                    r += m
            return count

        par_dmas = sum(2 * n if name.startswith("dsa") else (first + n - 1) // P - first // P + 1
                       for name, (first, n) in PAR.items())

        def constants(pool):
            step = Marks(sem("constant_step"))

            def then(ins):
                pool.wait_ge(step.sem, step.mark(ins))

            pool.memset(ident[:, :], 0.0).then_inc(step.sem, 1)
            step.n += 1
            pool.memset(mean_all[:, :], 1.0 / D).then_inc(step.sem, 1)
            step.n += 1
            pool.memset(eps[:, 0:1], EPS).then_inc(step.sem, 1)
            step.n += 1
            pool.memset(eps[:, 1:2], GN_EPS).then_inc(step.sem, 1)
            step.n += 1
            then(pool.memset(par_rows[:, PAR_BLOCKS - 1, :], 0.0))
            for x, value in ((mean_head, 1.0 / HALF), (sum_head, 1.0)):
                then(pool.memset(x[:, :], 0.0))
                then(pool.memset(x[0:HALF, 0:HALF], value))
                then(pool.memset(x[HALF:P, HALF:P], value))
            pool.affine_select(out=ident[:, :], in_=ident[:, :], compare_op=ALU.not_equal, fill=1.0, base=0,
                               pattern=[[-1, P]], channel_multiplier=1).then_inc(sem("constants"), 1)

        def chunk_constants(pool):
            step = Marks(sem("chunk_constant_step"))

            def then(ins):
                pool.wait_ge(step.sem, step.mark(ins))

            def select(x, pattern, base, slope, op=ALU.is_ge):
                then(pool.affine_select(out=x, in_=x, compare_op=op, fill=0.0, base=base, pattern=pattern,
                                        channel_multiplier=slope))

            then(pool.memset(masks[:, :, :], 0.0))
            for r in range(0, P, CH):
                then(pool.memset(masks[r:r + CH, :, r:r + CH], 1.0))
            select(masks[:, 0, :], [[-1, P]], -1, 1)
            for i, base in ((1, -1), (2, 0), (3, -1)):
                select(masks[:, i, :], [[1, P]], base, -1)
            then(pool.memset(pair_masks[:, :, :], 0.0))
            for i, n in ((0, 1), (2, 2), (3, 4), (4, 8), (5, 16)):
                v = pair_masks[:, i, :].rearrange("p (b h c) -> p b h c", h=2, c=n)[:, :, 0, :]
                nb = P // (2 * n)
                then(pool.memset(v, 1.0))
                select(v, [[-2 * n, nb], [0, n]], -n, 1)
                select(v, [[2 * n, nb], [0, n]], 2 * n - 1, -1)
            v = pair_masks[:, 1, :].rearrange("p (b h) -> p b h", h=2)[:, :, 1]
            then(pool.memset(v, 1.0))
            select(v, [[-2, P // 2]], 0, 1)
            select(v, [[2, P // 2]], 0, -1)
            then(pool.memset(chunk_cols[:, :], 0.0))
            for i in range(P // CH):
                then(pool.memset(chunk_cols[i * CH:(i + 1) * CH, i:i + 1], 1.0))
            then(pool.memset(chunk_reset[:, :], 1.0))
            then(pool.memset(chunk_reset[:, :].rearrange("p (c s) -> p c s", s=CH)[:, :, 0:1], 0.0))
            then(pool.tensor_copy(head_eye[0:HALF, :], ident[0:HALF, 0:HALF]))
            then(pool.memset(causal[:, :], 1.0))
            select(causal[:, :].rearrange("p (t c) -> p t c", c=S5_C), [[S5_C, S5_L], [0, S5_C]], S5_C - 1, -1)
            then(pool.memset(swap[:, :], 0.0))
            then(pool.tensor_copy(swap[:, 0:HALF], ident[:, HALF:P]))
            then(pool.tensor_scalar(swap[:, HALF:P], ident[:, 0:HALF], -1.0, None, ALU.mult))
            then(pool.memset(sign[0:HALF, :], 1.0))
            then(pool.memset(sign[HALF:P, :], -1.0))
            then(pool.memset(half_pi[:, :], TWO_PI / 4))
            pool.tensor_copy(head_eye[HALF:P, :], ident[HALF:P, HALF:P]).then_inc(sem("chunk_constants"), 1)

        def load_pe(pe):
            pe.wait_ge(sem("constants"), 1)
            pe.wait_ge(sem("x_in"), 32)
            for c in range(DC):
                for b in range(TT):
                    mm = pe.transpose(banks[c // 2][:, (c % 2) * T + b * P:(c % 2) * T + (b + 1) * P],
                                      x_tok[:, b, c * P:(c + 1) * P], ident[:, :])
                if c % 2:
                    mm.then_inc(sem("xt_full"), 1)
            pe.wait_ge(sem("par_in"), 16 * par_dmas)
            for i in range(PAR_BLOCKS):
                mm = pe.transpose(banks[4 + i // 4][:, (i % 4) * P:(i % 4 + 1) * P], par_rows[:, i, :], ident[:, :])
                if i % 4 == 3:
                    mm.then_inc(sem("par_full"), 1)
            pe.wait_ge(sem("par_ready"), 2)

        def load_dve(dve):
            for m in range(4):
                dve.wait_ge(sem("xt_full"), m + 1)
                dve.tensor_copy(xT[:, 2 * m:2 * m + 2, :].rearrange("p a b -> p (a b)"),
                                banks[m][:, :]).then_inc(sem("x_ready"), 1)
            for i in range(2):
                dve.wait_ge(sem("par_full"), i + 1)
                dve.tensor_copy(par[:, i * 512:(i + 1) * 512], banks[4 + i][:, :]).then_inc(sem("par_ready"), 1)

        out_tok = slot_view(0, TT, D)
        total_updates = 4 * (1 + 2 * len(layers))

        def store_pe(pe):
            for m in range(4):
                pe.wait_ge(sem("x_ready"), total_updates - 4 + m + 1)
                for b in range(TT):
                    for c in range(2):
                        mm = pe.transpose(banks[m][:, (b * 2 + c) * P:(b * 2 + c + 1) * P],
                                          xT[:, 2 * m + c, b * P:(b + 1) * P], ident[:, :])
                mm.then_inc(sem("out_full"), 1)

        def store_act(act):
            for m in range(4):
                act.wait_ge(sem("out_full"), m + 1)
                act.activation(out_tok[:, :, 2 * m * P:(2 * m + 2) * P],
                               banks[m][:, :].rearrange("p (b n) -> p b n", b=TT), ACT.Copy).then_inc(sem("out_ready"), 1)

        def store_sp(sp):
            for m in range(4):
                sp.wait_ge(sem("out_ready"), m + 1)
                c = slice(2 * m * P, (2 * m + 2) * P)
                sp.dma_start(out[0].rearrange("(b p) d -> p b d", p=P)[:, :, c], out_tok[:, :, c]).then_inc(sem("stored"), 16)
            sp.wait_ge(sem("stored"), 64)

        block = ctx.enter_context(nc.Block())

        @block.sync
        def _(sp):
            load_sp(sp)
            for L in layers:
                [send_dsa, send_rwkv, send_s5][L % 3](sp, L)
                send_mlp(sp, L)
            store_sp(sp)

        @block.gpsimd
        def _(pool):
            constants(pool)
            pool.wait_ge(sem("constants"), 1)
            load_params(pool)
            chunk_constants(pool)
            for L in layers:
                if L % 3:
                    [None, rwkv_pool, s5_pool][L % 3](pool, L)

        @block.scalar
        def _(act):
            for L in layers:
                norm_squares(act, norm_index(L, 0))
                norm_root(act, norm_index(L, 0))
                [dsa_act, rwkv_act, s5_act][L % 3](act, L)
                norm_squares(act, norm_index(L, 1))
                norm_root(act, norm_index(L, 1))
                mlp_act(act, L)
            store_act(act)

        @block.tensor
        def _(pe):
            load_pe(pe)
            for L in layers:
                norm_mean(pe, norm_index(L, 0))
                [dsa_pe, rwkv_pe, s5_pe][L % 3](pe, L)
                norm_mean(pe, norm_index(L, 1))
                mlp_pe(pe, L)
            store_pe(pe)

        @block.vector
        def _(dve):
            load_dve(dve)
            dve.wait_ge(sem("chunk_constants"), 1)
            for L in layers:
                norm_scale(dve, norm_index(L, 0), "norm_mix", L)
                [dsa_dve, rwkv_dve, s5_dve][L % 3](dve, L)
                norm_scale(dve, norm_index(L, 1), "norm_ffn", L)
                mlp_dve(dve, L)


def kernel(**inputs):
    import numpy as _np
    import concourse.bacc as _bacc
    from concourse import mybir as _mybir
    from concourse.bass_utils import run_bass_kernel_spmd as _run

    nc = _bacc.Bacc("TRN2", target_bir_lowering=False, num_devices=1)
    arrays, args = {}, {}
    for name, a in inputs.items():
        a = _np.ascontiguousarray(a)
        arrays[f"in_{name}_dram"] = a
        args[name] = nc.dram_tensor(f"in_{name}_dram", a.shape, _mybir.dt.from_np(a.dtype), kind="ExternalInput").ap()
    out = nc.dram_tensor("out_0_dram", (1, T, D), F32, kind="ExternalOutput").ap()
    trunk(nc, args, out)
    r = _run(nc, [arrays], core_ids=[0])
    return r.results[0]["out_0_dram"]
```

```python
from contextlib import ExitStack

import numpy as np

import concourse.bass as bass
from concourse import mybir

ALU = mybir.AluOpType
ACT = mybir.ActivationFunctionType
AX_X = mybir.AxisListType.X
F32 = mybir.dt.float32
F32R = mybir.dt.float32r

P = 128
D = 1024
T = 256
DEPTH = 4
DC = D // P
TT = T // P
HALF = 64
EPS = 1e-6
GN_EPS = 64e-5

DSA_HEADS = 16
IDX_HEADS = 8
TOPK = T // 4
Q_BLOCK = 64
F = 2816
FC = F // P
MASKED = -1e30
TAKEN = -3e38

TILE = 256
SLOT = DC * TILE
NSLOT = 3
NSPLIT = 2
ROUND = 6
NBANK = 6

CH = 32
NCH = T // CH
UNITS = 4

S5_L = 8
S5_N = T // S5_L
S5_G = 64
S5_C = 16
TWO_PI = 6.283185307179586

PAR = {}
_n = 0
for _name, _rows in (("ffn_conv_w", DEPTH * 3 * 2 * FC), ("ffn_conv_b", DEPTH * 2 * FC),
                     ("norm_mix", DEPTH * DC), ("norm_ffn", DEPTH * DC), ("rwkv_mu", 6 * DC),
                     ("rwkv_w0", DC), ("rwkv_a0", DC), ("rwkv_k_k", DC), ("rwkv_k_a", DC),
                     ("rwkv_ln_g", DC), ("rwkv_ln_b", DC), ("rwkv_r_k", DC), ("s5_d", DC),
                     ("s5_b_glu", 2 * DC), ("dsa_q_norm", 2), ("dsa_k_norm", 2), ("dsa_kidx_norm", 2)):
    PAR[_name] = (_n, _rows)
    _n += _rows
PAR_ROWS = _n
PAR_BLOCKS = -(-PAR_ROWS // P)


class Marks:

    def __init__(self, sem):
        self.sem, self.n = sem, 0

    def mark(self, ins):
        ins.then_inc(self.sem, 1)
        self.n = self.n + 1
        return self.n


class Plan:

    def __init__(self):
        self.tiles = []
        self.tile = {}
        self.used = {}
        self.split = {}
        self.split_tiles = []
        self.slot_dmas = [0] * NSLOT
        self.fills = [0] * NBANK
        self.bank = {}

    def weights(self, key, dmas=1, split=False):
        if split:
            self.split[key] = len(self.split_tiles)
            self.split_tiles.append(key)
        n = len(self.tiles)
        slot = n % NSLOT
        self.slot_dmas[slot] += 16 * dmas
        self.tiles.append(key)
        self.tile[key] = (n, slot, self.slot_dmas[slot])

    def fill(self, key, bank):
        self.fills[bank] += 1
        self.bank[key] = (bank, self.fills[bank])


def make_plan(layers):
    plan = Plan()

    def simple(keys, dmas=1, split=False):
        for i, key in enumerate(keys):
            plan.weights(key, dmas, split)
            plan.fill(key, plan.next % NBANK)
            plan.next += 1
            plan.used[key] = ("bank_full", plan.bank[key])

    plan.next = 0
    for L in layers:
        kind = L % 3
        plan.next = 0
        if kind == 0:
            simple([(L, s, i) for s in "qkv" for i in range(4)], split=True)
            simple([(L, "i", i) for i in range(2)], split=True)
            simple([(L, "s", 0)], 3)
            simple([(L, "o", i) for i in range(4)], split=True)
        elif kind == 1:
            simple([(L, "lora1", 0)], 3)
            plan.weights((L, "lora2", 0), 3)
            for s in "wag":
                for i in range(4):
                    plan.fill((L, s, i), plan.next % NBANK)
                    plan.next += 1
            plan.used[(L, "lora2", 0)] = ("bank_full", plan.bank[(L, "g", 3)])
            simple([(L, s, i) for s in "krv" for i in range(4)])
            simple([(L, "o", i) for i in range(4)], split=True)
        else:
            simple([(L, "glu", i) for i in range(8)], split=True)
        plan.next = 0
        simple([(L, "up", i) for i in range(2 * FC // 2)], split=True)
        for m in range(4):
            for g in range(3):
                plan.weights((L, "down", m, g), split=True)
            plan.fill((L, "down", m), 4 + m % 2)
            for g in range(3):
                plan.used[(L, "down", m, g)] = (("down_part", L), 2 * m + g + 1) if g < 2 else \
                    ("bank_full", plan.bank[(L, "down", m)])
    return plan


def trunk(nc, A, out, layers=(0, 1, 2, 3)):
    plan = make_plan(layers)
    ctx = ExitStack()
    with ctx:
        sems = {}

        def sem(*name):
            if name not in sems:
                sems[name] = ctx.enter_context(nc.semaphore("_".join(str(x) for x in name)))
            return sems[name]

        def sb(name, *shape):
            return ctx.enter_context(nc.sbuf_tensor(name, [P, *shape], F32))

        xT = sb("xT", DC, T)
        ring = sb("ring", NSLOT, SLOT)
        par = sb("par", PAR_BLOCKS * P)
        ident = sb("ident", P)
        mean_all = sb("mean_all", P)
        mean_head = sb("mean_head", P)
        sum_head = sb("sum_head", P)
        rstd = sb("rstd", T)
        warm = sb("warm", 2 * DEPTH)
        masks = sb("masks", 4, P)
        pair_masks = sb("pair_masks", 6, P)
        chunk_cols = sb("chunk_cols", P // CH)
        chunk_reset = sb("chunk_reset", T)
        head_eye = sb("head_eye", HALF)
        chunk_decay = sb("chunk_decay", DC, NCH)
        causal = sb("causal", P)
        swap = sb("swap", P)
        sign = sb("sign", 1)
        half_pi = sb("half_pi", 1)
        lam8 = sb("lam8", 3, S5_G)
        eps = sb("eps", 2)
        area_at = -(-nc.sbuf_base // 64) * 64

        def placed(name, slot, shape, dtype=F32R):
            return nc.alloc_sbuf_tensor_at(name, [P, *shape], dtype, offset=area_at + int(slot * 2048) * 4)

        work = placed("work", 0, [20, 2048], F32)
        w_high = [placed(f"w_high{i}", s, [2, DC, P]) for i, s in enumerate((17, 18))]
        w_low = [placed(f"w_low{i}", s, [2, DC, P]) for i, s in enumerate((19, 15))]
        inner_high = placed("inner_high", 0, [FC, T])
        inner_low = placed("inner_low", FC * T / 2048, [FC, T])
        x_high = placed("x_high", 7, [DC, T])
        x_low = placed("x_low", 8, [DC, T])
        banks = [ctx.enter_context(nc.psum_tensor(f"bank{i}", [P, 512], F32)) for i in range(8)]

        def slot_view(s, a, b):
            return work[:, s, 0:a * b].rearrange("p (a b) -> p a b", a=a)

        def col(name, i=0, r=0):
            i += PAR[name][0]
            return par[:, i:i + 1] if isinstance(r, int) else par[:, bass.ds(r * ROUND + i, 1)]

        def bank_of(key):
            return banks[plan.bank[key][0]]

        def wait_full(eng, key, more=0):
            b, n = plan.bank[key]
            eng.wait_ge(sem("bank_full", b), more + n)

        per_layer = dict(tap2_done=2 * FC, tap1_done=2 * FC, taps_done=2 * FC, silu_done=FC // 2,
                         inner_ready=FC // 2, inner_rounded=FC // 2, gated_done=FC // 2, down_part=8,
                         qk_raw=8, qk_squares=8, qk_mean=8, qk_root=8, qk_normed=8, v_ready=4, qi_ready=2,
                         ki_raw=2, ki_squares=1, ki_mean=1, ki_root=1, ki_ready=1, logits=2, relu_done=6,
                         att_full=8, att_masked=16, neg_max=8, exp_done=32, pt_full=8, pt_copied=12,
                         o_full=8, o_scaled=8, ot_full=2, ot_rounded=4, ot_ready=4)
        mlp_names = ("tap2_done", "tap1_done", "taps_done", "silu_done", "inner_ready", "inner_rounded", "gated_done",
                     "down_part")

        def since(name, L):
            if name not in per_layer:
                return 0
            earlier = [x for x in layers if x < L and (name in mlp_names or x % 3 == 0)]
            return per_layer[name] * len(earlier)

        def signal(name):
            return sem(name[0]), since(*name) if len(name) > 1 else 0

        vector_step, pool_step = Marks(sem("vector_step")), Marks(sem("pool_step"))

        hT = slot_view(16, DC, T)
        sq = [slot_view(8, DC, T), slot_view(13, DC, T)]

        def updates(L, ffn=0):
            return 4 * (1 + 2 * layers.index(L) + ffn)

        freed = {}
        for L in layers:
            if L % 3 == 0:
                for i in range(4):
                    freed[(L, "q", i)] = (("qk_raw", L), i + 1)
                    freed[(L, "k", i)] = (("qk_raw", L), 4 + i + 1)
                    freed[(L, "v", i)] = (("v_ready", L), i + 1)
                for i in range(2):
                    freed[(L, "i", i)] = (("qi_ready", L), i + 1)
                freed[(L, "s", 0)] = (("ki_raw", L), 2)
            if L % 3 == 1:
                for i in range(4):
                    for n, s in enumerate("krv"):
                        freed[(L, s, i)] = (("rkv_ready", L), 4 * n + i + 1)
                    freed[(L, "w", i)] = (("wa_ready", L), 2 * i + 2)
                    freed[(L, "a", i)] = (("wa_ready", L), 8 + 2 * i + 2)
                    freed[(L, "g", i)] = (("g_ready", L), i + 1)
                freed[(L, "lora1", 0)] = (("lora_ready", L), 3)
            if L % 3 == 2:
                for m in range(4):
                    freed[(L, "glu", 2 * m)] = (("glu_ready", L), m + 1)
                    freed[(L, "glu", 2 * m + 1)] = (("glu_gate", L), 2 * m + 2)
            else:
                for m in range(4):
                    freed[(L, "o", m)] = (("x_ready",), updates(L) + m + 1)
            for j in range(FC // 2):
                freed[(L, "up", 2 * j)] = (("taps_done", L), 4 * j + 2)
                freed[(L, "up", 2 * j + 1)] = (("taps_done", L), 4 * j + 4)
            for m in range(4):
                freed[(L, "down", m)] = (("x_ready",), updates(L, 1) + m + 1)
        by_fill = {v: k for k, v in plan.bank.items()}

        def wait_free(pe, key):
            b, n = plan.bank[key]
            if n > 1:
                name, value = freed[by_fill[(b, n - 1)]]
                done, offset = signal(name)
                pe.wait_ge(done, value + offset)

        PER_ROUND = ROUND // NSLOT * 16

        def landed(eng, key, r=0):
            _, slot, count = plan.tile[key]
            eng.wait_ge(sem("weights_in", slot), r * PER_ROUND + count)
            return ring[:, slot, :].rearrange("p (k n) -> p k n", n=TILE)

        def wait_used(eng, key, r=0):
            name, at = plan.used[key]
            if name == "bank_full":
                eng.wait_ge(sem("bank_full", at[0]), r + at[1])
            else:
                done, offset = signal(name)
                eng.wait_ge(done, at + offset)

        def rows_of(key):
            return min(DC, FC - key[3] * DC) if key[1] == "down" else DC

        def split_part(key, b, w):
            n = plan.split[key] % NSPLIT
            k = rows_of(key)
            return w[:, 0:k, b * P:(b + 1) * P], w_high[n][:, b, 0:k, :], w_low[n][:, b, 0:k, :]

        def round_weights(act, key, r=0):
            n = plan.split[key]
            w = landed(act, key, r)
            if n >= NSPLIT:
                wait_used(act, plan.split_tiles[n - NSPLIT], r)
            for b in range(2):
                raw, high, _ = split_part(key, b, w)
                act.activation(high, raw, ACT.Copy).then_inc(sem("w_rounded", b), 1)

        def rest_of_weights(eng, key, b, r=0):
            n = plan.split[key]
            w = ring[:, plan.tile[key][1], :].rearrange("p (k n) -> p k n", n=TILE)
            raw, high, low = split_part(key, b, w)
            eng.wait_ge(sem("w_rounded", b), r * ROUND + n + 1)
            eng.tensor_tensor(low, raw, high.bitcast(F32), ALU.subtract).then_inc(sem("w_split", b), 1)

        def ahead(split, eng, key, *block, r=0):
            n = plan.split[key] + NSPLIT
            if n < len(plan.split_tiles) and (plan.split_tiles[n][0] == key[0] or plan.split_tiles[n][0] % 3 == 0):
                split(eng, plan.split_tiles[n], *block, r=r)

        def split_weights(pe, key, b, r=0):
            n = plan.split[key]
            pe.wait_ge(sem("w_split", b), r * ROUND + n + 1)
            return w_high[n % NSPLIT][:, b], w_low[n % NSPLIT][:, b]

        def product(pe, out_, lhs, rhs, start, stop):
            pe.matmul(out_, lhs[0], rhs[0], start=start, stop=False, skip_group_check=True)
            pe.matmul(out_, lhs[0], rhs[1], start=False, stop=False, skip_group_check=True)
            return pe.matmul(out_, lhs[1], rhs[0], start=False, stop=stop, skip_group_check=True)

        def norm_squares(act, n):
            for m in range(4):
                if m == 3:
                    act.activation(warm[:, n:n + 1], eps[:, 0:1], ACT.Sqrt).then_inc(sem("warm"), 1)
                act.wait_ge(sem("x_ready"), 4 * n + m + 1)
                act.activation(sq[n % 2][:, 2 * m:2 * m + 2, :], xT[:, 2 * m:2 * m + 2, :],
                               ACT.Square).then_inc(sem("squares"), 1)

        def norm_mean(pe, n):
            for c in range(DC):
                if c % 2 == 0:
                    pe.wait_ge(sem("squares"), 4 * n + c // 2 + 1)
                mm = pe.matmul(banks[7][:, 0:T], mean_all[:, :], sq[n % 2][:, c, :], start=c == 0, stop=c == DC - 1)
            mm.then_inc(sem("mean_square"), 1)

        def norm_root(act, n):
            act.wait_ge(sem("mean_square"), n + 1)
            act.activation(rstd[:, :], banks[7][:, 0:T], ACT.Sqrt, bias=eps[:, 0:1]).then_inc(sem("root"), 1)

        def norm_scale(dve, n, gain, L):
            dve.wait_ge(sem("root"), n + 1)
            dve.reciprocal(rstd[:, :], rstd[:, :]).then_inc(sem("rstd"), 1)
            dve.wait_ge(sem("rstd"), n + 1)
            for c in range(DC + 1):
                if c < DC:
                    dve.scalar_tensor_tensor(out=hT[:, c, :], in0=xT[:, c, :], scalar=col(gain, L * DC + c),
                                             in1=rstd[:, :], op0=ALU.mult, op1=ALU.mult).then_inc(sem("h_ready"), 1)
                if c and splits_h(n):
                    dve.wait_ge(sem("h_rounded"), DC * h_splits(n) + c)
                    dve.tensor_tensor(x_low[:, c - 1, :], hT[:, c - 1, :], x_high[:, c - 1, :].bitcast(F32),
                                      ALU.subtract).then_inc(sem("h_split"), 1)

        def splits_h(n):
            return n % 2 == 1 or layers[n // 2] % 3 == 0

        def h_splits(n):
            return sum(splits_h(m) for m in range(n))

        def norm_round(act, n):
            for c in range(DC):
                wait_h(act, n, c)
                act.activation(x_high[:, c, :], hT[:, c, :], ACT.Copy).then_inc(sem("h_rounded"), 1)

        def norm_index(L, ffn):
            return 2 * layers.index(L) + ffn

        def wait_h(eng, n, c=DC - 1):
            eng.wait_ge(sem("h_ready"), DC * n + c + 1)

        def wait_split_h(pe, n, c=DC - 1):
            pe.wait_ge(sem("h_split"), DC * h_splits(n) + c + 1)

        def project(pe, key, x, ready=None):
            wait_free(pe, key)
            parts = {}
            for k, b in chunks_and_blocks(DC, ready):
                if ready and b == 0:
                    ready(k)
                if b not in parts:
                    parts[b] = split_weights(pe, key, b) if key in plan.split else landed(pe, key)
                out_, start, stop = bank_of(key)[:, b * T:(b + 1) * T], k == 0 and (b == 0 or not ready), k == DC - 1
                if key in plan.split:
                    mm = product(pe, out_, (parts[b][0][:, k, :], parts[b][1][:, k, :]), (x[0][:, k, :], x[1][:, k, :]),
                                 start, stop)
                else:
                    mm = pe.matmul(out_, parts[b][:, k, b * P:(b + 1) * P], x[:, k, :], start=start, stop=stop,
                                   skip_group_check=True)
            mm.then_inc(sem("bank_full", plan.bank[key][0]), 1)

        def chunks_and_blocks(n, as_ready):
            if as_ready:
                return [(k, b) for k in range(n) for b in range(2)]
            return [(k, b) for b in range(2) for k in range(n)]

        def project_tokens(pe, key, x):
            wait_free(pe, key)
            split_weights(pe, key, 0)
            split_weights(pe, key, 1)
            n = plan.split[key] % NSPLIT
            for b in range(TT):
                tok = slice(b * P, (b + 1) * P)
                for k in range(DC):
                    mm = product(pe, bank_of(key)[:, b * TILE:(b + 1) * TILE], (x[0][:, k, tok], x[1][:, k, tok]),
                                 (w_high[n][:, :, k, :], w_low[n][:, :, k, :]), k == 0, k == DC - 1)
            mm.then_inc(sem("bank_full", plan.bank[key][0]), 1)

        def add_residual(dve, L, s):
            for m in range(4):
                if s == "down":
                    for g in range(3):
                        ahead(rest_of_weights, dve, (L, s, m, g), 0)
                        if before_s5(L):
                            s5_tables(dve, 3 * m + g)
                wait_full(dve, (L, s, m))
                pair = xT[:, 2 * m:2 * m + 2, :]
                dve.tensor_tensor(pair, pair, bank_of((L, s, m))[:, :].rearrange("p (a b) -> p a b", a=2),
                                  ALU.add).then_inc(sem("x_ready"), 1)
                if s == "o" and (L, s, m) in plan.split:
                    ahead(rest_of_weights, dve, (L, s, m), 0)

        def wait_slot(sp, key, r=0):
            n = plan.tile[key][0] - NSLOT
            if n >= 0:
                old = plan.tiles[n]
                if old in plan.split:
                    for b in range(2):
                        sp.wait_ge(sem("w_split", b), r * ROUND + plan.split[old] + 1)
                else:
                    wait_used(sp, old)

        def send(sp, key, pieces, r=0):
            slot = plan.tile[key][1]
            wait_slot(sp, key, r)
            dst = ring[:, slot, :].rearrange("p (k n) -> p k n", n=TILE)
            for place, src in pieces(dst):
                sp.dma_start(place, src).then_inc(sem("weights_in", slot), 16)

        def rows(w, c0, k0=0, kn=DC, cn=TILE):
            v = w.rearrange("(k p) n -> p k n", p=P)
            cols = slice(c0, c0 + cn) if isinstance(c0, int) else bass.ds(c0, cn)
            return v[:, k0:k0 + kn, cols]

        def send_plain(sp, key, w, c0):
            send(sp, key, lambda dst: [(dst, rows(w, c0))])

        def send_dsa(sp, L):
            w = A["dsa_w_in"][L // 3]
            for n, s in enumerate("qkv"):
                for i in range(4):
                    send_plain(sp, (L, s, i), w, n * D + i * TILE)
            for i in range(2):
                send_plain(sp, (L, "i", i), w, 3 * D + i * TILE)
            c = 3 * D + IDX_HEADS * HALF
            send(sp, (L, "s", 0), lambda dst: [(dst[:, :, 0:HALF], rows(w, c, cn=HALF)),
                                               (dst[:, :, HALF:P], rows(w, c, cn=HALF)),
                                               (dst[:, :, P:P + IDX_HEADS], rows(w, c + HALF, cn=IDX_HEADS))])
            for i in range(4):
                send_plain(sp, (L, "o", i), A["dsa_w_out"][L // 3], i * TILE)

        UP_TILES = FC
        LOOPED = UP_TILES // ROUND - 1
        REST = ROUND * (LOOPED + 1)

        def send_mlp(sp, L):
            up, down = A["ffn_w_up"][L], A["ffn_w_down"][L]

            def up_tile(k, r=0):
                c0 = k % 2 * F + k // 2 * TILE
                send(sp, (L, "up", k), lambda dst: [(dst, rows(up, c0 + r * (ROUND // 2 * TILE)))], r)

            for k in range(ROUND):
                up_tile(k)
            with sp.Fori(0, LOOPED) as r:
                for k in range(ROUND, 2 * ROUND):
                    up_tile(k, r)
            for k in range(REST, UP_TILES):
                up_tile(k)
            for m in range(4):
                for g in range(3):
                    kn = rows_of((L, "down", m, g))
                    send(sp, (L, "down", m, g),
                         lambda dst: [(dst[:, 0:kn, :], rows(down, m * TILE, g * DC, kn))])

        conv = work[:, 9:11, :].rearrange("p a b -> p (a b)")[:, 0:3 * 1024].rearrange(
            "p (j h c t) -> p j h c t", j=3, h=2, c=2)
        gated = work[:, 10:12, :].rearrange("p a b -> p (a b)")[:, 1024:2560].rearrange(
            "p (j c t) -> p j c t", j=3, c=2)

        def over_up_tiles(eng, pair):
            for j in range(ROUND // 2):
                pair(j, 0)
            with eng.Fori(0, LOOPED) as r:
                for j in range(ROUND // 2, ROUND):
                    pair(j, r)
            for j in range(REST // 2, UP_TILES // 2):
                pair(j, 0)

        PJ = ROUND // 2

        def before_s5(L):
            return L + 1 in layers and (L + 1) % 3 == 2

        def mlp_pe(pe, L):
            n = norm_index(L, 1)

            def pair(j, r):
                for h in range(2):
                    key = (L, "up", 2 * j + h)
                    if j >= PJ:
                        name, value = freed[(L, "up", 2 * j + h - ROUND)]
                        done, offset = signal(name)
                        pe.wait_ge(done, r * (4 * PJ) + (value + offset))
                    else:
                        wait_free(pe, key)
                    bank = plan.bank[key][0]
                    parts, first = {}, j == 0 and h == 0
                    for c, b in chunks_and_blocks(DC, first):
                        if first:
                            wait_split_h(pe, n, c)
                        if b not in parts:
                            parts[b] = split_weights(pe, key, b, r)
                        mm = product(pe, banks[bank][:, b * T:(b + 1) * T], (parts[b][0][:, c, :], parts[b][1][:, c, :]),
                                     (x_high[:, c, :], x_low[:, c, :]), c == 0 and (b == 0 or not first), c == DC - 1)
                    mm.then_inc(sem("bank_full", bank), 1)

            over_up_tiles(pe, pair)
            for m in range(4):
                key = (L, "down", m)
                bank = plan.bank[key][0]
                wait_free(pe, key)
                for g in range(3):
                    if m == 0:
                        pe.wait_ge(sem("inner_ready"), min(4 * (g + 1), FC // 2) + since("inner_ready", L))
                    kn = rows_of((L, "down", m, g))
                    for b in range(2):
                        high, low = split_weights(pe, (L, "down", m, g), b)
                        for k in range(kn):
                            c = g * DC + k
                            mm = product(pe, banks[bank][:, b * T:(b + 1) * T], (high[:, k, :], low[:, k, :]),
                                         (inner_high[:, c, :], inner_low[:, c, :]),
                                         g == 0 and k == 0 and b == 0, g == 2 and k == kn - 1)
                    mm.then_inc(sem("down_part") if g < 2 else sem("bank_full", bank), 1)
                if m == 0 and before_s5(L):
                    s5_turn_a(pe)
            if before_s5(L):
                s5_turn_c(pe)

        def mlp_act(act, L):
            def round_inner(j, r):
                act.wait_ge(sem("gated_done"), r * PJ + (j + 1 + since("gated_done", L)))
                act.activation(inner_high[:, at(2 * j, r), :], gated[:, j % 3], ACT.Copy).then_inc(sem("inner_rounded"), 1)

            def pair(j, r):
                for h in range(2):
                    key = (L, "up", 2 * j + h)
                    wait_full(act, key, r)
                    for b in range(2):
                        c = h * FC + 2 * j + b
                        act.activation(conv[:, j % 3, h, b, :], bank_of(key)[:, b * T:(b + 1) * T], ACT.Identity,
                                       bias=col("ffn_conv_b", c + L * 2 * FC, r),
                                       scale=col("ffn_conv_w", c + (L * 3 + 2) * 2 * FC, r)).then_inc(sem("tap2_done"), 1)
                    ahead(round_weights, act, key, r=r)
                act.wait_ge(sem("taps_done"), r * (4 * PJ) + (4 * j + 2 + since("taps_done", L)))
                act.activation(conv[:, j % 3, 0], conv[:, j % 3, 0], ACT.Silu).then_inc(sem("silu_done"), 1)
                if j:
                    round_inner(j - 1, r)

            over_up_tiles(act, pair)
            round_inner(UP_TILES // 2 - 1, 0)
            for m in range(4):
                for g in range(3):
                    ahead(round_weights, act, (L, "down", m, g))
                    if before_s5(L):
                        s5_exponentials(act, 3 * m + g)

        def at(c, r, n=2):
            return slice(c, c + n) if isinstance(r, int) else bass.ds(r * ROUND + c, n)

        def mlp_pool(pool, L):
            def rest_of_inner(j, r):
                pool.wait_ge(sem("inner_rounded"), r * PJ + (j + 1 + since("inner_rounded", L)))
                pool.tensor_tensor(inner_low[:, at(2 * j, r), :], gated[:, j % 3],
                                   inner_high[:, at(2 * j, r), :].bitcast(F32), ALU.subtract).then_inc(sem("inner_ready"), 1)

            def pair(j, r):
                for h in range(2):
                    ahead(rest_of_weights, pool, (L, "up", 2 * j + h), 1, r=r)
                if j:
                    rest_of_inner(j - 1, r)

            over_up_tiles(pool, pair)
            rest_of_inner(UP_TILES // 2 - 1, 0)
            for m in range(4):
                for g in range(3):
                    ahead(rest_of_weights, pool, (L, "down", m, g), 1)

        def mlp_dve(dve, L):
            def pair(j, r):
                for h in range(2):
                    bank = bank_of((L, "up", 2 * j + h))
                    for tap in (1, 0):
                        for b in range(2):
                            c = h * FC + 2 * j + b
                            lag = 2 - tap
                            if tap == 1:
                                dve.wait_ge(sem("tap2_done"), r * (4 * PJ) + (4 * j + 2 * h + 2 + since("tap2_done", L)))
                                done = sem("tap1_done")
                            else:
                                dve.wait_ge(sem("tap1_done"), r * (4 * PJ) + (4 * j + 2 * h + b + 1 + since("tap1_done", L)))
                                done = sem("taps_done")
                            row = conv[:, j % 3, h, b, lag:T]
                            dve.scalar_tensor_tensor(
                                out=row, in0=bank[:, b * T:(b + 1) * T - lag],
                                scalar=col("ffn_conv_w", c + (L * 3 + tap) * 2 * FC, r),
                                in1=row, op0=ALU.mult, op1=ALU.add).then_inc(done, 1)
                    ahead(rest_of_weights, dve, (L, "up", 2 * j + h), 0, r=r)
                dve.wait_ge(sem("silu_done"), r * PJ + (j + 1 + since("silu_done", L)))
                dve.wait_ge(sem("taps_done"), r * (4 * PJ) + (4 * j + 4 + since("taps_done", L)))
                if j >= 3:
                    dve.wait_ge(sem("inner_ready"), r * PJ + (j - 2 + since("inner_ready", L)))
                dve.tensor_tensor(gated[:, j % 3], conv[:, j % 3, 0], conv[:, j % 3, 1],
                                  ALU.mult).then_inc(sem("gated_done"), 1)

            over_up_tiles(dve, pair)
            add_residual(dve, L, "down")

        qT, kT = slot_view(0, DC, T), slot_view(1, DC, T)
        v_tok = slot_view(2, TT, D)
        qiT = work[:, 3, 0:1024].rearrange("p (c t) -> p c t", t=T)
        kiT = work[:, 3, 1024:1280]
        ki_sq = work[:, 3, 1280:1536]
        rs_qk = work[:, 12, 0:1024].rearrange("p (b n) -> p b n", b=2)
        qk_sq = work[:, 4, 0:1024].rearrange("p (b n) -> p b n", b=2)
        relu = [work[:, 4, 1024:2048].rearrange("p (h k) -> p h k", h=IDX_HEADS),
                work[:, 5, :].rearrange("p (h k) -> p h k", h=IDX_HEADS)]
        score = [work[:, 6, 0:128], work[:, 6, 256:512]]
        bias = [work[:, 6, 512:640], work[:, 6, 768:1024]]
        top8 = work[:, 6, 1024:1032]
        w_idx = work[:, 6, 1040:1056]
        row_max = work[:, 6, 1056:1088]
        neg_max = work[:, 6, 1088:1120]
        row_sum = work[:, 6, 1120:1152]
        recip = work[:, 6, 1152:1184]
        att = work[:, 7, :].rearrange("p (b n) -> p b n", b=2)
        prob = work[:, 8, :].rearrange("p (b n) -> p b n", b=2)
        probT = work[:, 9, :].rearrange("p (b n) -> p b n", b=2)
        o_tok = slot_view(10, TT, D)
        x_parts = (x_high, x_low)
        HG = 4
        NU = TT * DSA_HEADS // HG

        def unit(u):
            qt, g = divmod(u, DSA_HEADS // HG)
            return qt, HG * g, qt + 1

        def before(u):
            return sum(unit(x)[2] for x in range(u))

        def order(h0, i):
            return h0 + 2 * (i % 2) + i // 2

        IDX_ORDER = [0, 2, 4, 6, 1, 3, 5, 7]

        def heads(x, h):
            return x[HALF * (h % 2):HALF * (h % 2) + HALF, h // 2, :]

        def dsa_pe(pe, L):
            n = norm_index(L, 0)

            def mean_square(i):
                pe.wait_ge(sem("qk_raw"), i + 1 + since("qk_raw", L))
                if i >= 2:
                    pe.wait_ge(sem("qk_root"), i - 1 + since("qk_root", L))
                pe.matmul(banks[6 + i % 2][:, :], mean_head[:, :], qk_sq[:, i % 2, :], start=True,
                          stop=True).then_inc(sem("qk_mean"), 1)

            for i, key in enumerate([(L, s, i) for s in "qk" for i in range(4)]):
                project(pe, key, x_parts, (lambda c: wait_split_h(pe, n, c)) if i == 0 else None)
                if i:
                    mean_square(i - 1)
            project_tokens(pe, (L, "v", 0), x_parts)
            mean_square(7)
            for i in range(1, 4):
                project_tokens(pe, (L, "v", i), x_parts)
            for i in range(2):
                project(pe, (L, "i", i), x_parts)
            key = (L, "s", 0)
            w = landed(pe, key)
            wait_free(pe, key)
            bank = bank_of(key)
            for k in range(DC):
                pe.matmul(bank[:, 0:T], w[:, k, 0:P], hT[:, k, :], start=k == 0, stop=k == DC - 1)
            for b in range(TT):
                for k in range(DC):
                    mm = pe.matmul(bank[:, T + b * IDX_HEADS:T + (b + 1) * IDX_HEADS], hT[:, k, b * P:(b + 1) * P],
                                   w[:, k, P:P + IDX_HEADS], start=k == 0, stop=k == DC - 1)
            mm.then_inc(sem("bank_full", plan.bank[key][0]), 1)
            pe.wait_ge(sem("ki_raw"), 2 + since("ki_raw", L))
            pe.matmul(banks[6][:, 0:T], mean_head[:, :], ki_sq, start=True, stop=True).then_inc(sem("ki_mean"), 1)

            def scores(u):
                qt, h0, nk = unit(u)
                if u >= 2:
                    pe.wait_ge(sem("att_masked"), 2 * (u - 1) + since("att_masked", L))
                for i in range(HG):
                    bank = banks[2 * (u % 2) + i // 2]
                    at = (i % 2) * nk * P
                    h = order(h0, i)
                    mm = pe.matmul(bank[:, at:at + nk * P], heads(qT, h)[:, qt * P:(qt + 1) * P],
                                   heads(kT, h)[:, 0:nk * P], start=True, stop=True)
                mm.then_inc(sem("att_full"), 1)

            pe.wait_ge(sem("ki_ready"), 1 + since("ki_ready", L))
            for qt, first, per in ((0, 4, 4), (1, 0, 2)):
                kw = (qt + 1) * P
                for i, h in enumerate(IDX_ORDER):
                    at = (i % per) * kw
                    mm = pe.matmul(banks[first + i // per][:, at:at + kw],
                                   heads(qiT, h)[:, qt * P:(qt + 1) * P],
                                   kiT[HALF * (h % 2):HALF * (h % 2) + HALF, 0:kw], start=True, stop=True)
                mm.then_inc(sem("logits"), 1)

            def turn(u):
                qt, h0, nk = unit(u)
                pe.wait_ge(sem("exp_done"), HG * (u + 1) + since("exp_done", L))
                if u:
                    pe.wait_ge(sem("pt_copied"), before(u) + since("pt_copied", L))
                for i in range(HG * nk):
                    mm = pe.transpose(banks[4 + i // 4][:, (i % 4) * P:(i % 4 + 1) * P],
                                      prob[:, u % 2, i * P:(i + 1) * P], ident[:, :])
                mm.then_inc(sem("pt_full"), 1)

            def values(u):
                qt, h0, nk = unit(u)
                pe.wait_ge(sem("pt_copied"), before(u + 1) + since("pt_copied", L))
                if u >= 2:
                    pe.wait_ge(sem("o_scaled"), u - 1 + since("o_scaled", L))
                for i in range(HG):
                    h = order(h0, i)
                    for kt in range(nk):
                        at = (i * nk + kt) * P
                        mm = pe.matmul(banks[6 + u % 2][:, (h - h0) * HALF:(h - h0 + 1) * HALF], probT[:, u % 2, at:at + P],
                                       v_tok[:, kt, h * HALF:(h + 1) * HALF], start=kt == 0, stop=kt == nk - 1)
                mm.then_inc(sem("o_full"), 1)

            pe.wait_ge(sem("relu_done"), 6 + since("relu_done", L))
            scores(0)
            scores(1)
            for u in range(NU):
                turn(u)
                if u + 2 < NU:
                    scores(u + 2)
                values(u)
            pe.wait_ge(sem("o_scaled"), NU + since("o_scaled", L))
            for qt in range(TT):
                for c in range(DC):
                    mm = pe.transpose(banks[2 * qt + c // 4][:, (c % 4) * P:(c % 4 + 1) * P],
                                      o_tok[:, qt, c * P:(c + 1) * P], ident[:, :])
                mm.then_inc(sem("ot_full"), 1)
            pe.wait_ge(sem("ot_ready"), 4 + since("ot_ready", L))
            for m in range(4):
                project(pe, (L, "o", m), x_parts)

        def dsa_act(act, L):
            def root(i):
                act.wait_ge(sem("qk_mean"), i + 1 + since("qk_mean", L))
                if i >= 2:
                    act.wait_ge(sem("qk_normed"), i - 1 + since("qk_normed", L))
                act.activation(rs_qk[:, i % 2, :], banks[6 + i % 2][:, :], ACT.Sqrt,
                               bias=eps[:, 0:1]).then_inc(sem("qk_root"), 1)

            for i, key in enumerate([(L, s, i) for s in "qk" for i in range(4)]):
                x = qT if i < 4 else kT
                m = i % 4
                wait_full(act, key)
                ahead(round_weights, act, key)
                if i >= 2:
                    act.wait_ge(sem("qk_mean"), i - 1 + since("qk_mean", L))
                act.activation(qk_sq[:, i % 2, :], bank_of(key)[:, :], ACT.Square).then_inc(sem("qk_squares"), 1)
                act.activation(x[:, 2 * m:2 * m + 2, :].rearrange("p a b -> p (a b)"), bank_of(key)[:, :],
                               ACT.Copy).then_inc(sem("qk_raw"), 1)
                if i:
                    root(i - 1)
            root(7)
            for i in range(4):
                wait_full(act, (L, "v", i))
                ahead(round_weights, act, (L, "v", i))
                act.activation(v_tok[:, :, i * TILE:(i + 1) * TILE],
                               bank_of((L, "v", i))[:, :].rearrange("p (a b) -> p a b", a=TT),
                               ACT.Copy).then_inc(sem("v_ready"), 1)
            for i in range(2):
                wait_full(act, (L, "i", i))
                act.activation(qiT[:, 2 * i:2 * i + 2, :].rearrange("p a b -> p (a b)"), bank_of((L, "i", i))[:, :],
                               ACT.Copy).then_inc(sem("qi_ready"), 1)
            key = (L, "s", 0)
            wait_full(act, key)
            act.activation(ki_sq, bank_of(key)[:, 0:T], ACT.Square).then_inc(sem("ki_squares"), 1)
            act.activation(kiT, bank_of(key)[:, 0:T], ACT.Copy).then_inc(sem("ki_raw"), 1)
            act.activation(w_idx, bank_of(key)[:, T:T + TT * IDX_HEADS], ACT.Copy,
                           scale=IDX_HEADS ** -0.5).then_inc(sem("ki_raw"), 1)
            act.wait_ge(sem("ki_mean"), 1 + since("ki_mean", L))
            act.wait_ge(sem("qk_normed"), 7 + since("qk_normed", L))
            act.activation(rs_qk[:, 0, 0:T], banks[6][:, 0:T], ACT.Sqrt, bias=eps[:, 0:1]).then_inc(sem("ki_root"), 1)
            for qt, first, per in ((0, 4, 4), (1, 0, 2)):
                act.wait_ge(sem("logits"), qt + 1 + since("logits", L))
                for b in range(IDX_HEADS // per):
                    act.activation(relu[qt][:, b * per:(b + 1) * per, :].rearrange("p a b -> p (a b)"),
                                   banks[first + b][:, :], ACT.Relu,
                                   scale=HALF ** -0.5).then_inc(sem("relu_done"), 1)

            def copy_turned(u):
                _, _, nk = unit(u)
                act.wait_ge(sem("pt_full"), u + 1 + since("pt_full", L))
                if u >= 2:
                    act.wait_ge(sem("o_full"), u - 1 + since("o_full", L))
                for b in range(nk):
                    act.activation(probT[:, u % 2, b * 512:(b + 1) * 512], banks[4 + b][:, :],
                                   ACT.Copy).then_inc(sem("pt_copied"), 1)

            for u in range(NU):
                qt, h0, nk = unit(u)
                act.wait_ge(sem("neg_max"), u + 1 + since("neg_max", L))
                if u >= 2:
                    act.wait_ge(sem("pt_full"), u - 1 + since("pt_full", L))
                for i in range(HG):
                    r = slice(i * nk * P, (i + 1) * nk * P)
                    n, m = u * HG + i, u * HG + order(0, i)
                    act.activation(prob[:, u % 2, r], att[:, u % 2, r], ACT.Exp, bias=neg_max[:, n:n + 1],
                                   scale=HALF ** -0.5, accum_out=row_sum[:, m:m + 1]).then_inc(sem("exp_done"), 1)
                if u:
                    copy_turned(u - 1)
            for i in range(2):
                ahead(round_weights, act, (L, "i", i))
            copy_turned(NU - 1)
            for qt in range(TT):
                act.wait_ge(sem("ot_full"), qt + 1 + since("ot_full", L))
                for b in range(2):
                    act.activation(x_high[:, 4 * b:4 * b + 4, qt * P:(qt + 1) * P],
                                   banks[2 * qt + b][:, :].rearrange("p (a b) -> p a b", a=4),
                                   ACT.Copy).then_inc(sem("ot_rounded"), 1)
            for m in range(4):
                ahead(round_weights, act, (L, "o", m))


        def dsa_dve(dve, L):
            j = L // 3
            step = vector_step

            def then(ins):
                dve.wait_ge(step.sem, step.mark(ins))

            for i in range(8):
                x = qT if i < 4 else kT
                m = i % 4
                for k in range(2) if i == 0 else (i + 1,) if i < 7 else ():
                    ahead(rest_of_weights, dve, (L, "qk"[k // 4], k % 4), 0)
                dve.wait_ge(sem("qk_root"), i + 1 + since("qk_root", L))
                then(dve.reciprocal(rs_qk[:, i % 2, :], rs_qk[:, i % 2, :]))
                pair = x[:, 2 * m:2 * m + 2, :].rearrange("p a b -> p (a b)")
                dve.scalar_tensor_tensor(out=pair, in0=pair, scalar=col("dsa_q_norm" if i < 4 else "dsa_k_norm", j),
                                         in1=rs_qk[:, i % 2, :], op0=ALU.mult, op1=ALU.mult).then_inc(sem("qk_normed"), 1)
            for i in range(4):
                ahead(rest_of_weights, dve, (L, "v", i), 0)
            dve.wait_ge(sem("ki_root"), 1 + since("ki_root", L))
            then(dve.reciprocal(rs_qk[:, 0, 0:T], rs_qk[:, 0, 0:T]))
            dve.scalar_tensor_tensor(out=kiT, in0=kiT, scalar=col("dsa_kidx_norm", j), in1=rs_qk[:, 0, 0:T],
                                     op0=ALU.mult, op1=ALU.mult).then_inc(sem("ki_ready"), 1)

            def top_keys(qt):
                s = score[qt]
                w = w_idx[:, qt * IDX_HEADS:(qt + 1) * IDX_HEADS]
                dve.wait_ge(sem("relu_done"), 2 + 4 * qt + since("relu_done", L))
                then(dve.tensor_scalar(s, relu[qt][:, 0, :], w[:, 0:1], None, ALU.mult))
                for i, h in list(enumerate(IDX_ORDER))[1:]:
                    then(dve.scalar_tensor_tensor(out=s, in0=relu[qt][:, i, :], scalar=w[:, h:h + 1], in1=s,
                                                  op0=ALU.mult, op1=ALU.add))
                then(dve.memset(s[0:Q_BLOCK, qt * P + Q_BLOCK:(qt + 1) * P], MASKED))
                for _ in range(TOPK // 8):
                    then(dve.max(top8, s))
                    then(dve.match_replace(s, top8, s, TAKEN))
                then(dve.tensor_scalar(bias[qt], s, TAKEN / 2, MASKED, ALU.is_gt, ALU.mult))

            top_keys(0)

            def scale_values(u):
                qt, h0, _ = unit(u)
                dve.wait_ge(sem("o_full"), u + 1 + since("o_full", L))
                r = slice(u * HG, (u + 1) * HG)
                then(dve.reciprocal(recip[:, r], row_sum[:, r]))
                o = o_tok[:, qt, h0 * HALF:(h0 + HG) * HALF].rearrange("p (h d) -> p h d", h=HG)
                dve.tensor_tensor(o, banks[6 + u % 2][:, 0:HG * HALF].rearrange("p (h d) -> p h d", h=HG),
                                  recip[:, r].unsqueeze(2).to_broadcast([P, HG, HALF]),
                                  ALU.mult).then_inc(sem("o_scaled"), 1)

            for u in range(NU):
                qt, h0, nk = unit(u)
                dve.wait_ge(sem("att_full"), u + 1 + since("att_full", L))
                if u >= 2:
                    dve.wait_ge(sem("exp_done"), HG * (u - 1) + since("exp_done", L))
                w = 2 * nk * P
                for b in range(2):
                    dve.tensor_tensor(
                        att[:, u % 2, b * w:(b + 1) * w].rearrange("p (h k) -> p h k", h=2),
                        banks[2 * (u % 2) + b][:, 0:w].rearrange("p (h k) -> p h k", h=2),
                        bias[qt].unsqueeze(1).to_broadcast([P, 2, nk * P]),
                        ALU.add).then_inc(sem("att_masked"), 1)
                dve.wait_ge(sem("att_masked"), 2 * (u + 1) + since("att_masked", L))
                r = slice(u * HG, (u + 1) * HG)
                then(dve.tensor_reduce(row_max[:, r], att[:, u % 2, 0:512 * nk].rearrange("p (h k) -> p h k", h=HG),
                                       AX_X, ALU.max))
                dve.tensor_scalar(neg_max[:, r], row_max[:, r], -HALF ** -0.5, None,
                                  ALU.mult).then_inc(sem("neg_max"), 1)
                if u >= 2:
                    scale_values(u - 2)
                if u == 1:
                    top_keys(1)
            scale_values(NU - 2)
            for i in range(2):
                ahead(rest_of_weights, dve, (L, "i", i), 0)
            scale_values(NU - 1)
            for qt in range(TT):
                for b in range(2):
                    r = (slice(None), slice(4 * b, 4 * b + 4), slice(qt * P, (qt + 1) * P))
                    dve.wait_ge(sem("ot_rounded"), 2 * qt + b + 1 + since("ot_rounded", L))
                    dve.tensor_tensor(x_low[r], banks[2 * qt + b][:, :].rearrange("p (a b) -> p a b", a=4),
                                      x_high[r].bitcast(F32), ALU.subtract).then_inc(sem("ot_ready"), 1)
            add_residual(dve, L, "o")

        def dsa_pool(pool, L):
            for s in "qkvio":
                for i in range(2 if s == "i" else 4):
                    ahead(rest_of_weights, pool, (L, s, i), 1)

        flat = work[:, :, :].rearrange("p a b -> p (a b)")
        big = flat[:, 0:4 * 2048].rearrange("p (h s t) -> p h s t", h=DC, s=4)
        PT_all = flat[:, 0:4 * 2048].rearrange("p (h s c j) -> p h s c j", h=DC, s=2, j=HALF)
        rT, bonus, gT, y0T = (slot_view(i, DC, T) for i in (4, 5, 6, 7))
        y_gated = slot_view(11, DC, T)
        dh = slot_view(8, DC, T)
        MIXES = "wagkrv"
        mixed = dict(zip(MIXES, (slot_view(i, DC, T) for i in (17, 18, 19, 9, 10, 11))))
        kraw, sg, aT = (slot_view(i, DC, T) for i in (12, 14, 15))
        hidden = work[:, 7, 0:512]
        csum, e_prev, e_in, e_neg = (slot_view(i, DC, T) for i in (17, 18, 19, 13))
        kk, kk_sq = slot_view(5, DC, T), slot_view(8, DC, T)
        inv, rk = hT, hT
        GROUP = 5888

        def group(par_, first, n):
            base = 8 * 2048 + par_ * GROUP + first
            return flat[:, base:base + n]

        MM = [group(p, 0, 2560).rearrange("p (s u t) -> p s u t", s=5, t=P) for p in (0, 1)]
        Tm = [group(p, 2560, 512) for p in (0, 1)]
        TmT = [group(p, 3072, 512) for p in (0, 1)]
        Zm = [group(p, 3584, 512) for p in (0, 1)]
        M12 = [group(p, 4096, 512).rearrange("p (s u d) -> p s u d", s=2, d=HALF) for p in (0, 1)]
        AkV = [group(p, 4608, 256) for p in (0, 1)]
        Nat = [group(p, 4864, 1024).rearrange("p (s u d) -> p s u d", s=4, d=HALF) for p in (0, 1)]
        BX, VX, M2X = ([flat[:, at + i * 1024:at + (i + 1) * 1024] for at in (8 * 2048 + 2 * GROUP, 17 * 2048)]
                       for i in range(3))
        MEAN_BANK = (6, 7, 2, 3)
        NLEV = 4

        def send_rwkv(sp, L):
            send(sp, (L, "lora1", 0), lambda dst: [(dst[:, :, 0:HALF], rows(A["rwkv_w1"][0], 0, cn=HALF)),
                                                   (dst[:, :, HALF:P], rows(A["rwkv_a1"][0], 0, cn=HALF)),
                                                   (dst[:, :, P:2 * P], rows(A["rwkv_g1"][0], 0, cn=P))])

            def second(dst):
                wide = dst.rearrange("p k n -> p (k n)")
                return [(wide[0:HALF, 0:D], A["rwkv_w2"][0]), (wide[HALF:P, 0:D], A["rwkv_a2"][0]),
                        (wide[:, D:2 * D], A["rwkv_g2"][0])]

            send(sp, (L, "lora2", 0), second)
            for s in "krv":
                for i in range(4):
                    send_plain(sp, (L, s, i), A["rwkv_w_rkv"][0, "rkv".index(s)], i * TILE)
            for i in range(4):
                send_plain(sp, (L, "o", i), A["rwkv_w_out"][0], i * TILE)

        def level(l, hp):
            return (hp // 2) * 2 * NLEV + 2 * l + hp % 2 + 1

        def by_pairs(steps):
            for g in range(0, DC, 2):
                for step in steps:
                    for hp in (g, g + 1):
                        step(hp)

        def half_rows(h):
            return slice(HALF * h, HALF * h + HALF)

        def rwkv_pe(pe, L):
            key = (L, "lora1", 0)
            w = landed(pe, key)
            wait_free(pe, key)
            bank = bank_of(key)
            for i, (dst, c0, c1, x) in enumerate(((bank[0:HALF, 0:T], 0, HALF, mixed["w"]), (bank[HALF:P, 0:T], HALF, P, mixed["a"]),
                                   (bank[:, T:2 * T], P, 2 * P, mixed["g"]))):
                for k in range(DC):
                    pe.wait_ge(sem("mixed"), i * DC + k + 1)
                    mm = pe.matmul(dst, w[:, k, c0:c1], x[:, k, :], start=k == 0, stop=k == DC - 1)
            mm.then_inc(sem("bank_full", plan.bank[key][0]), 1)
            w = landed(pe, (L, "lora2", 0)).rearrange("p k n -> p (k n)")
            pe.wait_ge(sem("lora_ready"), 3)
            for s, r, c0, x in (("w", slice(0, HALF), 0, hidden[:, 0:T]), ("a", slice(HALF, P), 0, hidden[:, 0:T]),
                                ("g", slice(0, P), D, hidden[:, T:2 * T])):
                for i in range(4):
                    key = (L, s, i)
                    wait_free(pe, key)
                    for b in range(2):
                        c = c0 + (2 * i + b) * P
                        mm = pe.matmul(bank_of(key)[:, b * T:(b + 1) * T], w[r, c:c + P], x[r, :], start=True, stop=True)
                    mm.then_inc(sem("bank_full", plan.bank[key][0]), 1)
            for n, s in enumerate("krv"):
                for i in range(4):
                    project(pe, (L, s, i), mixed[s],
                            (lambda c, n=n: pe.wait_ge(sem("mixed"), DC * (3 + n) + c + 1)) if i == 0 else None)
                    if s == "r" and i == 0:
                        for m in range(4):
                            pe.wait_ge(sem("kk_squares"), m + 1)
                            if m >= 2:
                                pe.wait_ge(sem("kk_root"), m - 1)
                            pe.matmul(banks[6 + m % 2][:, :], sum_head[:, :], kk_sq[:, 2 * m:2 * m + 2, :], start=True,
                                      stop=True).then_inc(sem("kk_sum"), 1)
            pe.wait_ge(sem("kk_root"), 4)
            for m in range(4):
                pe.wait_ge(sem("rk_done"), 2 * m + 2)
                if m >= 2:
                    pe.wait_ge(sem("bonus_done"), m - 1)
                pe.matmul(banks[6 + m % 2][:, :], sum_head[:, :], rk[:, 2 * m:2 * m + 2, :], start=True,
                          stop=True).then_inc(sem("rk_sum"), 1)
            pe.wait_ge(sem("rkv_ready"), 12)
            pe.wait_ge(sem("factors_done"), 4)

            def bank3(hp):
                return banks[3 * (hp % 2):3 * (hp % 2) + 3]

            def natural(hp):
                X, Y, _ = bank3(hp)
                if hp >= 2:
                    pe.wait_ge(sem("r1_done"), hp - 1)
                    pe.wait_ge(sem("y0_done"), hp - 1)
                for s in range(4):
                    for b in range(TT):
                        mm = pe.transpose((X, Y)[s // 2][:, ((s % 2) * 2 + b) * P:((s % 2) * 2 + b + 1) * P],
                                          big[:, hp, s, b * P:(b + 1) * P], ident[:, :])
                mm.then_inc(sem("nat_full"), 1)

            def products(hp, h):
                X, Y, Z = bank3(hp)
                pe.wait_ge(*((sem("nat_done"), 2 * hp + 2) if h == 0 else (sem("a0_done"), 3 * hp + 3)))
                if h == 0 and hp >= 2:
                    pe.wait_ge(sem("pt_done"), hp - 1)
                r = half_rows(h)
                a, b, k = (big[r, hp, s, :] for s in range(3))
                rr = rT[r, hp, :]
                for n, (lhs, rhs) in enumerate(((a, b), (b, a), (b, rr), (k, a), (k, rr))):
                    for t in range(TT):
                        c = slice(t * P, (t + 1) * P)
                        at = ((n % 2) * 2 + t) * P
                        mm = pe.matmul((X, Y, Z)[n // 2][:, at:at + P], lhs[:, c], rhs[:, c], start=True, stop=True)
                mm.then_inc(sem(f"a{h}_full"), 1)

            def unit_cols(u, n=P):
                return slice(u * n, (u + 1) * n)

            def akv(hp):
                pe.wait_ge(sem("a1_done"), 3 * hp + 3)
                pe.wait_ge(*((sem("q_done"), hp - 1) if hp >= 2 else (sem("bonus_done"), 4)))
                p = hp % 2
                for u in range(UNITS):
                    mm = pe.matmul(banks[6 + p][:, unit_cols(u, HALF)], MM[p][:, 3, u, :], Nat[p][:, 3, u, :],
                                   start=True, stop=True)
                mm.then_inc(sem("akv_full"), 1)

            def z_product(l):
                def step(hp):
                    p = hp % 2
                    pe.wait_ge(*((sem("base_done"), hp + 1) if l == 0 else (sem("tt_done"), level(l - 1, hp))))
                    for u in range(UNITS):
                        mm = pe.matmul(bank3(hp)[0][:, unit_cols(u)], MM[p][:, 1, u, :], Tm[p][:, unit_cols(u)],
                                       start=True, stop=True)
                    mm.then_inc(sem("z_full"), 1)
                return step

            def t_product(l):
                def step(hp):
                    p = hp % 2
                    _, Y, Z = bank3(hp)
                    pe.wait_ge(sem("z_done"), level(l, hp))
                    for u in range(UNITS):
                        c = unit_cols(u)
                        mm = pe.matmul(Y[:, c], Zm[p][:, c], TmT[p][:, c], start=True, stop=True)
                    if l < NLEV - 1:
                        for u in range(UNITS):
                            c = unit_cols(u)
                            mm = pe.matmul(Z[:, c], TmT[p][:, c], Zm[p][:, c], start=True, stop=True)
                    mm.then_inc(sem("t_full"), 1)
                return step

            def solve(hp):
                p = hp % 2
                pe.wait_ge(sem("tt_done"), level(NLEV - 1, hp))
                pe.wait_ge(sem("akv_done"), hp + 1)
                for u in range(UNITS):
                    pe.matmul(banks[6 + p][:, unit_cols(u, HALF)], TmT[p][:, unit_cols(u)], Nat[p][:, 0, u, :],
                              start=True, stop=True)
                    mm = pe.matmul(banks[6 + p][:, 256 + u * HALF:256 + (u + 1) * HALF], TmT[p][:, unit_cols(u)],
                                   AkV[p][:, unit_cols(u, HALF)], start=True, stop=True)
                mm.then_inc(sem("m_full"), 1)

            def outputs(hp):
                p = hp % 2
                X, Y, _ = bank3(hp)
                pe.wait_ge(sem("m_done"), hp + 1)
                for u in range(UNITS):
                    t, h = divmod(u, 2)
                    r, c = half_rows(h), slice(t * P, (t + 1) * P)
                    pe.matmul(X[r, c], M12[p][:, 0, u, :], MM[p][:, 2, u, :], start=True, stop=True)
                    pe.matmul(Y[r, c], M12[p][:, 1, u, :], MM[p][:, 2, u, :], start=True, stop=False)
                    mm = pe.matmul(Y[r, c], Nat[p][:, 3, u, :], MM[p][:, 4, u, :], start=False, stop=True)
                mm.then_inc(sem("ry_full"), 1)

            def transitions(hp):
                p = hp % 2
                Z, Q = bank3(hp)[2], banks[6 + p]
                pe.wait_ge(sem("expanded"), 2 * hp + 2)
                pe.wait_ge(sem("m2_expanded"), hp + 1)
                for u in range(UNITS):
                    t, h = divmod(u, 2)
                    r, c = half_rows(h), slice(t * 256, (t + 1) * 256)
                    x = slice(u * 256, (u + 1) * 256)
                    pe.matmul(Z[r, c], M12[p][:, 0, u, :], BX[p][:, x], start=True, stop=True)
                    pe.matmul(Q[r, c], Nat[p][:, 1, u, :], M2X[p][:, x], start=True, stop=False)
                    mm = pe.matmul(Q[r, c], Nat[p][:, 2, u, :], VX[p][:, x], start=False, stop=True)
                mm.then_inc(sem("pq_full"), 1)

            levels = [f(l) for l in range(NLEV) for f in (z_product, t_product)]
            by_pairs([natural, lambda hp: products(hp, 0), lambda hp: products(hp, 1), akv, *levels, solve,
                      outputs, transitions])
            pe.wait_ge(sem("q_done"), DC)
            pe.wait_ge(sem("y0_done"), DC)
            for c in range(1, NCH - 1):
                for q in range(2):
                    if c > 1:
                        pe.wait_ge(sem("state_done"), 8 * (2 * (c - 2) + q + 1))
                    for i in range(4):
                        hp = 4 * q + i
                        for h in range(2):
                            r = half_rows(h)
                            mm = pe.matmul(banks[2 * q + h][r, i * HALF:(i + 1) * HALF], PT_all[r, hp, 0, c, :],
                                           PT_all[r, hp, 1, c - 1, :], start=True, stop=True)
                    mm.then_inc(sem("state_full"), 1)
            pe.wait_ge(sem("state_done"), 16 * (NCH - 2))
            for q in range(4):
                if q >= 3:
                    pe.wait_ge(sem("y_done"), 2 * (q - 2))
                for h in range(2):
                    for hp in (2 * q, 2 * q + 1):
                        for c in range(1, NCH):
                            r = half_rows(h)
                            at = (hp % 2) * T + c * CH
                            mm = pe.matmul(banks[2 * (q % 3) + h][r, at:at + CH], PT_all[r, hp, 1, c - 1, :],
                                           rT[r, hp, c * CH:(c + 1) * CH], start=True, stop=True)
                mm.then_inc(sem("y_full"), 1)
            for q in range(4):
                pe.wait_ge(sem("y_done"), 2 * q + 2)
                pe.matmul(banks[MEAN_BANK[q]][:, :], mean_head[:, :], y0T[:, 2 * q:2 * q + 2, :], start=True,
                          stop=True).then_inc(sem("y_mean"), 1)
            for q in range(4):
                if q >= 2:
                    pe.wait_ge(sem("centred"), q - 1)
                pe.wait_ge(sem("y_squares"), q + 1)
                pe.matmul(banks[4 + q][:, :], mean_head[:, :], slot_view(9, DC, T)[:, 2 * q:2 * q + 2, :], start=True,
                          stop=True).then_inc(sem("y_var"), 1)
            for m in range(4):
                project(pe, (L, "o", m), (x_high, x_low),
                        (lambda c: pe.wait_ge(sem("y_split"), c // 2 + 1)) if m == 0 else None)

        def rwkv_act(act, L):
            key = (L, "lora1", 0)
            wait_full(act, key)
            act.activation(hidden[0:HALF, 0:T], bank_of(key)[0:HALF, 0:T], ACT.Tanh).then_inc(sem("lora_ready"), 1)
            act.activation(hidden[HALF:P, 0:T], bank_of(key)[HALF:P, 0:T], ACT.Copy).then_inc(sem("lora_ready"), 1)
            act.activation(hidden[:, T:2 * T], bank_of(key)[:, T:2 * T], ACT.Sigmoid).then_inc(sem("lora_ready"), 1)
            for s, dst, b0 in (("w", sg, "rwkv_w0"), ("a", aT, "rwkv_a0")):
                for i in range(4):
                    key = (L, s, i)
                    wait_full(act, key)
                    for b in range(2):
                        act.activation(dst[:, 2 * i + b, :], bank_of(key)[:, b * T:(b + 1) * T], ACT.Sigmoid,
                                       bias=col(b0, 2 * i + b)).then_inc(sem("wa_ready"), 1)
            for i in range(4):
                key = (L, "g", i)
                wait_full(act, key)
                act.activation(gT[:, 2 * i:2 * i + 2, :].rearrange("p a b -> p (a b)"), bank_of(key)[:, :],
                               ACT.Copy).then_inc(sem("g_ready"), 1)
            act.wait_ge(sem("csum_done"), 2)
            for dst, src, scale in ((e_prev, e_prev, 1.0), (e_in, csum, 1.0), (e_neg, csum, -1.0)):
                act.activation(dst[:, :, :], src[:, :, :], ACT.Exp, scale=scale).then_inc(sem("exps_done"), 1)

            def copy_out(s, i):
                wait_full(act, (L, s, i))
                dst = big[:, 2 * i:2 * i + 2, 3, :] if s == "v" else (rT if s == "r" else kraw)[:, 2 * i:2 * i + 2, :]
                act.activation(dst, bank_of((L, s, i))[:, :].rearrange("p (a b) -> p a b", a=2),
                               ACT.Copy).then_inc(sem("rkv_ready"), 1)

            for i in range(4):
                copy_out("k", i)
            for m in range(4):
                act.wait_ge(sem("kk_raw"), 2 * m + 2)
                act.activation(kk_sq[:, 2 * m:2 * m + 2, :], kk[:, 2 * m:2 * m + 2, :],
                               ACT.Square).then_inc(sem("kk_squares"), 1)
            copy_out("r", 0)
            for m in range(4):
                act.wait_ge(sem("kk_sum"), m + 1)
                act.activation(inv[:, 2 * m:2 * m + 2, :].rearrange("p a b -> p (a b)"), banks[6 + m % 2][:, :],
                               ACT.Sqrt).then_inc(sem("kk_root"), 1)
            for i in range(1, 4):
                copy_out("r", i)
            for i in range(4):
                copy_out("v", i)

            def nat_copy(hp):
                p = hp % 2
                act.wait_ge(sem("nat_full"), hp + 1)
                for i in range(2):
                    act.activation(Nat[p][:, 2 * i:2 * i + 2, :, :].rearrange("p a b c -> p (a b c)"),
                                   banks[3 * p + i][:, :], ACT.Copy).then_inc(sem("nat_done"), 1)

            def akv_copy(hp):
                p = hp % 2
                act.wait_ge(sem("akv_full"), hp + 1)
                act.activation(AkV[p], banks[6 + p][:, 0:256], ACT.Copy).then_inc(sem("akv_done"), 1)

            def m_copy(hp):
                p = hp % 2
                act.wait_ge(sem("m_full"), hp + 1)
                act.activation(M12[p][:, :, :, :].rearrange("p a b c -> p (a b c)"), banks[6 + p][:, :],
                               ACT.Copy).then_inc(sem("m_done"), 1)

            def y0_copy(hp):
                p = hp % 2
                act.wait_ge(sem("ry_full"), hp + 1)
                act.activation(y0T[:, hp, :], banks[3 * p + 1][:, 0:T], ACT.Copy).then_inc(sem("y0_done"), 1)

            by_pairs([nat_copy, akv_copy, m_copy, y0_copy])
            act.wait_ge(sem("pq_full"), DC)
            for i in range(NSPLIT):
                round_weights(act, (L, "o", i))
            yc, y_sq, root = (slot_view(i, DC, T) for i in (8, 9, 10))

            def y_square(q):
                act.wait_ge(sem("centred"), q + 1)
                act.activation(y_sq[:, 2 * q:2 * q + 2, :], yc[:, 2 * q:2 * q + 2, :],
                               ACT.Square).then_inc(sem("y_squares"), 1)

            for q in range(4):
                y_square(q)
            for q in range(4):
                act.wait_ge(sem("y_var"), q + 1)
                act.activation(root[:, 2 * q:2 * q + 2, :].rearrange("p a b -> p (a b)"), banks[4 + q][:, :],
                               ACT.Sqrt, bias=eps[:, 1:2]).then_inc(sem("y_root"), 1)
            for q in range(4):
                pair = slice(2 * q, 2 * q + 2)
                act.wait_ge(sem("gated"), q + 1)
                act.activation(x_high[:, pair, :], y_gated[:, pair, :], ACT.Copy).then_inc(sem("y_rounded"), 1)
            for m in range(4):
                ahead(round_weights, act, (L, "o", m))

        def rwkv_pool(pool, L):
            def expand(hp):
                p = hp % 2
                pool.wait_ge(sem("nat_done"), 2 * hp + 2)
                if hp >= 2:
                    pool.wait_ge(sem("pq_full"), hp - 1)
                mask = chunk_cols[:, :].unsqueeze(1).unsqueeze(3).to_broadcast([P, UNITS, 4, HALF])
                for dst, src in ((BX[p], Nat[p][:, 1]), (VX[p], Nat[p][:, 3])):
                    pool.tensor_tensor(dst.rearrange("p (u c d) -> p u c d", u=UNITS, c=4),
                                       src.unsqueeze(2).to_broadcast([P, UNITS, 4, HALF]), mask,
                                       ALU.mult).then_inc(sem("expanded"), 1)

            by_pairs([expand])
            for i in range(NSPLIT):
                rest_of_weights(pool, (L, "o", i), 1)
            for m in range(4):
                ahead(rest_of_weights, pool, (L, "o", m), 1)

        def rwkv_dve(dve, L):
            step = vector_step
            n = norm_index(L, 0)

            def then(ins):
                dve.wait_ge(step.sem, step.mark(ins))

            wait_h(dve, n)
            dve.tensor_tensor(dh[:, :, 1:T], hT[:, :, 0:T - 1], hT[:, :, 1:T], ALU.subtract).then_inc(step.sem, 1)
            step.n += 1
            then(dve.tensor_scalar(dh[:, :, 0:1], hT[:, :, 0:1], -1.0, None, ALU.mult))
            for s in MIXES:
                for c in range(DC):
                    dve.scalar_tensor_tensor(out=mixed[s][:, c, :], in0=dh[:, c, :],
                                             scalar=col("rwkv_mu", "rkvwag".index(s) * DC + c),
                                             in1=hT[:, c, :], op0=ALU.mult, op1=ALU.add).then_inc(sem("mixed"), 1)
            dve.wait_ge(sem("mixed"), 6 * DC)
            dve.wait_ge(sem("wa_ready"), 8)
            then(dve.tensor_scalar(sg[:, :, :], sg[:, :, :], -float(np.exp(-0.5)), None, ALU.mult))
            for c in range(DC):
                ins = dve.tensor_tensor_scan(csum[:, c, :], chunk_reset[:, :], sg[:, c, :], 0.0, ALU.mult, ALU.add)
                if c < DC - 1:
                    ins.then_inc(step.sem, 1)
                    step.n += 1
            ins.then_inc(sem("csum_done"), 1)
            dve.wait_ge(sem("csum_done"), 1)
            dve.tensor_tensor(e_prev[:, :, :], csum[:, :, :], sg[:, :, :], ALU.subtract).then_inc(sem("csum_done"), 1)
            dve.wait_ge(sem("wa_ready"), 16)
            dve.wait_ge(sem("csum_done"), 2)
            for c in range(DC):
                dve.tensor_scalar(sg[:, c, :], aT[:, c, :], -1.0, col("rwkv_k_a", c), ALU.add,
                                  ALU.mult).then_inc(step.sem, 1)
                step.n += 1
            dve.wait_ge(step.sem, step.n)
            dve.wait_ge(sem("rkv_ready"), 4)
            for c in range(DC):
                dve.tensor_scalar(kk[:, c, :], kraw[:, c, :], col("rwkv_k_k", c), None,
                                  ALU.mult).then_inc(sem("kk_raw"), 1)
            dve.wait_ge(sem("kk_raw"), DC)
            then(dve.scalar_tensor_tensor(out=kraw[:, :, :].rearrange("p a b -> p (a b)"),
                                          in0=sg[:, :, :].rearrange("p a b -> p (a b)"), scalar=1.0,
                                          in1=kraw[:, :, :].rearrange("p a b -> p (a b)"), op0=ALU.add, op1=ALU.mult))
            for m in range(4):
                dve.wait_ge(sem("kk_root"), m + 1)
                pair = slice(2 * m, 2 * m + 2)
                then(dve.tensor_scalar(inv[:, pair, :], inv[:, pair, :], 1e-12, None, ALU.max))
                then(dve.reciprocal(inv[:, pair, :], inv[:, pair, :]))
                then(dve.tensor_tensor(kk[:, pair, :], kk[:, pair, :], inv[:, pair, :], ALU.mult))
            then(dve.tensor_tensor(aT[:, :, :], kk[:, :, :], aT[:, :, :], ALU.mult))
            dve.wait_ge(sem("exps_done"), 3)
            dve.scalar_tensor_tensor(out=big[:, :, 0, :], in0=kk[:, :, :], scalar=-1.0, in1=e_prev[:, :, :],
                                     op0=ALU.mult, op1=ALU.mult).then_inc(sem("factors_done"), 1)
            for dst, x, y in ((big[:, :, 1, :], aT, e_neg), (big[:, :, 2, :], kraw, e_neg)):
                dve.tensor_tensor(dst, x[:, :, :], y[:, :, :], ALU.mult).then_inc(sem("factors_done"), 1)
            then(dve.tensor_copy(chunk_decay[:, :, :],
                                 e_in[:, :, :].rearrange("p h (c s) -> p h c s", s=CH)[:, :, :, CH - 1]))
            for c in range(DC):
                if c % 2 == 0:
                    dve.wait_ge(sem("rkv_ready"), 4 + c // 2 + 1)
                dve.scalar_tensor_tensor(out=rk[:, c, :], in0=rT[:, c, :], scalar=col("rwkv_r_k", c), in1=kraw[:, c, :],
                                         op0=ALU.mult, op1=ALU.mult).then_inc(sem("rk_done"), 1)
            dve.wait_ge(sem("rk_done"), DC)
            dve.tensor_tensor(rT[:, :, :], rT[:, :, :], e_in[:, :, :], ALU.mult).then_inc(sem("factors_done"), 1)
            dve.wait_ge(sem("factors_done"), 1)
            for m in range(4):
                dve.wait_ge(sem("rk_sum"), m + 1)
                dve.wait_ge(sem("rkv_ready"), 8 + m + 1)
                dve.tensor_tensor(bonus[:, 2 * m:2 * m + 2, :],
                                  banks[6 + m % 2][:, :].rearrange("p (a b) -> p a b", a=2),
                                  big[:, 2 * m:2 * m + 2, 3, :], ALU.mult).then_inc(sem("bonus_done"), 1)

            def mask_products(h):
                def run(hp):
                    p = hp % 2
                    dve.wait_ge(sem(f"a{h}_full"), hp + 1)
                    for i, (s, m, k) in enumerate(((0, 0, 2), (2, 2, 2), (4, 2, 1))):
                        dve.tensor_tensor(
                            MM[p][:, s:s + k].rearrange("p s (t h) n -> p s t h n", h=2)[:, :, :, h, :],
                            banks[3 * p + i][:, 0:k * 256].rearrange("p (s t n) -> p s t n", s=k, t=TT),
                            masks[:, m:m + k, :].unsqueeze(2).to_broadcast([P, k, TT, P]),
                            ALU.mult).then_inc(sem(f"a{h}_done"), 1)
                return run

            def four(x):
                return x.rearrange("p (u n) -> p u n", u=UNITS)

            def everywhere(m):
                return m.unsqueeze(1).to_broadcast([P, UNITS, P])

            def base(hp):
                p = hp % 2
                dve.wait_ge(sem("a1_done"), 3 * hp + 3)
                for dst, s, m in ((Tm[p], 0, 0), (TmT[p], 1, 1)):
                    then(dve.tensor_tensor(four(dst), MM[p][:, s], everywhere(pair_masks[:, m, :]), ALU.mult))
                then(dve.tensor_tensor(four(Tm[p]), four(Tm[p]), everywhere(ident[:, :]), ALU.add))
                dve.tensor_tensor(four(TmT[p]), four(TmT[p]), everywhere(ident[:, :]),
                                  ALU.add).then_inc(sem("base_done"), 1)

            def z_mask(l):
                def run(hp):
                    p = hp % 2
                    dve.wait_ge(sem("z_full"), level(l, hp))
                    dve.tensor_tensor(four(Zm[p]), four(banks[3 * p][:, :]), everywhere(pair_masks[:, 2 + l, :]),
                                      ALU.mult).then_inc(sem("z_done"), 1)
                return run

            def t_add(l):
                def run(hp):
                    p = hp % 2
                    dve.wait_ge(sem("t_full"), level(l, hp))
                    if l < NLEV - 1:
                        dve.tensor_tensor(Tm[p], Tm[p], banks[3 * p + 2][:, :], ALU.add).then_inc(step.sem, 1)
                        step.n += 1
                    dve.tensor_tensor(TmT[p], TmT[p], banks[3 * p + 1][:, :], ALU.add).then_inc(sem("tt_done"), 1)
                return run

            def expand_m2(hp):
                p = hp % 2
                dve.wait_ge(sem("m_done"), hp + 1)
                if hp >= 2:
                    dve.wait_ge(sem("pq_full"), hp - 1)
                dve.tensor_tensor(M2X[p].rearrange("p (u c d) -> p u c d", u=UNITS, c=4),
                                  M12[p][:, 1].unsqueeze(2).to_broadcast([P, UNITS, 4, HALF]),
                                  chunk_cols[:, :].unsqueeze(1).unsqueeze(3).to_broadcast([P, UNITS, 4, HALF]),
                                  ALU.mult).then_inc(sem("m2_expanded"), 1)

            def r1(hp):
                p = hp % 2
                dve.wait_ge(sem("ry_full"), hp + 1)
                dve.tensor_tensor(rT[:, hp, :], rT[:, hp, :], banks[3 * p][:, 0:T], ALU.add).then_inc(sem("r1_done"), 1)

            def chunks(hp):
                p = hp % 2
                dve.wait_ge(sem("pq_full"), hp + 1)
                dve.tensor_tensor(PT_all[:, hp, 0], banks[3 * p + 2][:, :].rearrange("p (c j) -> p c j", j=HALF),
                                  head_eye[:, :].unsqueeze(1).to_broadcast([P, NCH, HALF]),
                                  ALU.add).then_inc(sem("pt_done"), 1)
                dve.tensor_tensor(PT_all[:, hp, 1], banks[6 + p][:, :].rearrange("p (c j) -> p c j", j=HALF),
                                  chunk_decay[:, hp, :].unsqueeze(2).to_broadcast([P, NCH, HALF]),
                                  ALU.mult).then_inc(sem("q_done"), 1)

            levels = [f(l) for l in range(NLEV) for f in (z_mask, t_add)]
            by_pairs([mask_products(0), mask_products(1), base, *levels, expand_m2, r1, chunks])
            dve.wait_ge(sem("q_done"), DC)
            for c in range(1, NCH - 1):
                for q in range(2):
                    dve.wait_ge(sem("state_full"), 2 * (c - 1) + q + 1)
                    for i in range(4):
                        hp = 4 * q + i
                        for h in range(2):
                            r = half_rows(h)
                            dve.scalar_tensor_tensor(out=PT_all[r, hp, 1, c, :],
                                                     in0=banks[2 * q + h][r, i * HALF:(i + 1) * HALF],
                                                     scalar=chunk_decay[r, hp, c:c + 1], in1=PT_all[r, hp, 1, c, :],
                                                     op0=ALU.mult, op1=ALU.add).then_inc(sem("state_done"), 1)
            yc, root = slot_view(8, DC, T), slot_view(10, DC, T)
            for i in range(NSPLIT):
                rest_of_weights(dve, (L, "o", i), 0)
            for q in range(4):
                dve.wait_ge(sem("y_full"), q + 1)
                if q == 0:
                    dve.wait_ge(sem("y0_done"), DC)
                for h in range(2):
                    r = half_rows(h)
                    y = y0T[r, 2 * q:2 * q + 2, CH:T]
                    dve.tensor_tensor(y, y, banks[2 * (q % 3) + h][r, :].rearrange("p (a b) -> p a b", a=2)[:, :, CH:T],
                                      ALU.add).then_inc(sem("y_done"), 1)

            def low_part(q):
                pair = slice(2 * q, 2 * q + 2)
                dve.wait_ge(sem("y_rounded"), q + 1)
                dve.tensor_tensor(x_low[:, pair, :], y_gated[:, pair, :], x_high[:, pair, :].bitcast(F32),
                                  ALU.subtract).then_inc(sem("y_split"), 1)

            for q in range(4):
                pair = slice(2 * q, 2 * q + 2)
                dve.wait_ge(sem("y_mean"), q + 1)
                dve.tensor_tensor(yc[:, pair, :], y0T[:, pair, :],
                                  banks[MEAN_BANK[q]][:, :].rearrange("p (a b) -> p a b", a=2),
                                  ALU.subtract).then_inc(sem("centred"), 1)
            for q in range(4):
                pair = slice(2 * q, 2 * q + 2)
                dve.wait_ge(sem("y_root"), q + 1)
                then(dve.reciprocal(root[:, pair, :], root[:, pair, :]))
                then(dve.tensor_tensor(yc[:, pair, :], yc[:, pair, :], root[:, pair, :], ALU.mult))
                for c in (2 * q, 2 * q + 1):
                    dve.tensor_scalar(yc[:, c, :], yc[:, c, :], col("rwkv_ln_g", c), col("rwkv_ln_b", c), ALU.mult,
                                      ALU.add).then_inc(step.sem, 1)
                    step.n += 1
                dve.wait_ge(step.sem, step.n)
                then(dve.tensor_tensor(yc[:, pair, :], yc[:, pair, :], bonus[:, pair, :], ALU.add))
                dve.tensor_tensor(y_gated[:, pair, :], yc[:, pair, :], gT[:, pair, :], ALU.mult).then_inc(sem("gated"), 1)
                if q:
                    low_part(q - 1)
            low_part(3)
            add_residual(dve, L, "o")

        NCOL = S5_G * S5_N
        GW = S5_L * S5_C
        FB, GC = flat[:, 0:8192], flat[:, 8192:16384]
        tok = flat[0:S5_N, 16384:24576]
        h_tok = tok.rearrange("p (g s c) -> p g s c", g=S5_G, s=S5_L)
        y_tok = tok.rearrange("p (s d) -> p s d", s=S5_L)
        u_all = work[:, 12, :]
        c_rows = work[:, 12, :].rearrange("p (v b q) -> p v b q", v=2, b=DC)
        V_all = work[:, 18, :]
        coef = work[:, 13, :].rearrange("p (v k g) -> p v k g", v=4, k=S5_L)
        b_raw = work[:, 14, :].rearrange("p (v g c) -> p v g c", v=2, c=S5_C)
        c_raw = work[:, 15, :].rearrange("p (v g c) -> p v g c", v=2, c=S5_C)
        fill_tmp = [work[:, 17, i * 1024:(i + 1) * 1024] for i in (0, 1)]
        FT = [work[:, 19, i * 512:(i + 1) * 512] for i in (0, 1)]
        TZ = [work[:, 19, i * 512:(i + 1) * 512] for i in (2, 3)]
        cos_n, sin_n, turned, decay8 = (work[:, i, :] for i in (14, 0, 1, 17))
        Z_all = work[:, 3, :]
        a_rows = work[0:S5_G, 6, 0:256].rearrange("p (v q) -> p v q", v=2)
        as_rows = work[0:S5_G, 6, 256:512].rearrange("p (v q) -> p v q", v=2)
        step_col = work[0:S5_G, 6, 512:513]
        y_s5 = slot_view(0, DC, T)
        glu_gate = work[:, 4, :].rearrange("p (i t) -> p i t", t=T)
        glu_out = work[:, 5, 0:1024].rearrange("p (i t) -> p i t", t=T)

        def small(i, n=1):
            return work[:, 7, i * S5_G:(i + n) * S5_G]

        def table(i, n):
            return small(i, n).rearrange("p (k g) -> p k g", g=S5_G)

        A_RE, A_IM, AS_RE, TH = 0, 1, 2, 3
        TURNS, ANGLE, CO_ARG, DEN, B_RE, B_IM, TMP = 4, 5, 6, 7, 8, 9, 10
        U_RE, U_IM, GROW = 12, 20, 28

        def send_s5(sp, L):
            for i in range(8):
                send_plain(sp, (L, "glu", i), A["s5_w_glu"][0], (i % 2) * D + (i // 2) * TILE)

        def s5_load(pool, L):
            if layers.index(L):
                pool.wait_ge(sem("x_ready"), updates(L) - 4)
            for v, (re, im) in enumerate((("re", "im"), ("im", "re"))):
                for half, part in enumerate((re, im)):
                    r = half_rows(half)
                    pool.dma_start(b_raw[r, v], A[f"s5_b_{part}"][0].rearrange("g p c -> p g c")).then_inc(sem("s5_in"), 16)
                    pool.dma_start(c_rows[:, v, :, half * HALF:(half + 1) * HALF],
                                   A[f"s5_c_{part}"][0].rearrange("(b g) c p -> (g c) b p", g=DC)).then_inc(sem("s5_in"), 16)
            for v, part in enumerate(("re", "im")):
                for half in range(2):
                    pool.dma_start(a_rows[:, v, half * HALF:(half + 1) * HALF], A[f"s5_a_{part}"][0]).then_inc(sem("s5_in"), 16)
            pool.dma_start(step_col, A["s5_log_step"].rearrange("a g -> g a")).then_inc(sem("s5_in"), 16)

        def s5_pool(pool, L):
            pool.wait_ge(sem("coef_done"), 2)
            pool.wait_ge(sem("c_ready"), 4)
            chain = pool_step
            for q in range(4):
                if q:
                    pool.wait_ge(sem("gc_done"), q)
                fill_quarter(pool, chain, q, GC, c_raw, 2, fill_tmp[1], "gc_done")
            for i in range(NSPLIT):
                rest_of_weights(pool, (L, "glu", i), 1)
            for i in range(8):
                ahead(rest_of_weights, pool, (L, "glu", i), 1)

        def fill_quarter(eng, chain, q, dst, raw, v, tmp, done):
            n = S5_G // 8

            def spread(x):
                return x.unsqueeze(2).to_broadcast([P, n, S5_L, S5_C])

            def along(x):
                return x.rearrange("p k g -> p g k").unsqueeze(3).to_broadcast([P, n, S5_L, S5_C])

            for h in range(2 * q, 2 * q + 2):
                g = slice(h * n, (h + 1) * n)
                out_ = dst[:, h * 1024:(h + 1) * 1024].rearrange("p (g k c) -> p g k c", g=n, k=S5_L)
                t = tmp.rearrange("p (g k c) -> p g k c", g=n, k=S5_L)
                chain.mark(eng.tensor_tensor(out_, spread(raw[:, 0, g]), along(coef[:, v, :, g]), ALU.mult))
                chain.mark(eng.tensor_tensor(t, spread(raw[:, 1, g]), along(coef[:, v + 1, :, g]), ALU.mult))
                eng.wait_ge(chain.sem, chain.n)
                ins = eng.tensor_tensor(out_, out_, t, ALU.subtract)
                if h % 2 == 0:
                    eng.wait_ge(chain.sem, chain.mark(ins))
            ins.then_inc(sem(done), 1)

        def s5_exponentials(act, part):
            if part == 0:
                act.wait_ge(sem("s5_in"), 16 * 13)
                act.activation(step_col, step_col, ACT.Exp).then_inc(sem("step_exp"), 1)
            if part == 4:
                act.wait_ge(sem("as_ready"), 1)
                for k in range(S5_L):
                    for v, s in ((0, -1.0), (1, 1.0)):
                        act.activation(coef[:, 2 * v, k, :], small(AS_RE), ACT.Exp,
                                       scale=s * (k + 1)).then_inc(sem("mag_done"), 1)
                act.wait_ge(sem("angle_done"), 1)
                act.activation(small(CO_ARG), small(ANGLE), ACT.Abs).then_inc(sem("abs_done"), 1)
                act.activation(small(U_IM), small(ANGLE), ACT.Sin).then_inc(sem("sin_done"), 1)
                act.wait_ge(sem("abs_done"), 1)
                act.activation(small(U_RE), small(CO_ARG), ACT.Sin, bias=half_pi[:, 0:1],
                               scale=-1.0).then_inc(sem("sin_done"), 1)

        def s5_act(act, L):
            if layers.index(L) == 0:
                for part in range(12):
                    s5_exponentials(act, part)
            for i in range(4):
                act.wait_ge(sem("c_full"), i + 1)
                v, b = divmod(i, 2)
                dst = c_raw[:, v, b * 32:(b + 1) * 32, :].rearrange("p g c -> p (g c)")
                act.activation(dst, banks[i][:, :], ACT.Copy,
                               scale=sign[:, 0:1] if v == 0 else 1.0).then_inc(sem("c_ready"), 1)
            for i in range(16):
                act.wait_ge(sem("h_full"), i + 1)
                act.activation(h_tok[:, 32 * (i % 2):32 * (i % 2) + 32, i // 2, :],
                               banks[i % 4][0:S5_N, :].rearrange("p (g c) -> p g c", c=S5_C), ACT.Copy).then_inc(sem("htok_done"), 1)
            for i in range(4):
                act.wait_ge(sem("u_full"), i + 1)
                act.activation(u_all[:, i * 512:(i + 1) * 512], banks[i][:, :], ACT.Copy).then_inc(sem("u_done"), 1)
            for i in range(16):
                act.wait_ge(sem("ft_full"), i + 1)
                if i >= 2:
                    act.wait_ge(sem("vy_full"), i - 1)
                act.activation(FT[i % 2], banks[i % 2][:, :], ACT.Copy).then_inc(sem("ft_done"), 1)
                if i:
                    pass_one_copies(act, L, i - 1)
            pass_one_copies(act, L, 15)
            act.wait_ge(sem("z_ready"), 1)
            round_weights(act, (L, "glu", 0))
            act.wait_ge(sem("yx_full"), 16)
            round_weights(act, (L, "glu", 1))
            for m in range(4):
                act.wait_ge(sem("ys5_done"), 2 * m + 2)
                pair = y_s5[:, 2 * m:2 * m + 2, :]
                act.activation(pair, pair, ACT.Gelu_apprx_tanh).then_inc(sem("gelu_done"), 1)
                act.wait_ge(sem("gelu_done"), m + 1)
                act.activation(x_high[:, 2 * m:2 * m + 2, :], pair, ACT.Copy).then_inc(sem("gelu_rounded"), 1)
            for m in range(4):
                for i in (2 * m, 2 * m + 1):
                    ahead(round_weights, act, (L, "glu", i))
                wait_full(act, (L, "glu", 2 * m + 1))
                for b in range(2):
                    c = 2 * m + b
                    act.activation(glu_gate[:, c, :], bank_of((L, "glu", 2 * m + 1))[:, b * T:(b + 1) * T], ACT.Sigmoid,
                                   bias=col("s5_b_glu", DC + c)).then_inc(sem("glu_gate"), 1)

        def pass_one_copies(act, L, i):
            act.wait_ge(sem("vy_full"), i + 1)
            act.activation(V_all[:, i * P:(i + 1) * P], banks[4 + i % 2][:, 0:P], ACT.Copy).then_inc(sem("v_done"), 1)
            act.activation(y_tok.rearrange("p s (g c) -> p g s c", c=S5_C)[:, 4 * i:4 * i + 4],
                           banks[6 + i % 2][0:S5_N, :].rearrange("p (g s c) -> p g s c", g=4, s=S5_L),
                           ACT.Copy).then_inc(sem("v_done"), 1)

        def s5_turn_a(pe):
            pe.wait_ge(sem("s5_in"), 16 * 13)
            pe.wait_ge(sem("a_scaled"), 2)
            for i, src in enumerate((a_rows[:, 0], a_rows[:, 1], as_rows[:, 0], as_rows[:, 1])):
                mm = pe.transpose(banks[6][:, i * S5_G:(i + 1) * S5_G], src, ident[0:S5_G, 0:S5_G])
            mm.then_inc(sem("as_full"), 1)

        def s5_turn_c(pe):
            pe.wait_ge(sem("s5_in"), 16 * 13)
            for i in range(4):
                v, b = divmod(i, 2)
                for j in range(4):
                    mm = pe.transpose(banks[i][:, j * P:(j + 1) * P], c_rows[:, v, 4 * b + j, :], ident[:, :])
                mm.then_inc(sem("c_full"), 1)

        def s5_pe(pe, L):
            if layers.index(L) == 0:
                s5_turn_a(pe)
                s5_turn_c(pe)
            wait_h(pe, norm_index(L, 0))
            for i in range(16):
                pe.wait_ge(*((sem("c_ready"), i + 1) if i < 4 else (sem("htok_done"), i - 3)))
                for j in range(4):
                    x = hT[:, 4 * (i % 2) + j, :].rearrange("p (n s) -> p s n", s=S5_L)[:, i // 2, :]
                    mm = pe.transpose(banks[i % 4][0:S5_N, j * P:(j + 1) * P], x, ident[:, :])
                mm.then_inc(sem("h_full"), 1)
            for i in range(4):
                pe.wait_ge(sem("htok_done"), 16)
                for j in range(16):
                    g = 16 * i + j
                    x = h_tok[:, g].rearrange("p s c -> p (s c)")
                    mm = pe.transpose(banks[i][:, j * S5_N:(j + 1) * S5_N], x, ident[0:S5_N, 0:S5_N])
                mm.then_inc(sem("u_full"), 1)

            def tables(i):
                if i % 4 == 0:
                    pe.wait_ge(sem("fb_done"), i // 4 + 1)
                    pe.wait_ge(sem("gc_done"), i // 4 + 1)
                if i < 2:
                    pe.wait_ge(sem("u_done"), 4)
                else:
                    pe.wait_ge(sem("ft_done"), i - 1)
                    pe.wait_ge(sem("toeplitz"), i - 1)
                for j in range(4):
                    g = slice((4 * i + j) * GW, (4 * i + j + 1) * GW)
                    pe.transpose(banks[i % 2][:, j * P:(j + 1) * P], FB[:, g], ident[:, :])
                    mm = pe.matmul(banks[2 + i % 2][:, j * P:(j + 1) * P], FB[:, g], GC[:, g], start=True, stop=True)
                mm.then_inc(sem("ft_full"), 1)

            def apply(i):
                pe.wait_ge(sem("ft_done"), i + 1)
                pe.wait_ge(sem("toeplitz"), i + 1)
                if i >= 2:
                    pe.wait_ge(sem("v_done"), 2 * (i - 1))
                for j in range(4):
                    u = u_all[:, (4 * i + j) * S5_N:(4 * i + j + 1) * S5_N]
                    c = slice(j * P, (j + 1) * P)
                    pe.matmul(banks[4 + i % 2][:, j * S5_N:(j + 1) * S5_N], FT[i % 2][:, c], u, start=True, stop=True)
                    mm = pe.matmul(banks[6 + i % 2][0:S5_N, c], u, TZ[i % 2][:, c], start=True, stop=True)
                mm.then_inc(sem("vy_full"), 1)

            tables(0)
            for i in range(16):
                if i < 15:
                    tables(i + 1)
                apply(i)
            pe.wait_ge(sem("v_done"), 32)
            for i in range(4):
                pe.matmul(banks[i][:, :], swap[:, :], V_all[:, i * 512:(i + 1) * 512], start=True,
                          stop=True).then_inc(sem("vs_full"), 1)
            pe.wait_ge(sem("z_ready"), 1)
            for i in range(4):
                pe.matmul(banks[4 + i][:, :], swap[:, :], Z_all[:, i * 512:(i + 1) * 512], start=True,
                          stop=True).then_inc(sem("zs_full"), 1)
            for i in range(16):
                pe.wait_ge(sem("x_state"), i // 4 + 1)
                if i >= 4:
                    pe.wait_ge(sem("y_added"), i - 3)
                for j in range(4):
                    g = 4 * i + j
                    mm = pe.matmul(banks[i % 4][0:S5_N, j * P:(j + 1) * P], V_all[:, g * S5_N:(g + 1) * S5_N],
                                   GC[:, g * GW:(g + 1) * GW], start=True, stop=True)
                mm.then_inc(sem("yx_full"), 1)
            pe.wait_ge(sem("y_added"), 16)
            for m in range(4):
                for b in range(2):
                    for s in range(S5_L):
                        at = b * T + s * S5_N
                        mm = pe.transpose(banks[4 + m][:, at:at + S5_N],
                                          y_tok[:, s, (2 * m + b) * P:(2 * m + b + 1) * P], ident[0:S5_N, 0:S5_N])
                mm.then_inc(sem("yt_full"), 1)
            pe.wait_ge(sem("ys5_done"), 8)
            for i in range(8):
                project(pe, (L, "glu", i), (x_high, x_low),
                        (lambda c: pe.wait_ge(sem("gelu_split"), c // 2 + 1)) if i == 0 else None)


        def s5_math(dve):
            step = vector_step

            def then(ins):
                dve.wait_ge(step.sem, step.mark(ins))

            def tt(out_, x, y, op):
                then(dve.tensor_tensor(out_, x, y, op))

            def ts(out_, x, a, b, op0, op1):
                then(dve.tensor_scalar(out_, x, a, b, op0, op1))

            def complex_product(re, im, a, b, t):
                tt(t, a[1], b[1], ALU.mult)
                tt(re, a[0], b[0], ALU.mult)
                tt(re, re, t, ALU.subtract)
                tt(t, a[1], b[0], ALU.mult)
                tt(im, a[0], b[1], ALU.mult)
                tt(im, im, t, ALU.add)

            return then, tt, ts, complex_product

        def s5_tables(dve, part):
            then, tt, ts, complex_product = s5_math(dve)
            if part == 0:
                dve.wait_ge(sem("s5_in"), 16 * 13)
                ts(b_raw[:, 1], b_raw[:, 1], sign[:, 0:1], None, ALU.mult, ALU.bypass)
                dve.wait_ge(sem("step_exp"), 1)
                for v in range(2):
                    dve.tensor_scalar(as_rows[:, v], a_rows[:, v], step_col, None, ALU.mult).then_inc(sem("a_scaled"), 1)
            if part == 3:
                dve.wait_ge(sem("as_full"), 1)
                dve.tensor_copy(small(0, 4), banks[6][:, 0:4 * S5_G]).then_inc(sem("as_ready"), 1)
                dve.wait_ge(sem("as_ready"), 1)
                big_ = 1.5 * 2.0 ** 23
                ts(small(TURNS), small(TH), 1.0 / TWO_PI, big_, ALU.mult, ALU.add)
                ts(small(TURNS), small(TURNS), -big_, None, ALU.add, ALU.bypass)
                turn_hi = 6.28125
                then(dve.scalar_tensor_tensor(out=small(ANGLE), in0=small(TURNS), scalar=-turn_hi, in1=small(TH),
                                              op0=ALU.mult, op1=ALU.add))
                then(dve.scalar_tensor_tensor(out=small(ANGLE), in0=small(TURNS), scalar=-(TWO_PI - turn_hi),
                                              in1=small(ANGLE), op0=ALU.mult, op1=ALU.add))
                dve.tensor_scalar(small(ANGLE), small(ANGLE), 3.1415925, -3.1415925, ALU.min,
                                  ALU.max).then_inc(sem("angle_done"), 1)
            if part == 4:
                tt(small(DEN), small(A_RE), small(A_RE), ALU.mult)
                tt(small(TMP), small(A_IM), small(A_IM), ALU.mult)
                tt(small(DEN), small(DEN), small(TMP), ALU.add)
                then(dve.reciprocal(small(DEN), small(DEN)))
            if part == 5:
                dve.wait_ge(sem("sin_done"), 2)
                have = 1
                while have < S5_L:
                    last = [table(x + have - 1, 1).to_broadcast([P, have, S5_G]) for x in (U_RE, U_IM)]
                    complex_product(table(U_RE + have, have), table(U_IM + have, have),
                                    (table(U_RE, have), table(U_IM, have)), last, table(GROW, have))
                    have *= 2
            if part == 7:
                dve.wait_ge(sem("mag_done"), 16)
                tt(small(B_RE), coef[:, 2, 0, :], small(U_RE), ALU.mult)
                ts(small(B_RE), small(B_RE), -1.0, None, ALU.add, ALU.bypass)
                tt(small(B_IM), coef[:, 2, 0, :], small(U_IM), ALU.mult)
                tt(small(TURNS), small(B_RE), small(A_RE), ALU.mult)
                tt(small(TMP), small(B_IM), small(A_IM), ALU.mult)
                tt(small(TURNS), small(TURNS), small(TMP), ALU.add)
                tt(small(B_IM), small(B_IM), small(A_RE), ALU.mult)
                tt(small(TMP), small(B_RE), small(A_IM), ALU.mult)
                tt(small(B_IM), small(B_IM), small(TMP), ALU.subtract)
                tt(small(B_RE), small(TURNS), small(DEN), ALU.mult)
                tt(small(B_IM), small(B_IM), small(DEN), ALU.mult)
            if part == 8:
                then(dve.tensor_copy(lam8[:, 0, :], coef[:, 2, S5_L - 1, :]))
                then(dve.tensor_copy(lam8[:, 1, :], small(U_RE + S5_L - 1)))
                then(dve.tensor_copy(lam8[:, 2, :], small(U_IM + S5_L - 1)))
                tt(coef[:, 3], coef[:, 2], table(U_IM, S5_L), ALU.mult)
                tt(coef[:, 2], coef[:, 2], table(U_RE, S5_L), ALU.mult)
            if part == 9:
                bre, bim = (table(x, 1).to_broadcast([P, S5_L, S5_G]) for x in (B_RE, B_IM))
                tt(coef[:, 1], table(U_RE, S5_L), bim, ALU.mult)
                half4 = S5_L // 2
                for k in (0, half4):
                    ks = slice(k, k + half4)
                    b4 = [table(x, 1).to_broadcast([P, half4, S5_G]) for x in (B_RE, B_IM)]
                    t = table(GROW, half4)
                    tt(t, table(U_IM + k, half4), b4[0], ALU.mult)
                    tt(coef[:, 1, ks], coef[:, 1, ks], t, ALU.subtract)
                    tt(t, table(U_IM + k, half4), b4[1], ALU.mult)
                    tt(table(U_RE + k, half4), table(U_RE + k, half4), b4[0], ALU.mult)
                    tt(table(U_RE + k, half4), table(U_RE + k, half4), t, ALU.add)
            if part == 11:
                dve.tensor_tensor(coef[:, 1], coef[:, 1], coef[:, 0], ALU.mult).then_inc(sem("coef_done"), 1)
                dve.wait_ge(sem("coef_done"), 1)
                dve.tensor_tensor(coef[:, 0], coef[:, 0], table(U_RE, S5_L), ALU.mult).then_inc(sem("coef_done"), 1)

        def s5_dve(dve, L):
            step = vector_step
            then, tt, ts, complex_product = s5_math(dve)
            if layers.index(L) == 0:
                for part in range(12):
                    s5_tables(dve, part)
            dve.wait_ge(sem("coef_done"), 2)

            def fill_fb(q):
                if q:
                    dve.wait_ge(sem("fb_done"), q)
                fill_quarter(dve, step, q, FB, b_raw, 0, fill_tmp[0], "fb_done")

            def toeplitz(first, last):
                for i in range(first, last):
                    dve.wait_ge(sem("ft_full"), i + 1)
                    if i >= 2:
                        dve.wait_ge(sem("vy_full"), i - 1)
                    dve.tensor_tensor(TZ[i % 2].rearrange("p (g n) -> p g n", g=4),
                                      banks[2 + i % 2][:, :].rearrange("p (g n) -> p g n", g=4),
                                      causal[:, :].unsqueeze(1).to_broadcast([P, 4, P]),
                                      ALU.mult).then_inc(sem("toeplitz"), 1)

            grid = [x.rearrange("p (g n) -> p g n", n=S5_N) for x in (cos_n, sin_n, turned)]

            def double(have):
                n = slice(have, 2 * have)
                factor = [x.unsqueeze(2).to_broadcast([P, S5_G, have]) for x in (lam8[:, 1, :], lam8[:, 2, :])]
                complex_product(grid[0][:, :, n], grid[1][:, :, n],
                                [x[:, :, 0:have] for x in grid[0:2]], factor, grid[2][:, :, 0:have])
                if 2 * have < S5_N:
                    t = [turned[:, i * S5_G:(i + 1) * S5_G] for i in range(3)]
                    complex_product(t[0], t[1], (lam8[:, 1, :], lam8[:, 2, :]), (lam8[:, 1, :], lam8[:, 2, :]), t[2])
                    then(dve.tensor_copy(lam8[:, 1, :], t[0]))
                    then(dve.tensor_copy(lam8[:, 2, :], t[1]))

            fill_fb(0)
            fill_fb(1)
            toeplitz(0, 2)
            fill_fb(2)
            toeplitz(2, 6)
            fill_fb(3)
            toeplitz(6, 9)
            dve.wait_ge(sem("fb_done"), 4)
            then(dve.memset(grid[0][:, :, 0:1], 1.0))
            then(dve.memset(grid[1][:, :, 0:1], 0.0))
            double(1)
            toeplitz(9, 11)
            double(2)
            toeplitz(11, 13)
            double(4)
            toeplitz(13, 15)
            double(8)
            toeplitz(15, 16)
            double(16)
            dve.wait_ge(sem("gc_done"), 4)
            d8 = decay8.rearrange("p (g n) -> p g n", n=S5_N)
            then(dve.tensor_copy(d8, lam8[:, 0, :].unsqueeze(2).to_broadcast([P, S5_G, S5_N])))
            then(dve.memset(d8[:, :, S5_N - 1:S5_N], 0.0))
            dve.wait_ge(sem("v_done"), 32)
            dve.wait_ge(sem("vs_full"), 4)
            for i in range(4):
                c = slice(i * 512, (i + 1) * 512)
                tt(turned[:, c], sin_n[:, c], banks[i][:, :], ALU.mult)
            tt(V_all, V_all, cos_n, ALU.mult)
            tt(V_all, V_all, turned, ALU.add)
            then(dve.memset(Z_all[:, 0:1], 0.0))
            dve.tensor_tensor_scan(Z_all[:, 1:NCOL], V_all[:, 0:NCOL - 1], decay8[:, 0:NCOL - 1], 0.0, ALU.add,
                                   ALU.mult).then_inc(sem("z_ready"), 1)
            dve.wait_ge(sem("z_ready"), 1)
            for i in range(4):
                c = slice(i * 512, (i + 1) * 512)
                dve.wait_ge(sem("zs_full"), i + 1)
                tt(turned[:, c], sin_n[:, c], banks[4 + i][:, :], ALU.mult)
                tt(V_all[:, c], Z_all[:, c], cos_n[:, c], ALU.mult)
                dve.tensor_tensor(V_all[:, c], V_all[:, c], turned[:, c], ALU.subtract).then_inc(sem("x_state"), 1)
            for i in range(16):
                dve.wait_ge(sem("yx_full"), i + 1)
                y = y_tok.rearrange("p s (g c) -> p g s c", c=S5_C)[:, 4 * i:4 * i + 4]
                dve.tensor_tensor(y, y, banks[i % 4][0:S5_N, :].rearrange("p (g s c) -> p g s c", g=4, s=S5_L),
                                  ALU.add).then_inc(sem("y_added"), 1)
            for i in range(NSPLIT):
                rest_of_weights(dve, (L, "glu", i), 0)
            for m in range(4):
                dve.wait_ge(sem("yt_full"), m + 1)
                for b in range(2):
                    c = 2 * m + b
                    dve.scalar_tensor_tensor(
                        out=y_s5[:, c, :].rearrange("p (n s) -> p n s", s=S5_L),
                        in0=hT[:, c, :].rearrange("p (n s) -> p n s", s=S5_L), scalar=col("s5_d", c),
                        in1=banks[4 + m][:, b * T:(b + 1) * T].rearrange("p (s n) -> p n s", s=S5_L),
                        op0=ALU.mult, op1=ALU.add).then_inc(sem("ys5_done"), 1)
            for m in range(4):
                pair = slice(2 * m, 2 * m + 2)
                dve.wait_ge(sem("gelu_rounded"), m + 1)
                dve.tensor_tensor(x_low[:, pair, :], y_s5[:, pair, :], x_high[:, pair, :].bitcast(F32),
                                  ALU.subtract).then_inc(sem("gelu_split"), 1)
            for m in range(4):
                for i in (2 * m, 2 * m + 1):
                    ahead(rest_of_weights, dve, (L, "glu", i), 0)
                wait_full(dve, (L, "glu", 2 * m))
                dve.wait_ge(sem("glu_gate"), 2 * m + 2)
                for b in range(2):
                    c = 2 * m + b
                    ins = dve.scalar_tensor_tensor(out=glu_out[:, 2 * (m % 2) + b, :],
                                                   in0=bank_of((L, "glu", 2 * m))[:, b * T:(b + 1) * T],
                                                   scalar=col("s5_b_glu", c), in1=glu_gate[:, c, :],
                                                   op0=ALU.add, op1=ALU.mult)
                    if b == 0:
                        step.mark(ins)
                ins.then_inc(sem("glu_ready"), 1)
                dve.wait_ge(sem("glu_ready"), m + 1)
                pair = xT[:, 2 * m:2 * m + 2, :]
                dve.tensor_tensor(pair, pair, glu_out[:, 2 * (m % 2):2 * (m % 2) + 2, :],
                                  ALU.add).then_inc(sem("x_ready"), 1)
                dve.wait_ge(sem("x_ready"), updates(L) + m + 1)

        x_tok = slot_view(0, TT, D)
        par_rows = slot_view(1, PAR_BLOCKS, P)

        def start_splits(split, eng, *block):
            for key in plan.tiles[:NSPLIT]:
                if key[0] % 3 == 0:
                    split(eng, key, *block)

        def load_sp(sp):
            for b in range(TT):
                sp.dma_start(x_tok[:, b, :], A["x"][0, b * P:(b + 1) * P, :]).then_inc(sem("x_in"), 16)

        SLOW_PAR = list(PAR)[2::3]
        FAST_PAR = [name for name in PAR if name not in SLOW_PAR]

        def load_params(q, names, signal_):
            for name in names:
                first, n = PAR[name]
                a = A[name]
                if name.startswith("dsa"):
                    for r in range(n):
                        row = first + r
                        for half in range(2):
                            q.dma_start(par_rows[row % P:row % P + 1, row // P, half * HALF:(half + 1) * HALF],
                                        a[r:r + 1, :]).then_inc(sem(signal_), 16)
                    continue
                letters = "abcd"[:len(a.shape)]
                flat = a.rearrange(f"{' '.join(letters)} -> ({' '.join(letters)})").rearrange("(r c) -> r c", c=P)
                r = 0
                while r < n:
                    row = first + r
                    m = min(n - r, P - row % P)
                    q.dma_start(par_rows[row % P:row % P + m, row // P, :], flat[r:r + m, :]).then_inc(sem(signal_), 16)
                    r += m

        def par_dmas(names):
            return sum(2 * PAR[name][1] if name.startswith("dsa") else (sum(PAR[name]) - 1) // P - PAR[name][0] // P + 1
                       for name in names)

        def constants(pool):
            step = pool_step

            def then(ins):
                pool.wait_ge(step.sem, step.mark(ins))

            pool.memset(par_rows[:, PAR_BLOCKS - 1, :], 0.0).then_inc(sem("par_cleared"), 1)
            pool.memset(ident[:, :], 0.0).then_inc(step.sem, 1)
            step.n += 1
            pool.memset(mean_all[:, :], 1.0 / D).then_inc(step.sem, 1)
            step.n += 1
            pool.memset(eps[:, 0:1], EPS).then_inc(step.sem, 1)
            step.n += 1
            pool.memset(eps[:, 1:2], GN_EPS).then_inc(step.sem, 1)
            step.n += 1
            for x, value in ((mean_head, 1.0 / HALF), (sum_head, 1.0)):
                then(pool.memset(x[:, :], 0.0))
                then(pool.memset(x[0:HALF, 0:HALF], value))
                then(pool.memset(x[HALF:P, HALF:P], value))
            pool.affine_select(out=ident[:, :], in_=ident[:, :], compare_op=ALU.not_equal, fill=1.0, base=0,
                               pattern=[[-1, P]], channel_multiplier=1).then_inc(sem("constants"), 1)

        def chunk_constants(pool):
            step = pool_step

            def then(ins):
                pool.wait_ge(step.sem, step.mark(ins))

            def select(x, pattern, base, slope, op=ALU.is_ge):
                then(pool.affine_select(out=x, in_=x, compare_op=op, fill=0.0, base=base, pattern=pattern,
                                        channel_multiplier=slope))

            then(pool.memset(masks[:, :, :], 0.0))
            for r in range(0, P, CH):
                then(pool.memset(masks[r:r + CH, :, r:r + CH], 1.0))
            select(masks[:, 0, :], [[-1, P]], -1, 1)
            for i, base in ((1, -1), (2, 0), (3, -1)):
                select(masks[:, i, :], [[1, P]], base, -1)
            then(pool.memset(pair_masks[:, :, :], 0.0))
            for i, n in ((0, 1), (2, 2), (3, 4), (4, 8), (5, 16)):
                v = pair_masks[:, i, :].rearrange("p (b h c) -> p b h c", h=2, c=n)[:, :, 0, :]
                nb = P // (2 * n)
                then(pool.memset(v, 1.0))
                select(v, [[-2 * n, nb], [0, n]], -n, 1)
                select(v, [[2 * n, nb], [0, n]], 2 * n - 1, -1)
            v = pair_masks[:, 1, :].rearrange("p (b h) -> p b h", h=2)[:, :, 1]
            then(pool.memset(v, 1.0))
            select(v, [[-2, P // 2]], 0, 1)
            select(v, [[2, P // 2]], 0, -1)
            then(pool.memset(chunk_cols[:, :], 0.0))
            for i in range(P // CH):
                then(pool.memset(chunk_cols[i * CH:(i + 1) * CH, i:i + 1], 1.0))
            then(pool.memset(chunk_reset[:, :], 1.0))
            then(pool.memset(chunk_reset[:, :].rearrange("p (c s) -> p c s", s=CH)[:, :, 0:1], 0.0))
            then(pool.tensor_copy(head_eye[0:HALF, :], ident[0:HALF, 0:HALF]))
            then(pool.memset(causal[:, :], 1.0))
            select(causal[:, :].rearrange("p (t c) -> p t c", c=S5_C), [[S5_C, S5_L], [0, S5_C]], S5_C - 1, -1)
            then(pool.memset(swap[:, :], 0.0))
            then(pool.tensor_copy(swap[:, 0:HALF], ident[:, HALF:P]))
            then(pool.tensor_scalar(swap[:, HALF:P], ident[:, 0:HALF], -1.0, None, ALU.mult))
            then(pool.memset(sign[0:HALF, :], 1.0))
            then(pool.memset(sign[HALF:P, :], -1.0))
            then(pool.memset(half_pi[:, :], TWO_PI / 4))
            pool.tensor_copy(head_eye[HALF:P, :], ident[HALF:P, HALF:P]).then_inc(sem("chunk_constants"), 1)

        def load_pe(pe):
            pe.wait_ge(sem("constants"), 1)
            pe.wait_ge(sem("x_in"), 32)
            for c in range(DC):
                for b in range(TT):
                    mm = pe.transpose(banks[c // 2][:, (c % 2) * T + b * P:(c % 2) * T + (b + 1) * P],
                                      x_tok[:, b, c * P:(c + 1) * P], ident[:, :])
                if c % 2:
                    mm.then_inc(sem("xt_full"), 1)
            pe.wait_ge(sem("par_in"), 16 * par_dmas(FAST_PAR))
            pe.wait_ge(sem("par_in_pool"), 16 * par_dmas(SLOW_PAR))
            for i in range(PAR_BLOCKS):
                mm = pe.transpose(banks[4 + i // 4][:, (i % 4) * P:(i % 4 + 1) * P], par_rows[:, i, :], ident[:, :])
                if i % 4 == 3:
                    mm.then_inc(sem("par_full"), 1)
            pe.wait_ge(sem("par_ready"), 2)

        def load_dve(dve):
            for m in range(4):
                dve.wait_ge(sem("xt_full"), m + 1)
                dve.tensor_copy(xT[:, 2 * m:2 * m + 2, :].rearrange("p a b -> p (a b)"),
                                banks[m][:, :]).then_inc(sem("x_ready"), 1)
            for i in range(2):
                dve.wait_ge(sem("par_full"), i + 1)
                dve.tensor_copy(par[:, i * 512:(i + 1) * 512], banks[4 + i][:, :]).then_inc(sem("par_ready"), 1)

        out_tok = slot_view(0, TT, D)
        total_updates = 4 * (1 + 2 * len(layers))

        def store_pe(pe):
            for m in range(4):
                pe.wait_ge(sem("x_ready"), total_updates - 4 + m + 1)
                for b in range(TT):
                    for c in range(2):
                        mm = pe.transpose(banks[m][:, (b * 2 + c) * P:(b * 2 + c + 1) * P],
                                          xT[:, 2 * m + c, b * P:(b + 1) * P], ident[:, :])
                mm.then_inc(sem("out_full"), 1)

        def store_act(act):
            for m in range(4):
                act.wait_ge(sem("out_full"), m + 1)
                act.activation(out_tok[:, :, 2 * m * P:(2 * m + 2) * P],
                               banks[m][:, :].rearrange("p (b n) -> p b n", b=TT), ACT.Copy).then_inc(sem("out_ready"), 1)

        def store_sp(sp):
            for m in range(4):
                sp.wait_ge(sem("out_ready"), m + 1)
                c = slice(2 * m * P, (2 * m + 2) * P)
                sp.dma_start(out[0].rearrange("(b p) d -> p b d", p=P)[:, :, c], out_tok[:, :, c]).then_inc(sem("stored"), 16)
            sp.wait_ge(sem("stored"), 64)

        block = ctx.enter_context(nc.Block())

        @block.sync
        def _(sp):
            load_sp(sp)
            for L in layers:
                [send_dsa, send_rwkv, send_s5][L % 3](sp, L)
                send_mlp(sp, L)
            store_sp(sp)

        @block.gpsimd
        def _(pool):
            constants(pool)
            pool.wait_ge(sem("par_cleared"), 1)
            load_params(pool, SLOW_PAR, "par_in_pool")
            chunk_constants(pool)
            pool.wait_ge(sem("chunk_constants"), 1)
            start_splits(rest_of_weights, pool, 1)
            for i, L in enumerate(layers):
                if i == 0 and L % 3 == 2:
                    s5_load(pool, L)
                [dsa_pool, rwkv_pool, s5_pool][L % 3](pool, L)
                if i + 1 < len(layers) and layers[i + 1] % 3 == 2:
                    s5_load(pool, layers[i + 1])
                mlp_pool(pool, L)

        @block.scalar
        def _(act):
            act.wait_ge(sem("par_cleared"), 1)
            load_params(act, FAST_PAR, "par_in")
            for L in layers:
                norm_squares(act, norm_index(L, 0))
                if layers.index(L) == 0:
                    start_splits(round_weights, act)
                norm_root(act, norm_index(L, 0))
                if splits_h(norm_index(L, 0)):
                    norm_round(act, norm_index(L, 0))
                [dsa_act, rwkv_act, s5_act][L % 3](act, L)
                norm_squares(act, norm_index(L, 1))
                norm_root(act, norm_index(L, 1))
                norm_round(act, norm_index(L, 1))
                mlp_act(act, L)
            store_act(act)

        @block.tensor
        def _(pe):
            load_pe(pe)
            for L in layers:
                norm_mean(pe, norm_index(L, 0))
                [dsa_pe, rwkv_pe, s5_pe][L % 3](pe, L)
                norm_mean(pe, norm_index(L, 1))
                mlp_pe(pe, L)
            store_pe(pe)

        @block.vector
        def _(dve):
            load_dve(dve)
            for L in layers:
                if layers.index(L) == 0:
                    start_splits(rest_of_weights, dve, 0)
                norm_scale(dve, norm_index(L, 0), "norm_mix", L)
                if L % 3:
                    dve.wait_ge(sem("chunk_constants"), 1)
                [dsa_dve, rwkv_dve, s5_dve][L % 3](dve, L)
                norm_scale(dve, norm_index(L, 1), "norm_ffn", L)
                mlp_dve(dve, L)


def kernel(**inputs):
    import numpy as _np
    import concourse.bacc as _bacc
    from concourse import mybir as _mybir
    from concourse.bass_utils import run_bass_kernel_spmd as _run

    nc = _bacc.Bacc("TRN2", target_bir_lowering=False, num_devices=1)
    arrays, args = {}, {}
    for name, a in inputs.items():
        a = _np.ascontiguousarray(a)
        arrays[f"in_{name}_dram"] = a
        args[name] = nc.dram_tensor(f"in_{name}_dram", a.shape, _mybir.dt.from_np(a.dtype), kind="ExternalInput").ap()
    out = nc.dram_tensor("out_0_dram", (1, T, D), F32, kind="ExternalOutput").ap()
    trunk(nc, args, out)
    r = _run(nc, [arrays], core_ids=[0])
    return r.results[0]["out_0_dram"]
```
